# Optimizing a Trainium2 kernel written in Bass

```python
import jax, jax.numpy as jnp
from jax import lax
import numpy as np

D_MODEL = 1024
BATCH = 1
SEQ = 256
DEPTH = 1

CHUNK = 64
PLE_DIM = 256
EPS = 1e-6

D_SGU = 1024
SGU_BLOCK = 128
SGU_HEADS = 8
SGU_HEAD_DIM = D_SGU // SGU_HEADS

D_CONV = 1024
CONV_WIDTH = 31

D_POOL = 1024
POOL_WINDOWS = (2, 4, 8, 16)
POOL_GROUPS = len(POOL_WINDOWS)
POOL_GROUP_DIM = D_POOL // POOL_GROUPS

N_BRANCH = 3
D_IN = 2 * D_SGU + 2 * D_CONV + D_POOL + N_BRANCH * D_MODEL
SPLITS = (2 * D_SGU, 2 * D_SGU + 2 * D_CONV, 2 * D_SGU + 2 * D_CONV + D_POOL)

D_FF = -(-8 * D_MODEL // (3 * 256)) * 256


def rms_norm(x, g):
    xf = x.astype(jnp.float32)
    y = xf * lax.rsqrt(jnp.mean(xf * xf, axis=-1, keepdims=True) + EPS)
    return (y * g.astype(jnp.float32)).astype(x.dtype)

def layer_norm(x, g, b):
    xf = x.astype(jnp.float32)
    mu = jnp.mean(xf, axis=-1, keepdims=True)
    xc = xf - mu
    var = jnp.mean(xc * xc, axis=-1, keepdims=True)
    y = xc * lax.rsqrt(var + EPS) * g.astype(jnp.float32) + b.astype(jnp.float32)
    return y.astype(x.dtype)

def sgu_mask():
    c = jnp.arange(SGU_BLOCK) // CHUNK
    return c[None, :] <= c[:, None]

def spatial_gating(z, w_s, b_s, g_v, b_v):
    u, v = jnp.split(z, 2, axis=-1)
    v = layer_norm(v, g_v, b_v)
    bsz, s, _ = v.shape
    nb = s // SGU_BLOCK
    v = v.reshape(bsz, nb, SGU_BLOCK, SGU_HEADS, SGU_HEAD_DIM)
    w = jnp.where(sgu_mask()[None], w_s, jnp.zeros_like(w_s))
    mixed = jnp.einsum('hij,bnjhc->bnihc', w, v) + b_s.T[None, None, :, :, None]
    return u * mixed.reshape(bsz, s, D_SGU)

def conformer_conv(z, w_dw, b_dw, g_ln, b_ln):
    a, gate = jnp.split(z, 2, axis=-1)
    h = a * jax.nn.sigmoid(gate)
    h = lax.conv_general_dilated(
        h, w_dw, window_strides=(1,), padding=((CONV_WIDTH - 1, 0),),
        dimension_numbers=('NWC', 'WIO', 'NWC'),
        feature_group_count=D_CONV) + b_dw
    h = layer_norm(h, g_ln, b_ln)
    return jax.nn.silu(h)

def multiscale_pool(z, w_pool, s_pool):
    bsz, s, _ = z.shape
    zf = z.astype(jnp.float32)
    cs = jnp.cumsum(zf, axis=1)
    t = jnp.arange(1, s + 1, dtype=jnp.float32)
    outs = []
    for gi, w in enumerate(POOL_WINDOWS):
        sl = slice(gi * POOL_GROUP_DIM, (gi + 1) * POOL_GROUP_DIM)
        c = cs[..., sl]
        prev = jnp.pad(c[:, :s - w], ((0, 0), (w, 0), (0, 0)))
        cnt = jnp.minimum(t, float(w))[None, :, None]
        outs.append((c - prev) / cnt - zf[..., sl])
    pooled = jnp.stack(outs, axis=2).astype(z.dtype)
    mixed = jnp.einsum('bsgc,gcd->bsgd', pooled, w_pool)
    return mixed.reshape(bsz, s, D_POOL) * s_pool

def first_inputs(seed: int = 0) -> dict:
    key = jax.random.key(seed)
    ks = jax.random.split(key, 32)
    f32 = jnp.float32

    def nrm(k, shape, scale):
        return jax.random.normal(k, shape, f32) * scale

    def gain(k, shape):
        return 1.0 + 0.05 * jax.random.normal(k, shape, f32)

    L = DEPTH
    return {
        "x": nrm(ks[0], (BATCH, SEQ, D_MODEL), 1.0),
        "p": nrm(ks[1], (DEPTH, BATCH, SEQ, PLE_DIM), 1.0),
        "g_mix_pre": gain(ks[2], (L, D_MODEL)),
        "w_in": nrm(ks[3], (L, D_MODEL, D_IN), D_MODEL ** -0.5),
        "w_sgu_s": nrm(ks[4], (L, SGU_HEADS, SGU_BLOCK, SGU_BLOCK), SGU_BLOCK ** -0.5),
        "b_sgu_s": 1.0 + 0.1 * jax.random.normal(ks[5], (L, SGU_HEADS, SGU_BLOCK), f32),
        "g_sgu_v": gain(ks[6], (L, D_SGU)),
        "b_sgu_v": nrm(ks[7], (L, D_SGU), 0.02),
        "w_sgu_out": nrm(ks[8], (L, D_SGU, D_MODEL), D_SGU ** -0.5),
        "w_dw": nrm(ks[9], (L, CONV_WIDTH, 1, D_CONV), CONV_WIDTH ** -0.5),
        "b_dw": nrm(ks[10], (L, D_CONV), 0.02),
        "g_conv_ln": gain(ks[11], (L, D_CONV)),
        "b_conv_ln": nrm(ks[12], (L, D_CONV), 0.02),
        "w_conv_out": nrm(ks[13], (L, D_CONV, D_MODEL), D_CONV ** -0.5),
        "w_pool": nrm(ks[14], (L, POOL_GROUPS, POOL_GROUP_DIM, POOL_GROUP_DIM), POOL_GROUP_DIM ** -0.5),
        "s_pool": 1.0 + 0.1 * jax.random.normal(ks[15], (L, D_POOL), f32),
        "w_pool_out": nrm(ks[16], (L, D_POOL, D_MODEL), D_POOL ** -0.5),
        "w_out": nrm(ks[17], (L, D_MODEL, D_MODEL), D_MODEL ** -0.5),
        "g_mix_post": gain(ks[18], (L, D_MODEL)),
        "g_ffn_pre": gain(ks[19], (L, D_MODEL)),
        "w_ffn_in": nrm(ks[20], (L, D_MODEL, 2 * D_FF), D_MODEL ** -0.5),
        "w_ffn_out": nrm(ks[21], (L, D_FF, D_MODEL), D_FF ** -0.5),
        "g_ffn_post": gain(ks[22], (L, D_MODEL)),
        "w_ple": nrm(ks[23], (L, PLE_DIM, D_MODEL), PLE_DIM ** -0.5),
        "w_ple_gate": nrm(ks[24], (L, D_MODEL, D_MODEL), D_MODEL ** -0.5),
    }

def first_block(x, p, g_mix_pre, w_in, w_sgu_s, b_sgu_s, g_sgu_v, b_sgu_v, w_sgu_out,
              w_dw, b_dw, g_conv_ln, b_conv_ln, w_conv_out, w_pool, s_pool, w_pool_out,
              w_out, g_mix_post, g_ffn_pre, w_ffn_in, w_ffn_out, g_ffn_post,
              w_ple, w_ple_gate):
    h = x
    bsz, s, _ = x.shape
    for i in range(DEPTH):
        hn = rms_norm(h, g_mix_pre[i])
        proj = hn @ w_in[i]
        z_sgu, z_conv, z_pool, z_gate = jnp.split(proj, SPLITS, axis=-1)

        br_a = spatial_gating(jax.nn.gelu(z_sgu), w_sgu_s[i], b_sgu_s[i],
                              g_sgu_v[i], b_sgu_v[i]) @ w_sgu_out[i]
        br_b = conformer_conv(z_conv, w_dw[i], b_dw[i],
                              g_conv_ln[i], b_conv_ln[i]) @ w_conv_out[i]
        br_c = multiscale_pool(z_pool, w_pool[i], s_pool[i]) @ w_pool_out[i]

        gates = jax.nn.sigmoid(z_gate).reshape(bsz, s, N_BRANCH, D_MODEL)
        merged = gates[:, :, 0] * br_a + gates[:, :, 1] * br_b + gates[:, :, 2] * br_c
        h = h + rms_norm(merged @ w_out[i], g_mix_post[i])

        hn = rms_norm(h, g_ffn_pre[i])
        f_gate, f_up = jnp.split(hn @ w_ffn_in[i], 2, axis=-1)
        f = (jax.nn.silu(f_gate) * f_up) @ w_ffn_out[i]
        h = h + rms_norm(f, g_ffn_post[i])

        h = h + jax.nn.sigmoid(h @ w_ple_gate[i]) * (p[i] @ w_ple[i])
    return h


HEAD_DIM = 64
N_HEADS_DIL = 8
N_HEADS_SB = 8
D_DIL = N_HEADS_DIL * HEAD_DIM
D_SB = N_HEADS_SB * HEAD_DIM
D_MIX = D_DIL + D_SB
DILATION_PATTERNS = ((128, 1), (512, 4), (2048, 16))
SB_BLOCK = 128
N_GROUPS = 4
EXPERTS_PER_GROUP = 8
N_EXPERTS = N_GROUPS * EXPERTS_PER_GROUP
TOP_K = 2
D_FF_EXPERT = D_MODEL // 2
MOE_BLOCK = 128
NORM_EPS = 1e-6


def _rmsnorm(x, g):
    xf = x.astype(jnp.float32)
    y = xf * lax.rsqrt(jnp.mean(xf * xf, axis=-1, keepdims=True) + NORM_EPS)
    return (y * g.astype(jnp.float32)).astype(x.dtype)

def _modulate(h, shift, scale):
    return h * (1 + scale[:, None, :]) + shift[:, None, :]

def _alibi_slopes(n_heads):
    return np.array([2.0 ** (-8.0 * (i + 1) / n_heads) for i in range(n_heads)], dtype=np.float32)

def _dilated_window_attention(q, k, v, window, dilation, slopes):
    b, s, h, e = q.shape
    n = window // dilation
    unit = n * dilation
    s_pad = -(-s // unit) * unit
    nb = s_pad // unit
    pad = ((0, 0), (0, s_pad - s), (0, 0), (0, 0))

    def split(t):
        return jnp.pad(t, pad).reshape(b, nb, n, dilation, h, e)

    def with_prev(t):
        prev = jnp.pad(t[:, :-1], ((0, 0), (1, 0), (0, 0), (0, 0), (0, 0), (0, 0)))
        return jnp.concatenate([prev, t], axis=2)

    qb = split(q)
    kc = with_prev(split(k))
    vc = with_prev(split(v)).astype(jnp.float32)
    scores = jnp.einsum('bgidhe,bgjdhe->bgdhij', qb, kc,
                        preferred_element_type=jnp.float32) * (e ** -0.5)
    i_idx = np.arange(n)[:, None]
    j_idx = np.arange(2 * n)[None, :]
    steps = i_idx + n - j_idx
    blk = np.arange(nb)[:, None, None]
    valid = (steps >= 0) & (steps <= n) & (blk * n + j_idx - n >= 0)
    bias = -slopes[:, None, None] * (steps * dilation).astype(np.float32)[None]
    logits = jnp.where(valid[None, :, None, None], scores + jnp.asarray(bias)[None, None, None], -jnp.inf)
    m = jnp.max(logits, axis=-1)
    p = jnp.exp(logits - m[..., None])
    den = jnp.sum(p, axis=-1)
    den_t = den.transpose(0, 1, 4, 2, 3)
    o = jnp.einsum('bgdhij,bgjdhe->bgidhe', p, vc) / den_t[..., None]
    o = o.reshape(b, s_pad, h, e)[:, :s]
    m = m.transpose(0, 1, 4, 2, 3).reshape(b, s_pad, h)[:, :s]
    den = den_t.reshape(b, s_pad, h)[:, :s]
    return o, m, den

def _dilated_mixture(q, k, v):
    slopes = _alibi_slopes(q.shape[2])
    outs, maxes, dens = [], [], []
    for window, dilation in DILATION_PATTERNS:
        o, m, den = _dilated_window_attention(q, k, v, window, dilation, slopes)
        outs.append(o)
        maxes.append(m)
        dens.append(den)
    outs = jnp.stack(outs)
    maxes = jnp.stack(maxes)
    dens = jnp.stack(dens)
    w = dens * jnp.exp(maxes - jnp.max(maxes, axis=0, keepdims=True))
    w = w / jnp.sum(w, axis=0, keepdims=True)
    return jnp.sum(w[..., None] * outs, axis=0).astype(q.dtype)

def _stick_breaking_attention(q, k, v):
    b, s, h, e = q.shape
    nb = s // SB_BLOCK
    qblocks = q.reshape(b, nb, SB_BLOCK, h, e).transpose(1, 0, 2, 3, 4)
    key_pos = jnp.arange(s)
    vf = v.astype(jnp.float32)

    def block(args):
        qb, idx = args
        z = jnp.einsum('bqhe,bshe->bhqs', qb, k, preferred_element_type=jnp.float32) * (e ** -0.5)
        q_pos = idx * SB_BLOCK + jnp.arange(SB_BLOCK)
        causal = key_pos[None, :] < q_pos[:, None]
        log_beta = jax.nn.log_sigmoid(z)
        log_keep = jnp.where(causal, jax.nn.log_sigmoid(-z), 0.0)
        between = lax.cumsum(log_keep, axis=3, reverse=True) - log_keep
        weights = jnp.where(causal, jnp.exp(log_beta + between), 0.0)
        return jnp.einsum('bhqs,bshe->bqhe', weights, vf)

    out = lax.map(block, (qblocks, jnp.arange(nb)))
    return out.transpose(1, 0, 2, 3, 4).reshape(b, s, h, e).astype(q.dtype)

def _hierarchical_moe(h, w_group, w_expert, w_gate, w_up, w_down):
    n, d = h.shape
    group_prob = jax.nn.softmax((h @ w_group).astype(jnp.float32), axis=-1)
    group = jnp.argmax(group_prob, axis=-1)
    group_gate = jnp.take_along_axis(group_prob, group[:, None], axis=1)
    exp_logits = (h @ w_expert).astype(jnp.float32).reshape(n, N_GROUPS, EXPERTS_PER_GROUP)
    exp_logits = jnp.take_along_axis(exp_logits, group[:, None, None], axis=1)[:, 0]
    top_p, top_local = lax.top_k(jax.nn.softmax(exp_logits, axis=-1), TOP_K)
    top_p = top_p / jnp.sum(top_p, axis=-1, keepdims=True)
    weight = (group_gate * top_p).reshape(-1)
    expert = (group[:, None] * EXPERTS_PER_GROUP + top_local).reshape(-1)
    token = jnp.repeat(jnp.arange(n), TOP_K)

    order = jnp.argsort(expert)
    e_sorted = expert[order]
    tok_sorted = token[order]
    w_sorted = weight[order]
    counts = jnp.zeros((N_EXPERTS,), jnp.int32).at[expert].add(1)
    padded = (counts + MOE_BLOCK - 1) // MOE_BLOCK * MOE_BLOCK
    start = jnp.cumsum(counts) - counts
    pad_end = jnp.cumsum(padded)
    pad_start = pad_end - padded
    nk = n * TOP_K
    dest = pad_start[e_sorted] + jnp.arange(nk) - start[e_sorted]
    cap = -(-nk // MOE_BLOCK) * MOE_BLOCK + N_EXPERTS * MOE_BLOCK
    n_blocks = cap // MOE_BLOCK
    buf = jnp.zeros((cap, d), h.dtype).at[dest].set(h[tok_sorted])
    block_expert = jnp.minimum(
        jnp.searchsorted(pad_end, jnp.arange(n_blocks) * MOE_BLOCK, side='right'), N_EXPERTS - 1)

    def expert_block(args):
        xb, e = args
        return (jax.nn.silu(xb @ w_gate[e]) * (xb @ w_up[e])) @ w_down[e]

    y = lax.map(expert_block, (buf.reshape(n_blocks, MOE_BLOCK, d), block_expert)).reshape(cap, d)
    contrib = y[dest] * w_sorted[:, None].astype(y.dtype)
    return jnp.zeros((n, d), y.dtype).at[tok_sorted].add(contrib)

def second_inputs(seed: int = 0) -> dict:
    key = jax.random.key(seed)
    ks = jax.random.split(key, 16)
    d = D_MODEL

    def nrm(k, shape, std):
        return jax.random.normal(k, shape, jnp.float32) * std

    return {
        "x": nrm(ks[0], (BATCH, SEQ, d), 1.0),
        "c": nrm(ks[1], (BATCH, d), 1.0),
        "w_ada": nrm(ks[2], (DEPTH, d, 6 * d), 0.5 * d ** -0.5),
        "b_ada": nrm(ks[3], (DEPTH, 6 * d), 0.02),
        "g_mix": 1.0 + nrm(ks[4], (DEPTH, d), 0.02),
        "w_in": nrm(ks[5], (DEPTH, d, 3 * D_MIX), d ** -0.5),
        "g_dil_out": 1.0 + nrm(ks[6], (DEPTH, D_DIL), 0.02),
        "g_sb_out": 1.0 + nrm(ks[7], (DEPTH, D_SB), 0.02),
        "w_out": nrm(ks[8], (DEPTH, D_MIX, d), D_MIX ** -0.5),
        "g_ffn": 1.0 + nrm(ks[9], (DEPTH, d), 0.02),
        "w_group": nrm(ks[10], (DEPTH, d, N_GROUPS), d ** -0.5),
        "w_expert": nrm(ks[11], (DEPTH, d, N_EXPERTS), d ** -0.5),
        "w_gate": nrm(ks[12], (DEPTH, N_EXPERTS, d, D_FF_EXPERT), d ** -0.5),
        "w_up": nrm(ks[13], (DEPTH, N_EXPERTS, d, D_FF_EXPERT), d ** -0.5),
        "w_down": nrm(ks[14], (DEPTH, N_EXPERTS, D_FF_EXPERT, d), D_FF_EXPERT ** -0.5),
        "g_final": 1.0 + nrm(ks[15], (d,), 0.02),
    }

def second_block(x, c, w_ada, b_ada, g_mix, w_in, g_dil_out, g_sb_out, w_out, g_ffn,
              w_group, w_expert, w_gate, w_up, w_down, g_final):
    b, s, d = x.shape
    cond = jax.nn.silu(c)
    for layer in range(DEPTH):
        mod = cond @ w_ada[layer] + b_ada[layer]
        shift_mix, scale_mix, gate_mix, shift_ffn, scale_ffn, gate_ffn = jnp.split(mod, 6, axis=-1)

        h = _modulate(_rmsnorm(x, g_mix[layer]), shift_mix, scale_mix)
        qkv = h @ w_in[layer]
        q_d, k_d, v_d, q_s, k_s, v_s = jnp.split(
            qkv, [D_DIL, 2 * D_DIL, 3 * D_DIL, 3 * D_DIL + D_SB, 3 * D_DIL + 2 * D_SB], axis=-1)
        heads_d = lambda t: t.reshape(b, s, N_HEADS_DIL, HEAD_DIM)
        heads_s = lambda t: t.reshape(b, s, N_HEADS_SB, HEAD_DIM)
        o_dil = _dilated_mixture(heads_d(q_d), heads_d(k_d), heads_d(v_d)).reshape(b, s, D_DIL)
        o_sb = _stick_breaking_attention(heads_s(q_s), heads_s(k_s), heads_s(v_s)).reshape(b, s, D_SB)
        mixed = jnp.concatenate([_rmsnorm(o_dil, g_dil_out[layer]),
                                 _rmsnorm(o_sb, g_sb_out[layer])], axis=-1)
        x = x + gate_mix[:, None, :] * (mixed @ w_out[layer])

        h2 = _modulate(_rmsnorm(x, g_ffn[layer]), shift_ffn, scale_ffn).reshape(b * s, d)
        y = _hierarchical_moe(h2, w_group[layer], w_expert[layer],
                              w_gate[layer], w_up[layer], w_down[layer]).reshape(b, s, d)
        x = x + gate_ffn[:, None, :] * y
    return _rmsnorm(x, g_final)


def setup_inputs(seed=0):
    out = dict(first_inputs(seed))
    for name, value in second_inputs(seed + 1).items():
        if name != "x":
            out[name + "_2"] = value
    return out


def reference(
    x, p, g_mix_pre, w_in, w_sgu_s, b_sgu_s, g_sgu_v, b_sgu_v, w_sgu_out, w_dw, b_dw, g_conv_ln,
    b_conv_ln, w_conv_out, w_pool, s_pool, w_pool_out, w_out, g_mix_post, g_ffn_pre, w_ffn_in,
    w_ffn_out, g_ffn_post, w_ple, w_ple_gate, c_2, w_ada_2, b_ada_2, g_mix_2, w_in_2,
    g_dil_out_2, g_sb_out_2, w_out_2, g_ffn_2, w_group_2, w_expert_2, w_gate_2, w_up_2,
    w_down_2, g_final_2,
):
    x = first_block(
        x, p, g_mix_pre, w_in, w_sgu_s, b_sgu_s, g_sgu_v, b_sgu_v, w_sgu_out, w_dw, b_dw,
        g_conv_ln, b_conv_ln, w_conv_out, w_pool, s_pool, w_pool_out, w_out, g_mix_post,
        g_ffn_pre, w_ffn_in, w_ffn_out, g_ffn_post, w_ple, w_ple_gate,
    )
    return second_block(
        x, c_2, w_ada_2, b_ada_2, g_mix_2, w_in_2, g_dil_out_2, g_sb_out_2, w_out_2, g_ffn_2,
        w_group_2, w_expert_2, w_gate_2, w_up_2, w_down_2, g_final_2,
    )


_drawn_inputs = setup_inputs


def setup_inputs(seed=0):
    import zlib

    import numpy as np

    out = dict(_drawn_inputs(seed))
    spreads = {}
    factors = {'g_sgu_v': 3.193,
     'b_sgu_v': 8.0,
     'b_dw': 3.369,
     'b_conv_ln': 6.66,
     'b_ada_2': 3.798,
     'g_mix_2': 8.0,
     'g_dil_out_2': 8.0,
     'g_sb_out_2': 8.0,
     'g_ffn_2': 8.0,
     'g_final_2': 2.873}
    for name, (base, spread) in spreads.items():
        noise = np.random.default_rng([zlib.crc32(name.encode()), seed]).standard_normal(out[name].shape)
        drawn = base * np.exp(spread * noise) if base else spread * noise
        out[name] = __import__('jax').numpy.asarray(drawn.astype(out[name].dtype))
    for name, factor in factors.items():
        out[name] = (out[name] * factor).astype(out[name].dtype)
    return out
```

```python
from contextlib import ExitStack

import numpy as np

import concourse.bass as bass
from concourse import mybir

F32 = mybir.dt.float32
ALU = mybir.AluOpType
ACTF = mybir.ActivationFunctionType
AX = mybir.AxisListType.X

T = 256
D = 1024
NFF = 22
NE = 32
EPS = 1e-6
WIN = (2, 4, 8, 16)
NSLOT = 5
BIG = 1e30


def constants():
    p = np.arange(128)
    at, parts, n = {}, [], 0

    def put(name, a):
        nonlocal n
        a = np.asarray(a, np.float32).reshape(128, -1)
        at[name] = (n, a.shape[1])
        parts.append(a)
        n += a.shape[1]

    put("ident", np.eye(128))
    put("ones", np.ones((128, 128)))
    put("mean", np.full((128, 128), 1.0 / D))
    put("upto", p[:, None] >= p[None, :])
    put("before", p[:, None] < p[None, :])
    put("sgum", (p[:, None] // 64) <= (p[None, :] // 64))
    dist = np.concatenate([p[:, None] - p[None, :], p[:, None] + 128 - np.arange(256)[None, :]], 1)
    count = ((dist >= 0) & (dist <= 128)) * 1.0 + ((dist >= 0) & (dist % 4 == 0)) + ((dist >= 0) & (dist % 16 == 0))
    put("dist", np.where(count > 0, dist, 1e30))
    put("count", count)
    sb = np.concatenate([np.where(p[:, None] < p[None, :], 0.0, -BIG), np.zeros((128, 128)),
                         np.where(p[:, None] < p[None, :], 0.0, -BIG)], 1)
    put("sbneg", sb)
    put("invc", np.tile(np.stack([1.0 / np.minimum(np.arange(1, 17), w) for w in WIN]).reshape(1, -1), (128, 1)))
    put("eps", np.full((128, 1), EPS))
    put("one", np.ones((128, 1)))
    put("zero", np.zeros((128, 1)))
    put("iota", np.tile(np.arange(32)[None], (128, 1)))
    return np.concatenate(parts, 1), at


class Tok:

    def __init__(self, sem, val):
        self.sem, self.val = sem, val


class Queue:

    def __init__(self, sem, chained):
        self.sem, self.chained, self.n, self.items, self.last = sem, chained, 0, [], None

    def op(self, fn, *waits):
        waits = [w for w in waits if w is not None]
        if self.chained and self.last:
            waits.append(self.last)
        self.n += 1
        self.last = Tok(self.sem, self.n)
        self.items.append((fn, waits, (self.sem, 1)))
        return self.last

    def quiet(self, fn, *waits):
        self.items.append((fn, [w for w in waits if w is not None], None))

    def dma(self, dst, src, sem, *waits):
        self.items.append((lambda e: e.dma_start(dst, src), [w for w in waits if w is not None], (sem, 16)))

    def wait(self, *waits):
        self.items.append((None, [w for w in waits if w is not None], None))

    def emit(self, eng):
        seen = {}
        for fn, waits, inc in self.items:
            need = {}
            for w in waits:
                need[id(w.sem)] = max(need.get(id(w.sem), (0, None))[0], w.val), w.sem
            for key, (val, sem) in need.items():
                if seen.get(key, 0) < val:
                    eng.wait_ge(sem, val)
                    seen[key] = val
            if fn is None:
                continue
            ins = fn(eng)
            if inc:
                ins.then_inc(*inc)


def program(nc, I, out, const_at):
    with ExitStack() as ctx:
        def sb(name, shape, dt=F32):
            return ctx.enter_context(nc.sbuf_tensor(name, shape, dt))

        def sem(name):
            return ctx.enter_context(nc.semaphore(name))

        PE, ACT, DVE, POOL, SP = (Queue(sem("s_" + n), n in ("act", "dve", "pool"))
                                  for n in ("pe", "act", "dve", "pool", "sp"))
        sems = {}

        def dsem(name):
            if name not in sems:
                sems[name] = [sem("d_" + name), 0]
            sems[name][1] += 16
            return sems[name][0]

        def dtok(name):
            return Tok(*sems[name])

        ps = [ctx.enter_context(nc.psum_tensor(f"ps{i}", [128, 512], F32)) for i in range(8)]
        ps_free = [[] for _ in range(8)]
        ps_next = [0]
        ps_held = set()

        def bank():
            i = ps_next[0]
            while i in ps_held:
                i = (i + 1) % 8
            ps_next[0] = (i + 1) % 8
            return i

        ring = [sb(f"ring{i}", [128, 4096]) for i in range(NSLOT)]
        ring_sem = [sem(f"d_ring{i}") for i in range(NSLOT)]
        ring_n = [0] * NSLOT
        ring_free = [None] * NSLOT
        ring_at = [0]

        def stream(*pieces):
            i = ring_at[0] % NSLOT
            ring_at[0] += 1
            for view, src in pieces:
                SP.dma(view(ring[i]), src, ring_sem[i], ring_free[i])
                ring_n[i] += 16
            return i, Tok(ring_sem[i], ring_n[i])

        def cols(w, a, n):
            return w[:, a:a + n].rearrange("(k p) n -> p k n", p=128)

        def k8(t):
            return t[:, :].rearrange("p (k n) -> p k n", k=8)

        cst_w = const_at["iota"][0] + const_at["iota"][1]
        CST = sb("cst", [128, cst_w])

        def c_(name):
            o, n = const_at[name]
            return CST[:, o:o + n]

        ident, ones, mean = c_("ident"), c_("ones"), c_("mean")
        X = sb("X", [128, 2, D])
        HT = sb("HT", [128, 8, T])
        COL = sb("COL", [128, 328])
        SM = sb("SM", [128, 512])
        sm_at = [0]

        def small(n):
            a = sm_at[0]
            sm_at[0] += n
            assert sm_at[0] <= 512
            return SM[:, a:a + n]

        AR = 24064
        arena = sb("arena", [128, AR])

        def ar(off, n, k=None):
            assert off + n <= AR, (off, n)
            v = arena[:, off:off + n]
            return v if k is None else v.rearrange("p (k n) -> p k n", k=k)

        SP.dma(X[:, :, :], I["x"][0].rearrange("(t p) d -> p t d", p=128), dsem("x"))
        ACT.dma(CST[:, :], I["cst"], dsem("cst"))
        rows = ar(0, 384)
        row_at = {}
        r = 0
        for name, n in (("g_mix_pre", 8), ("b_dw", 8), ("g_conv_ln", 8), ("b_conv_ln", 8), ("s_pool", 8),
                        ("g_ffn_pre", 8), ("c_2", 8), ("g_mix_2", 8), ("g_dil_out_2", 4), ("g_sb_out_2", 4)):
            row_at[name] = r
            ACT.dma(rows[r:r + n, 0:128], I[name][0].rearrange("(a b) -> a b", b=128), dsem("rows"))
            r += n
        NR = r
        wdw = I["w_dw"][0].rearrange("k o (c p) -> (k o c) p", p=128)
        for j in range(2):
            ACT.dma(rows[0:124, 128 + 128 * j:256 + 128 * j], wdw[124 * j:124 * j + 124, :], dsem("rows"))

        def col(name, k):
            a = row_at[name] + k
            return COL[:, a:a + 1]

        def tap(k, c):
            a = NR + k * 8 + c
            return COL[:, a:a + 1]

        bank()
        cst, rws = dtok("cst"), dtok("rows")
        PE.quiet(lambda e: e.transpose(ps[0][:, 0:NR], rows[0:NR, 0:128], ident[0:NR, 0:NR]), cst, rws)
        PE.quiet(lambda e: e.transpose(ps[0][:, NR:NR + 124], rows[0:124, 128:256], ident[0:124, 0:124]))
        t = PE.op(lambda e: e.transpose(ps[0][:, NR + 124:NR + 248], rows[0:124, 256:384], ident[0:124, 0:124]))
        t_col = DVE.op(lambda e: e.tensor_copy(COL[:, 0:NR + 248], ps[0][:, 0:NR + 248]), t)
        ps_free[0] = [t_col]

        def rstd(ss, scale=1.0 / D, *waits):
            t = ACT.op(lambda e: e.activation(ss, ss, ACTF.Sqrt, bias=c_("eps"), scale=scale), cst, *waits)
            return DVE.op(lambda e: e.reciprocal(ss, ss), t)

        def sumsq(srcs, junk, acc, *waits):
            for n, s in enumerate(srcs):
                t = ACT.op(lambda e, s=s, n=n: e.activation(junk, s, ACTF.Square, accum_out=acc[:, n:n + 1]), *waits)
            return t

        def to_T(src, dst, nk, evac, *waits):
            tok = None
            for k0 in range(0, nk, 2):
                b = bank()
                for k in range(k0, k0 + 2):
                    for tt in range(2):
                        o = (k - k0) * 256 + tt * 128
                        f = (lambda e, b=b, o=o, s=src(tt, k): e.transpose(ps[b][:, o:o + 128], s, ident))
                        if k == k0 + 1 and tt == 1:
                            t = PE.op(f, *waits, *ps_free[b])
                        else:
                            PE.quiet(f, *waits, *ps_free[b])
                if evac is None:
                    q = DVE if (k0 // 2) % 2 else ACT
                    v = ps[b][:, :].rearrange("p (k n) -> p k n", k=2)
                    if q is DVE:
                        tok = [DVE.op(lambda e, k0=k0, v=v: e.tensor_copy(dst[:, k0:k0 + 2, :], v), t)]
                    else:
                        tok = [ACT.op(lambda e, k0=k0, v=v: e.activation(dst[:, k0:k0 + 2, :], v, ACTF.Copy), t)]
                    ps_free[b] = tok
                else:
                    done = []
                    for k in range(k0, k0 + 2):
                        s, bi = evac(k)
                        v = ps[b][:, (k - k0) * 256:(k - k0) * 256 + 256]
                        if bi is None:
                            done.append(DVE.op(lambda e, k=k, v=v, s=s: e.tensor_scalar(
                                dst[:, k, :], v, s, None, ALU.mult), t))
                        else:
                            done.append(DVE.op(lambda e, k=k, v=v, s=s, bi=bi: e.tensor_scalar(
                                dst[:, k, :], v, s, bi, ALU.mult, ALU.add), t))
                    ps_free[b] = done
            return [DVE.last, ACT.last]

        def fm(W, nt, xT, nk, b, o, waits, first_free, inc):
            for k in range(nk):
                f = (lambda e, k=k: e.matmul(ps[b][:, o:o + 256], W[:, k, nt * 128:nt * 128 + 128], xT[:, k, :],
                                             start=(k == 0), stop=(k == nk - 1)))
                w = (*waits, *(first_free if k == 0 else ()))
                if inc and k == nk - 1:
                    return PE.op(f, *w)
                PE.quiet(f, *w)

        def fm_slot(W, xT, waits, on_bank, pairs=((0, 1), (2, 3)), nk=8):
            for n, pair in enumerate(pairs):
                b = bank()
                fm(W, pair[0], xT, nk, b, 0, waits, ps_free[b], False)
                t = fm(W, pair[1], xT, nk, b, 256, waits, (), True)
                ps_free[b] = on_bank(n, b, t)
            return t

        def tmaj(xT, W, nk, tt, b, waits, start=True, stop=True, o=0, n=512):
            for k in range(nk):
                f = (lambda e, k=k, x=xT(k)[:, tt * 128:tt * 128 + 128], w=W(k): e.matmul(
                    ps[b][:, o:o + n], x, w, start=(start and k == 0), stop=(stop and k == nk - 1)))
                w = (*waits, *(ps_free[b] if start and k == 0 else ()))
                if k == nk - 1:
                    return PE.op(f, *w)
                PE.quiet(f, *w)

        def post_norm(banks, toks, grow, gtok, tmp):
            ss4, ss = small(4), small(2)
            for j in range(4):
                t = ACT.op(lambda e, j=j: e.activation(tmp[:, 0:512], ps[banks[j]][:, :], ACTF.Square,
                                                       accum_out=ss4[:, j:j + 1]), toks[j], DVE.last)
            v = ss4.rearrange("p (t n) -> p t n", n=2)
            t = DVE.op(lambda e: e.tensor_tensor(ss, v[:, :, 0], v[:, :, 1], ALU.add), t)
            t = rstd(ss, 1.0 / D, t)
            for j in range(4):
                tt, nn = j // 2, j % 2
                a = DVE.op(lambda e, j=j, tt=tt, nn=nn: e.scalar_tensor_tensor(
                    out=tmp[:, 512:1024], in0=ps[banks[j]][:, :], scalar=ss[:, tt:tt + 1],
                    in1=grow[:, nn * 512:nn * 512 + 512], op0=ALU.mult, op1=ALU.mult), gtok)
                ps_free[banks[j]] = [a]
                t = DVE.op(lambda e, tt=tt, nn=nn: e.tensor_tensor(
                    X[:, tt, nn * 512:nn * 512 + 512], X[:, tt, nn * 512:nn * 512 + 512],
                    tmp[:, 512:1024], ALU.add))
            return t

        def norm_scaled(dst, tmp, *waits):
            ss = small(2)
            t = sumsq([X[:, 0, :], X[:, 1, :]], tmp, ss, *waits)
            t = rstd(ss, 1.0 / D, t)
            for tt in range(2):
                t = DVE.op(lambda e, tt=tt: e.tensor_scalar(dst[:, tt, :], X[:, tt, :], ss[:, tt:tt + 1], None,
                                                            ALU.mult), *waits)
            return t

        G = ar(0, 6144, 24)
        CV = ar(6144, 8 * 286, 8)
        CVO = ar(8432, 2048, 8)
        U = ar(10480, 2048, 8)
        V = ar(12528, 2048, 2)
        ZP = ar(14576, 8 * 272, 8)
        ZB = ar(16752, 8 * 272, 8)
        ZC = ar(18928, 8 * 272, 8)
        TMP = ar(21104, 1024)
        TMP2 = ar(22128, 1024)
        XS = V

        t = norm_scaled(XS, TMP, dtok("x"), t_col)
        hts = to_T(lambda tt, k: XS[:, tt, k * 128:k * 128 + 128], HT, 8, lambda k: (col("g_mix_pre", k), None), t)

        mz = POOL.op(lambda e: e.memset(CV[:, :, 0:30], 0.0))
        mz2 = POOL.op(lambda e: e.memset(ZP[:, :, 0:16], 0.0))
        w_in = I["w_in"][0]

        for j in range(4):
            i, tw = stream((lambda r: k8(r)[:, :, 0:256], cols(w_in, 2048 + 256 * j, 256)),
                           (lambda r: k8(r)[:, :, 256:512], cols(w_in, 3072 + 256 * j, 256)))

            def glu(n, b, t, j=j):
                c = 2 * j + n
                h = n * 512
                s = ACT.op(lambda e: e.activation(TMP[:, h:h + 256], ps[b][:, 256:512], ACTF.Sigmoid), t,
                           glu_free[n])
                m = DVE.op(lambda e: e.tensor_tensor(CV[:, c, 30:286], ps[b][:, 0:256], TMP[:, h:h + 256],
                                                     ALU.mult), s, mz)
                glu_free[n] = m
                DVE.op(lambda e: e.tensor_scalar(CVO[:, c, :], CV[:, c, 0:256], tap(0, c), col("b_dw", c),
                                                 ALU.mult, ALU.add))
                for k in range(1, 31):
                    DVE.op(lambda e, k=k: e.scalar_tensor_tensor(
                        out=CVO[:, c, :], in0=CV[:, c, k:k + 256], scalar=tap(k, c), in1=CVO[:, c, :],
                        op0=ALU.mult, op1=ALU.add))
                return [m, s]

            if j == 0:
                glu_free = [None, None]
            ring_free[i] = fm_slot(k8(ring[i]), HT, [tw, *hts], glu, pairs=((0, 2), (1, 3)))
        t_cv = DVE.last

        vt = []
        for nn in range(2):
            i, tw = stream((k8, cols(w_in, 1024 + 512 * nn, 512)))
            for tt in range(2):
                b = bank()
                t = tmaj(lambda k: HT[:, k, :], lambda k, i=i: k8(ring[i])[:, k, :], 8, tt, b, [tw])
                a = ACT.op(lambda e, tt=tt, nn=nn, b=b: e.activation(
                    V[:, tt, nn * 512:nn * 512 + 512], ps[b][:, :], ACTF.Gelu_apprx_tanh), t)
                ps_free[b] = [a]
            ring_free[i] = t
        t_v = ACT.last
        for nn in range(2):
            i, tw = stream((k8, cols(w_in, 512 * nn, 512)))

            def gelu(n, b, t, nn=nn):
                return [ACT.op(lambda e: e.activation(
                    U[:, nn * 4 + 2 * n:nn * 4 + 2 * n + 2, :], ps[b][:, :].rearrange("p (k n) -> p k n", k=2),
                    ACTF.Gelu_apprx_tanh), t)]

            ring_free[i] = fm_slot(k8(ring[i]), HT, [tw], gelu)
        t_u = ACT.last
        GV, BV = ZB[:, :, :].rearrange("p k n -> p (k n)")[:, 0:1024], ZB[:, :, :].rearrange("p k n -> p (k n)")[:, 1024:2048]
        WS = ZC[:, :, :].rearrange("p k n -> p (k n)")[:, 0:1024]
        WST = ZC[:, :, :].rearrange("p k n -> p (k n)")[:, 1024:2048]
        SP.dma(GV, I["g_sgu_v"][0].partition_broadcast(128), dsem("gv"))
        SP.dma(BV, I["b_sgu_v"][0].partition_broadcast(128), dsem("gv"))
        SP.dma(WS.rearrange("p (h j) -> p h j", h=8), I["w_sgu_s"][0].rearrange("h i j -> i h j"), dsem("ws"))
        BSR = sb("bsr", [1, 1024])
        SP.dma(BSR[:, :], I["b_sgu_s"].rearrange("a h i -> a (h i)"), dsem("ws"))
        st, mv = small(24), small(4)
        for tt in range(2):
            for nn in range(2):
                DVE.op(lambda e, tt=tt, nn=nn: e.bn_stats(st[:, (tt * 2 + nn) * 6:(tt * 2 + nn) * 6 + 6],
                                                          V[:, tt, nn * 512:nn * 512 + 512]), t_v)
            t = DVE.op(lambda e, tt=tt: e.bn_aggr(mv[:, 2 * tt:2 * tt + 2], st[:, tt * 12:tt * 12 + 12]))
        for tt in range(2):
            a = ACT.op(lambda e, tt=tt: e.activation(mv[:, 2 * tt + 1:2 * tt + 2], mv[:, 2 * tt + 1:2 * tt + 2],
                                                     ACTF.Sqrt, bias=c_("eps")), t)
        for tt in range(2):
            DVE.op(lambda e, tt=tt: e.reciprocal(mv[:, 2 * tt + 1:2 * tt + 2], mv[:, 2 * tt + 1:2 * tt + 2]), a)
            DVE.op(lambda e, tt=tt: e.tensor_scalar(V[:, tt, :], V[:, tt, :], mv[:, 2 * tt:2 * tt + 1],
                                                    mv[:, 2 * tt + 1:2 * tt + 2], ALU.subtract, ALU.mult))
            DVE.op(lambda e, tt=tt: e.tensor_tensor(V[:, tt, :], V[:, tt, :], GV, ALU.mult), dtok("gv"))
            t_vn = DVE.op(lambda e, tt=tt: e.tensor_tensor(V[:, tt, :], V[:, tt, :], BV, ALU.add))

        gate_toks = []
        for s_ in range(6):
            i, tw = stream((k8, cols(w_in, 5120 + 512 * s_, 512)))

            def sig(n, b, t, s_=s_):
                return [ACT.op(lambda e: e.activation(
                    G[:, s_ * 4 + 2 * n:s_ * 4 + 2 * n + 2, :], ps[b][:, :].rearrange("p (k n) -> p k n", k=2),
                    ACTF.Sigmoid), t, t_col)]

            ring_free[i] = fm_slot(k8(ring[i]), HT, [tw], sig)
        t_g = ACT.last

        for h0 in (0, 4):
            b = bank()
            for h in range(h0, h0 + 4):
                f = (lambda e, h=h, b=b, h0=h0: e.transpose(ps[b][:, (h - h0) * 128:(h - h0) * 128 + 128],
                                                            WS[:, h * 128:h * 128 + 128], ident))
                t = PE.op(f, dtok("ws"), *ps_free[b])
            a = DVE.op(lambda e, b=b, h0=h0: e.tensor_tensor(
                WST[:, h0 * 128:h0 * 128 + 512].rearrange("p (h i) -> p h i", h=4),
                ps[b][:, :].rearrange("p (h i) -> p h i", h=4),
                c_("sgum").unsqueeze(1).broadcast_to((128, 4, 128)), ALU.mult), t)
            ps_free[b] = [a]
        t_ws = a
        for h0 in range(0, 8, 2):
            b = bank()
            for h in (h0, h0 + 1):
                for tt in range(2):
                    o = (h - h0) * 256 + tt * 128
                    PE.quiet(lambda e, b=b, o=o, h=h: e.matmul(ps[b][:, o:o + 128], ones[0:1, :],
                                                               BSR[0:1, h * 128:h * 128 + 128],
                                                               start=True, stop=False), t_ws, t_vn, *ps_free[b])
                    t = PE.op(lambda e, b=b, o=o, h=h, tt=tt: e.matmul(
                        ps[b][:, o:o + 128], V[:, tt, h * 128:h * 128 + 128], WST[:, h * 128:h * 128 + 128],
                        start=False, stop=True))
            a = DVE.op(lambda e, b=b, h0=h0: e.tensor_tensor(
                U[:, h0:h0 + 2, :], U[:, h0:h0 + 2, :], ps[b][:, :].rearrange("p (k n) -> p k n", k=2),
                ALU.mult), t, t_u)
            ps_free[b] = [a]
        t_um = a
        t_mix = t

        def branch(src, w, br, *waits):
            for nn in range(2):
                i, tw = stream((k8, cols(w, 512 * nn, 512)))

                def ev(n, b, t, nn=nn):
                    k = nn * 4 + 2 * n
                    pv = ps[b][:, :].rearrange("p (k n) -> p k n", k=2)
                    if br == 0:
                        return [DVE.op(lambda e: e.tensor_tensor(G[:, k:k + 2, :], G[:, k:k + 2, :], pv, ALU.mult),
                                       t, t_g)]
                    q = G[:, br * 8 + k:br * 8 + k + 2, :]
                    a = DVE.op(lambda e: e.tensor_tensor(q, q, pv, ALU.mult), t, t_g)
                    DVE.op(lambda e: e.tensor_tensor(G[:, k:k + 2, :], G[:, k:k + 2, :], q, ALU.add))
                    return [a]

                ring_free[i] = fm_slot(k8(ring[i]), src, [tw, *waits], ev)

        branch(U, I["w_sgu_out"][0], 0, t_um)

        for nn in range(2):
            i, tw = stream((k8, cols(w_in, 4096 + 512 * nn, 512)))

            def zcp(n, b, t, nn=nn):
                k = nn * 4 + 2 * n
                return [ACT.op(lambda e: e.activation(ZP[:, k:k + 2, 16:272],
                                                      ps[b][:, :].rearrange("p (k n) -> p k n", k=2), ACTF.Copy),
                               t, mz2)]

            ring_free[i] = fm_slot(k8(ring[i]), HT, [tw], zcp)
        t_z = ACT.last
        POOL.op(lambda e: e.tensor_tensor(ZB[:, :, 1:272], ZP[:, :, 1:272], ZP[:, :, 0:271], ALU.add), t_z, t_um,
                t_mix)
        POOL.op(lambda e: e.tensor_tensor(ZC[:, 2:8, 3:272], ZB[:, 2:8, 3:272], ZB[:, 2:8, 1:270], ALU.add))
        POOL.op(lambda e: e.tensor_tensor(ZB[:, 4:8, 7:272], ZC[:, 4:8, 7:272], ZC[:, 4:8, 3:268], ALU.add))
        t_p = POOL.op(lambda e: e.tensor_tensor(ZC[:, 6:8, 15:272], ZB[:, 6:8, 15:272], ZB[:, 6:8, 7:264], ALU.add))
        o = const_at["invc"][0]
        for g, (S_, w) in enumerate(zip((ZB, ZC, ZB, ZC), WIN)):
            k = 2 * g
            inv = CST[:, o + 16 * g:o + 16 * g + 16].unsqueeze(1).broadcast_to((128, 2, 16))
            DVE.op(lambda e, S_=S_, k=k, inv=inv: e.tensor_tensor(S_[:, k:k + 2, 16:32], S_[:, k:k + 2, 16:32], inv,
                                                                  ALU.mult), t_p)
            DVE.op(lambda e, S_=S_, k=k: e.tensor_tensor(ZP[:, k:k + 2, 16:32], S_[:, k:k + 2, 16:32],
                                                         ZP[:, k:k + 2, 16:32], ALU.subtract))
            t_pl = DVE.op(lambda e, S_=S_, k=k, w=w: e.scalar_tensor_tensor(
                out=ZP[:, k:k + 2, 32:272], in0=S_[:, k:k + 2, 32:272], scalar=1.0 / w, in1=ZP[:, k:k + 2, 32:272],
                op0=ALU.mult, op1=ALU.subtract))

        b = bank()
        for c in range(8):
            t = PE.op(lambda e, c=c, b=b: e.matmul(ps[b][:, 0:256], mean, CVO[:, c, :], start=(c == 0),
                                                   stop=(c == 7)), t_cv, *ps_free[b])
        t = DVE.op(lambda e, b=b: e.tensor_tensor(CVO, CVO, ps[b][:, 0:256].unsqueeze(1).broadcast_to((128, 8, 256)),
                                                  ALU.subtract), t)
        ps_free[b] = [t]
        SQ = ZB[:, :, 0:256]
        t = ACT.op(lambda e: e.activation(SQ, CVO, ACTF.Square), t, t_pl)
        b = bank()
        for c in range(8):
            t2 = PE.op(lambda e, c=c, b=b: e.matmul(ps[b][:, 0:256], mean, SQ[:, c, :], start=(c == 0),
                                                    stop=(c == 7)), t, *ps_free[b])
        RS = TMP[:, 0:256]
        t = ACT.op(lambda e, b=b: e.activation(RS, ps[b][:, 0:256], ACTF.Sqrt, bias=c_("eps")), t2, t_cv)
        ps_free[b] = [t]
        t = DVE.op(lambda e: e.reciprocal(RS, RS), t)
        t = DVE.op(lambda e: e.tensor_tensor(CVO, CVO, RS.unsqueeze(1).broadcast_to((128, 8, 256)), ALU.mult))
        for c in range(8):
            t_cs = ACT.op(lambda e, c=c: e.activation(CVO[:, c, :], CVO[:, c, :], ACTF.Silu,
                                                      bias=col("b_conv_ln", c), scale=col("g_conv_ln", c)), t)

        i, tw = stream((lambda r: r[:, 0:2048].rearrange("p (g k n) -> p g k n", g=4, k=2),
                        I["w_pool"][0].rearrange("g (k p) n -> p g k n", p=128)))
        WP = ring[i][:, 0:2048].rearrange("p (g k n) -> p g k n", g=4, k=2)
        PM = ZC[:, :, 0:256]
        for g in range(4):
            b = bank()
            for d in range(2):
                for k in range(2):
                    t = PE.op(lambda e, b=b, d=d, k=k, g=g: e.matmul(
                        ps[b][:, d * 256:d * 256 + 256], WP[:, g, k, d * 128:d * 128 + 128],
                        ZP[:, 2 * g + k, 16:272], start=(k == 0), stop=(k == 1)), tw, t_pl, *ps_free[b])
            for d in range(2):
                a = ACT.op(lambda e, b=b, d=d, g=g: e.activation(PM[:, 2 * g + d, :], ps[b][:, d * 256:d * 256 + 256],
                                                                 ACTF.Copy, scale=col("s_pool", 2 * g + d)), t)
            ps_free[b] = [a]
        ring_free[i] = t
        branch(PM, I["w_pool_out"][0], 2, a)
        branch(CVO, I["w_conv_out"][0], 1, t_cs)
        t_m = DVE.last

        GR = U[:, :, :].rearrange("p k n -> p (k n)")[:, 0:1024]
        SP.dma(GR, I["g_mix_post"][0].partition_broadcast(128), dsem("gmp"), t_um, PE.last)
        banks, toks = [None] * 4, [None] * 4
        for nn in range(2):
            i, tw = stream((k8, cols(I["w_out"][0], 512 * nn, 512)))
            for tt in range(2):
                b = bank()
                toks[tt * 2 + nn] = tmaj(lambda k: G[:, k, :], lambda k, i=i: k8(ring[i])[:, k, :], 8, tt, b,
                                         [tw, t_m])
                banks[tt * 2 + nn] = b
            ring_free[i] = PE.last
        t_x1 = post_norm(banks, toks, GR, dtok("gmp"), TMP)

        XS = V
        t = norm_scaled(XS, TMP, t_x1, PE.last)
        hts = to_T(lambda tt, k: XS[:, tt, k * 128:k * 128 + 128], HT, 8, lambda k: (col("g_ffn_pre", k), None), t)
        FF = ar(0, NFF * 256, NFF)
        ADA = ar(5632, 6144)
        GR2 = ar(14576, 1024)
        SP.dma(GR2, I["g_ffn_post"][0].partition_broadcast(128), dsem("gfp"), PE.last, DVE.last)
        cond = small(8)
        t_c = ACT.op(lambda e: e.activation(cond, COL[:, row_at["c_2"]:row_at["c_2"] + 8], ACTF.Silu))
        t_az = POOL.op(lambda e: e.memset(ADA, 0.0), t_x1, PE.last)
        SP.dma(ADA[0:1, :], I["b_ada_2"], dsem("ada"), t_az)
        w_ff, w_ada = I["w_ffn_in"][0], I["w_ada_2"][0]

        def ada(m):
            i, tw = stream((k8, cols(w_ada, 512 * m, 512)))
            for k in range(8):
                a = DVE.op(lambda e, i=i, k=k, m=m: e.scalar_tensor_tensor(
                    out=ADA[:, 512 * m:512 * m + 512], in0=k8(ring[i])[:, k, :], scalar=cond[:, k:k + 1],
                    in1=ADA[:, 512 * m:512 * m + 512], op0=ALU.mult, op1=ALU.add), tw, t_c, dtok("ada"))
            ring_free[i] = a
            return a

        sil = [None, None]
        t_pe = PE.last
        for j in range(11):
            i, tw = stream((lambda r: k8(r)[:, :, 0:256], cols(w_ff, 256 * j, 256)),
                           (lambda r: k8(r)[:, :, 256:512], cols(w_ff, 2816 + 256 * j, 256)))

            def ffg(n, b, t, j=j):
                h = n * 512
                s = ACT.op(lambda e: e.activation(TMP[:, h:h + 256], ps[b][:, 0:256], ACTF.Silu), t, sil[n], t_x1)
                m = DVE.op(lambda e: e.tensor_tensor(FF[:, 2 * j + n, :], ps[b][:, 256:512], TMP[:, h:h + 256],
                                                     ALU.mult), s, t_pe)
                sil[n] = m
                return [m, s]

            ring_free[i] = fm_slot(k8(ring[i]), HT, [tw, *hts], ffg, pairs=((0, 2), (1, 3)))
            ada(j)
        t_ada = ada(11)
        t_ff = sil[1]
        banks = [bank() for _ in range(4)]
        w_fo = I["w_ffn_out"][0]
        for s_ in range(6):
            n = 4 if s_ < 5 else 2
            i, tw = stream((lambda r, n=n: r[:, 0:1024 * n].rearrange("p (k n) -> p k n", k=n),
                            w_fo[512 * s_:512 * s_ + 128 * n, :].rearrange("(k p) n -> p k n", p=128)))
            W = ring[i][:, :].rearrange("p (k n) -> p k n", k=4)
            for j in range(4):
                tt, nn = j // 2, j % 2
                toks[j] = tmaj(lambda k, s_=s_: FF[:, 4 * s_ + k, :], lambda k, W=W, nn=nn: W[:, k, nn * 512:nn * 512 + 512],
                               n, tt, banks[j], [tw, t_ff], start=(s_ == 0), stop=(s_ == 5))
            ring_free[i] = PE.last
        t_x2 = post_norm(banks, toks, GR2, dtok("gfp"), TMP)

        PT_ = ar(12000, 512, 2)
        PR = ar(12512, 512, 2)
        SP.dma(PR, I["p"][0, 0].rearrange("(t p) d -> p t d", p=128), dsem("p"), t_ff)
        h2 = to_T(lambda tt, k: X[:, tt, k * 128:k * 128 + 128], HT, 8, None, t_x2)
        pts = to_T(lambda tt, k: PR[:, tt, k * 128:k * 128 + 128], PT_, 2, None, dtok("p"))
        i0, tw0 = stream((lambda r: r[:, 0:2048].rearrange("p (k n) -> p k n", k=2),
                          I["w_ple"][0].rearrange("(k p) n -> p k n", p=128)))
        WPL = ring[i0][:, 0:2048].rearrange("p (k n) -> p k n", k=2)
        for nn in range(2):
            i, tw = stream((k8, cols(I["w_ple_gate"][0], 512 * nn, 512)))
            for tt in range(2):
                b = bank()
                t = tmaj(lambda k: HT[:, k, :], lambda k, i=i: k8(ring[i])[:, k, :], 8, tt, b, [tw, *h2])
                b2 = bank()
                t2 = tmaj(lambda k: PT_[:, k, :], lambda k, nn=nn: WPL[:, k, nn * 512:nn * 512 + 512], 2, tt, b2,
                          [tw0, *pts])
                a = ACT.op(lambda e, b=b: e.activation(TMP[:, 0:512], ps[b][:, :], ACTF.Sigmoid), t, DVE.last)
                ps_free[b] = [a]
                a = DVE.op(lambda e, b2=b2: e.tensor_tensor(TMP[:, 512:1024], TMP[:, 0:512], ps[b2][:, :], ALU.mult),
                           a, t2)
                ps_free[b2] = [a]
                t_x3 = DVE.op(lambda e, tt=tt, nn=nn: e.tensor_tensor(
                    X[:, tt, nn * 512:nn * 512 + 512], X[:, tt, nn * 512:nn * 512 + 512], TMP[:, 512:1024], ALU.add))
            ring_free[i] = PE.last
        ring_free[i0] = PE.last

        MC = small(16)
        b = bank()
        for j in range(16):
            t = PE.op(lambda e, j=j, b=b: e.matmul(ps[b][:, j:j + 1], ADA[:, 128 * j:128 * j + 128], ones[:, 0:1],
                                                   start=True, stop=True), t_ada, *ps_free[b])
        t = DVE.op(lambda e, b=b: e.tensor_copy(MC, ps[b][:, 0:16]), t)
        ps_free[b] = [t]
        t_mc = DVE.op(lambda e: e.scalar_tensor_tensor(out=MC[:, 8:16], in0=MC[:, 8:16], scalar=1.0,
                                                       in1=COL[:, row_at["g_mix_2"]:row_at["g_mix_2"] + 8],
                                                       op0=ALU.add, op1=ALU.mult))
        MR = ADA[:, 2048:6144].rearrange("p (k n) -> p k n", k=4)
        for j in range(8):
            b = bank()
            v = ADA[:, 2048 + 512 * j:2560 + 512 * j]
            t = PE.op(lambda e, b=b, v=v: e.matmul(ps[b][:, :], ones, v, start=True, stop=True), *ps_free[b], t_ada)
            a = ACT.op(lambda e, b=b, v=v: e.activation(v, ps[b][:, :], ACTF.Copy), t)
            ps_free[b] = [a]
        t_mr = a

        XS = ar(14576, 2048, 2)
        t = norm_scaled(XS, TMP, t_x3, PE.last)
        hts = to_T(lambda tt, k: XS[:, tt, k * 128:k * 128 + 128], HT, 8,
                   lambda k: (MC[:, 8 + k:9 + k], MC[:, k:k + 1]), t, t_mc)
        w2 = I["w_in_2"][0]
        QK = [ar(1024 * n, 1024, 4) for n in range(4)]
        VV = [ar(4096, 1024, 2), ar(11776, 1024, 2)]
        t_qk = {}
        for n, (kind, a0) in enumerate((("qs", 1536), ("ks", 2048), ("vs", 2560), ("qd", 0), ("kd", 512), ("vd", 1024))):
            i, tw = stream((k8, cols(w2, a0, 512)))
            if kind[0] == "v":
                dst = VV[0] if kind == "vd" else VV[1]
                for tt in range(2):
                    b = bank()
                    t = tmaj(lambda k: HT[:, k, :], lambda k, i=i: k8(ring[i])[:, k, :], 8, tt, b, [tw, *hts])
                    ps_free[b] = [ACT.op(lambda e, tt=tt, b=b, dst=dst: e.activation(dst[:, tt, :], ps[b][:, :],
                                                                                    ACTF.Copy), t, t_x3)]
                ring_free[i] = PE.last
            else:
                dst = QK[("qd", "kd", "qs", "ks").index(kind)]

                def cp(n, b, t, dst=dst):
                    return [ACT.op(lambda e: e.activation(dst[:, 2 * n:2 * n + 2, :],
                                                          ps[b][:, :].rearrange("p (k n) -> p k n", k=2), ACTF.Copy),
                                   t, t_x3)]

                ring_free[i] = fm_slot(k8(ring[i]), HT, [tw, *hts], cp)
            t_qk[kind] = ACT.last

        def head(n, h):
            return QK[n][64 * (h % 2):64 * (h % 2) + 64, h // 2, :]

        OD, OS = ar(14576, 1024, 2), ar(15600, 1024, 2)
        LA = ar(16624, 4 * 384, 4)
        LB = ar(18160, 4 * 384, 4)
        LC = ar(19696, 4 * 384, 4)
        t_hts = PE.last
        before, upto = c_("before"), c_("upto")
        for hg in (0, 4):
            zb = []
            for h in range(hg, hg + 4):
                b = bank()
                zb.append(b)
                PE.quiet(lambda e, b=b, h=h: e.matmul(ps[b][:, 0:256], head(3, h)[:, 0:128], head(2, h),
                                                      start=True, stop=True), t_qk["qs"], t_qk["ks"], *ps_free[b])
                t = PE.op(lambda e, b=b, h=h: e.matmul(ps[b][:, 256:384], head(3, h)[:, 128:256],
                                                       head(2, h)[:, 128:256], start=True, stop=True))
                ACT.op(lambda e, b=b, h=h: e.activation(LA[:, h % 4, :], ps[b][:, 0:384], ACTF.Copy, scale=0.125),
                       t, t_hts, t_x3, DVE.last)
                a = ACT.op(lambda e, b=b, h=h: e.activation(LB[:, h % 4, :], ps[b][:, 0:384], ACTF.Abs, scale=0.125))
                ps_free[b] = [a]
            ACT.op(lambda e: e.activation(LB, LB, ACTF.Exp, scale=-1.0))
            a = ACT.op(lambda e: e.activation(LB, LB, ACTF.Ln, bias=c_("one")))
            DVE.op(lambda e: e.scalar_tensor_tensor(out=LB, in0=LA, scalar=0.0, in1=LB, op0=ALU.max, op1=ALU.add), a)
            for o in (0, 256):
                t = DVE.op(lambda e, o=o: e.tensor_tensor(
                    LB[:, :, o:o + 128], LB[:, :, o:o + 128], before.unsqueeze(1).broadcast_to((128, 4, 128)),
                    ALU.mult))
            for h in range(4):
                b = bank()
                PE.quiet(lambda e, b=b, h=h: e.matmul(ps[b][:, 0:128], upto, LB[:, h, 0:128], start=True, stop=True),
                         t, *ps_free[b])
                PE.quiet(lambda e, b=b, h=h: e.matmul(ps[b][:, 128:256], upto, LB[:, h, 128:256], start=True,
                                                      stop=False))
                PE.quiet(lambda e, b=b, h=h: e.matmul(ps[b][:, 128:256], ones, LB[:, h, 256:384], start=False,
                                                      stop=True))
                t3 = PE.op(lambda e, b=b, h=h: e.matmul(ps[b][:, 256:384], upto, LB[:, h, 256:384], start=True,
                                                        stop=True))
                a = DVE.op(lambda e, b=b, h=h: e.tensor_tensor(LA[:, h, :], LA[:, h, :], ps[b][:, 0:384],
                                                               ALU.subtract), t3)
                ps_free[b] = [a]
            t = DVE.op(lambda e: e.scalar_tensor_tensor(
                out=LA, in0=LA, scalar=0.0, in1=c_("sbneg").unsqueeze(1).broadcast_to((128, 4, 384)),
                op0=ALU.min, op1=ALU.add))
            a = ACT.op(lambda e: e.activation(LA, LA, ACTF.Exp), t)
            b0, b1 = bank(), bank()
            for h in range(4):
                hh = (hg + h) * 64
                o = h * 64
                PE.quiet(lambda e, h=h, o=o, hh=hh, b0=b0: e.matmul(ps[b0][:, o:o + 64], LA[:, h, 0:128],
                                                                    VV[1][:, 0, hh:hh + 64], start=True, stop=True),
                         a, t_qk["vs"], *ps_free[b0])
                PE.quiet(lambda e, h=h, o=o, hh=hh, b1=b1: e.matmul(ps[b1][:, o:o + 64], LA[:, h, 128:256],
                                                                    VV[1][:, 0, hh:hh + 64], start=True, stop=False),
                         *ps_free[b1])
                t = PE.op(lambda e, h=h, o=o, hh=hh, b1=b1: e.matmul(ps[b1][:, o:o + 64], LA[:, h, 256:384],
                                                                     VV[1][:, 1, hh:hh + 64], start=False, stop=True))
            for tt, b in ((0, b0), (1, b1)):
                ps_free[b] = [DVE.op(lambda e, tt=tt, b=b, hg=hg: e.tensor_copy(
                    OS[:, tt, hg * 64:hg * 64 + 256], ps[b][:, 0:256]), t)]

        mx, den = small(16), small(16)
        mx3, den3 = (v.rearrange("p (t h) -> p t h", t=2) for v in (mx, den))
        for hg in (0, 4):
            for h in range(hg, hg + 4):
                b = bank()
                PE.quiet(lambda e, b=b, h=h: e.matmul(ps[b][:, 0:128], head(0, h)[:, 0:128], head(1, h)[:, 0:128],
                                                      start=True, stop=True), t_qk["qd"], t_qk["kd"], *ps_free[b])
                t = PE.op(lambda e, b=b, h=h: e.matmul(ps[b][:, 128:384], head(0, h)[:, 128:256], head(1, h),
                                                       start=True, stop=True))
                slope = 2.0 ** -(h + 1)
                a = DVE.op(lambda e, b=b, h=h, slope=slope: e.scalar_tensor_tensor(
                    out=LC[:, h % 4, :], in0=c_("dist"), scalar=-8.0 * slope, in1=ps[b][:, 0:384],
                    op0=ALU.mult, op1=ALU.add), t, PE.last)
                ps_free[b] = [a]
            DVE.op(lambda e, hg=hg: e.reduce_max(mx3[:, 0, hg:hg + 4], LC[:, :, 0:128], AX))
            DVE.op(lambda e, hg=hg: e.reduce_max(mx3[:, 1, hg:hg + 4], LC[:, :, 128:384], AX))
            t = DVE.op(lambda e, hg=hg: e.tensor_scalar(mx3[:, :, hg:hg + 4], mx3[:, :, hg:hg + 4], -0.125, None,
                                                        ALU.mult))
            for h in range(4):
                for tt, o, n in ((0, 0, 128), (1, 128, 256)):
                    a = ACT.op(lambda e, h=h, tt=tt, o=o, n=n, hg=hg: e.activation(
                        LC[:, h, o:o + n], LC[:, h, o:o + n], ACTF.Exp, bias=mx3[:, tt, hg + h:hg + h + 1],
                        scale=0.125), t)
            DVE.op(lambda e: e.tensor_tensor(LC, LC, c_("count").unsqueeze(1).broadcast_to((128, 4, 384)),
                                             ALU.mult), a)
            t_lc = DVE.last
            DVE.op(lambda e, hg=hg: e.reduce_sum(den3[:, 0, hg:hg + 4], LC[:, :, 0:128], AX))
            DVE.op(lambda e, hg=hg: e.reduce_sum(den3[:, 1, hg:hg + 4], LC[:, :, 128:384], AX))
            DVE.op(lambda e, hg=hg: e.reciprocal(den3[:, :, hg:hg + 4], den3[:, :, hg:hg + 4]))
            for h in range(4):
                b = bank()
                for o in (0, 128, 256):
                    t = PE.op(lambda e, b=b, h=h, o=o: e.transpose(ps[b][:, o:o + 128], LC[:, h, o:o + 128], ident),
                              t_lc, *ps_free[b])
                a = ACT.op(lambda e, b=b, h=h: e.activation(LB[:, h, :], ps[b][:, 0:384], ACTF.Copy), t, DVE.last)
                ps_free[b] = [a]
            b0, b1 = bank(), bank()
            for h in range(4):
                hh = (hg + h) * 64
                o = h * 64
                PE.quiet(lambda e, h=h, o=o, hh=hh, b0=b0: e.matmul(ps[b0][:, o:o + 64], LB[:, h, 0:128],
                                                                    VV[0][:, 0, hh:hh + 64], start=True, stop=True),
                         a, t_qk["vd"], *ps_free[b0])
                PE.quiet(lambda e, h=h, o=o, hh=hh, b1=b1: e.matmul(ps[b1][:, o:o + 64], LB[:, h, 128:256],
                                                                    VV[0][:, 0, hh:hh + 64], start=True, stop=False),
                         *ps_free[b1])
                t = PE.op(lambda e, h=h, o=o, hh=hh, b1=b1: e.matmul(ps[b1][:, o:o + 64], LB[:, h, 256:384],
                                                                     VV[0][:, 1, hh:hh + 64], start=False, stop=True))
            for tt, b in ((0, b0), (1, b1)):
                ps_free[b] = [DVE.op(lambda e, tt=tt, b=b, hg=hg: e.tensor_tensor(
                    OD[:, tt, hg * 64:hg * 64 + 256].rearrange("p (h c) -> p h c", h=4),
                    ps[b][:, 0:256].rearrange("p (h c) -> p h c", h=4),
                    den3[:, tt, hg:hg + 4].unsqueeze(2).broadcast_to((128, 4, 64)), ALU.mult), t)]
        ss = small(4)
        for n, O in enumerate((OD, OS)):
            for tt in range(2):
                t = ACT.op(lambda e, n=n, O=O, tt=tt: e.activation(TMP[:, 0:512], O[:, tt, :], ACTF.Square,
                                                                   accum_out=ss[:, 2 * n + tt:2 * n + tt + 1]),
                           DVE.last)
        t = rstd(ss, 1.0 / 512, t)
        for n, O in enumerate((OD, OS)):
            for tt in range(2):
                t = DVE.op(lambda e, n=n, O=O, tt=tt: e.tensor_scalar(O[:, tt, :], O[:, tt, :],
                                                                      ss[:, 2 * n + tt:2 * n + tt + 1], None, ALU.mult))
        mts = to_T(lambda tt, k: (OD if k < 4 else OS)[:, tt, (k % 4) * 128:(k % 4) * 128 + 128], HT, 8,
                   lambda k: (col("g_dil_out_2", k) if k < 4 else col("g_sb_out_2", k - 4), None), t)
        for nn in range(2):
            i, tw = stream((k8, cols(I["w_out_2"][0], 512 * nn, 512)))
            for tt in range(2):
                b = bank()
                t = tmaj(lambda k: HT[:, k, :], lambda k, i=i: k8(ring[i])[:, k, :], 8, tt, b, [tw, *mts])
                a = DVE.op(lambda e, b=b, nn=nn: e.tensor_tensor(TMP[:, 0:512], ps[b][:, :],
                                                                 MR[:, 0, nn * 512:nn * 512 + 512], ALU.mult),
                           t, t_mr)
                ps_free[b] = [a]
                t_x4 = DVE.op(lambda e, tt=tt, nn=nn: e.tensor_tensor(
                    X[:, tt, nn * 512:nn * 512 + 512], X[:, tt, nn * 512:nn * 512 + 512], TMP[:, 0:512], ALU.add))
            ring_free[i] = PE.last

        GF2 = ar(0, 1024)
        GFI = ar(1024, 1024)
        SP.dma(GF2, I["g_ffn_2"][0].partition_broadcast(128), dsem("gf2"), t_x4)
        SP.dma(GFI, I["g_final_2"].partition_broadcast(128), dsem("gfi"), t_x4)
        WR = ar(2048, 8 * 36, 8)
        SP.dma(WR[:, :, 0:4], I["w_group_2"][0].rearrange("(k p) n -> p k n", p=128), dsem("wr"), t_x4)
        SP.dma(WR[:, :, 4:36], I["w_expert_2"][0].rearrange("(k p) n -> p k n", p=128), dsem("wr"), t_x4)
        H2 = ar(14576, 2048, 2)
        t = norm_scaled(H2, TMP, t_x4, PE.last)
        DVE.op(lambda e: e.scalar_tensor_tensor(out=GF2, in0=MR[:, 2, :], scalar=1.0, in1=GF2, op0=ALU.add,
                                                op1=ALU.mult), dtok("gf2"), t_mr)
        for tt in range(2):
            DVE.op(lambda e, tt=tt: e.tensor_tensor(H2[:, tt, :], H2[:, tt, :], GF2, ALU.mult))
            t = DVE.op(lambda e, tt=tt: e.tensor_tensor(H2[:, tt, :], H2[:, tt, :], MR[:, 1, :], ALU.add))
        hts = to_T(lambda tt, k: H2[:, tt, k * 128:k * 128 + 128], HT, 8, None, t)
        RT = sb("RT", [128, 2, 36])
        for tt in range(2):
            b = bank()
            t = tmaj(lambda k: HT[:, k, :], lambda k: WR[:, k, :], 8, tt, b, [dtok("wr"), *hts], n=36)
            ps_free[b] = [DVE.op(lambda e, tt=tt, b=b: e.tensor_copy(RT[:, tt, :], ps[b][:, 0:36]), t)]
        gm, gs = small(2), small(2)
        GE, G1 = small(8).rearrange("p (t g) -> p t g", t=2), small(8).rearrange("p (t g) -> p t g", t=2)
        iota = c_("iota")
        gl = RT[:, :, 0:4]

        def bc(v, n):
            return v.unsqueeze(2).broadcast_to((128, 2, n))

        def first_max(vals, n, mx_, hot, tmp):
            ix = small(2)
            io = iota[:, 0:n].unsqueeze(1).broadcast_to((128, 2, n))
            DVE.op(lambda e: e.reduce_max(mx_, vals, AX))
            DVE.op(lambda e: e.tensor_tensor(tmp, vals, bc(mx_, n), ALU.is_lt))
            DVE.op(lambda e: e.scalar_tensor_tensor(out=tmp, in0=tmp, scalar=64.0, in1=io, op0=ALU.mult, op1=ALU.add))
            DVE.op(lambda e: e.tensor_reduce(ix, tmp, AX, ALU.min))
            return DVE.op(lambda e: e.tensor_tensor(hot, io, bc(ix, n), ALU.is_equal))

        first_max(gl, 4, gm, G1, GE)
        DVE.op(lambda e: e.tensor_tensor(GE, gl, bc(gm, 4), ALU.subtract))
        t = ACT.op(lambda e: e.activation(GE, GE, ACTF.Exp), DVE.last)
        DVE.op(lambda e: e.reduce_sum(gs, GE, AX), t)
        DVE.op(lambda e: e.reciprocal(gs, gs))
        DVE.op(lambda e: e.tensor_scalar(G1, G1, 1.0, BIG, ALU.subtract, ALU.mult))
        el = RT[:, :, 4:36]
        for g in range(4):
            DVE.op(lambda e, g=g: e.tensor_tensor(el[:, :, 8 * g:8 * g + 8], el[:, :, 8 * g:8 * g + 8],
                                                  bc(G1[:, :, g], 8), ALU.add))
        hot1, hot2, tmp = (small(64).rearrange("p (t g) -> p t g", t=2) for _ in range(3))
        m1, m2, dd = small(2), small(2), small(2)
        first_max(el, 32, m1, hot1, tmp)
        DVE.op(lambda e: e.scalar_tensor_tensor(out=el, in0=hot1, scalar=-3.0 * BIG, in1=el, op0=ALU.mult,
                                                op1=ALU.add))
        first_max(el, 32, m2, hot2, tmp)
        DVE.op(lambda e: e.tensor_tensor(dd, m2, m1, ALU.subtract))
        t = ACT.op(lambda e: e.activation(dd, dd, ACTF.Exp), DVE.last)
        DVE.op(lambda e: e.tensor_scalar(m1, dd, 1.0, None, ALU.add), t)
        DVE.op(lambda e: e.reciprocal(m1, m1))
        DVE.op(lambda e: e.tensor_tensor(m1, m1, gs, ALU.mult))
        DVE.op(lambda e: e.tensor_tensor(m2, m1, dd, ALU.mult))
        WC = sb("WC", [128, 2, 32])
        DVE.op(lambda e: e.tensor_tensor(WC[:, :, :], hot1, bc(m1, 32), ALU.mult))
        DVE.op(lambda e: e.tensor_tensor(tmp, hot2, bc(m2, 32), ALU.mult))
        t_wc = DVE.op(lambda e: e.tensor_tensor(WC[:, :, :], WC[:, :, :], tmp, ALU.add))

        Y = ar(16624, 2048, 2)
        HH = ar(18672, 1024, 4)
        t_y = POOL.op(lambda e: e.memset(Y, 0.0), t_wc, PE.last)
        sil = [None, None]
        for x in range(NE):
            ig, tg = stream((k8, cols(I["w_gate_2"][0, x], 0, 512)))
            iu, tu = stream((k8, cols(I["w_up_2"][0, x], 0, 512)))
            idn, td = stream((lambda r: r[:, :].rearrange("p (k n) -> p k n", k=4),
                              I["w_down_2"][0, x].rearrange("(k p) n -> p k n", p=128)))
            t_dn = PE.last
            for f in range(4):
                b = bank()
                fm(k8(ring[ig]), f, HT, 8, b, 0, [tg, tu], ps_free[b], False)
                t = fm(k8(ring[iu]), f, HT, 8, b, 256, [], (), True)
                h = (f % 2) * 512
                s = ACT.op(lambda e, b=b, h=h: e.activation(TMP[:, h:h + 256], ps[b][:, 0:256], ACTF.Silu), t,
                           sil[f % 2], t_wc)
                m = DVE.op(lambda e, b=b, h=h, f=f: e.tensor_tensor(HH[:, f, :], ps[b][:, 256:512],
                                                                   TMP[:, h:h + 256], ALU.mult), s, t_dn)
                sil[f % 2] = m
                ps_free[b] = [m, s]
            ring_free[ig] = ring_free[iu] = t
            W = ring[idn][:, :].rearrange("p (k n) -> p k n", k=4)
            for tt in range(2):
                for nn in range(2):
                    b = bank()
                    t = tmaj(lambda k: HH[:, k, :], lambda k, W=W, nn=nn: W[:, k, nn * 512:nn * 512 + 512], 4, tt, b,
                             [td, m])
                    a = DVE.op(lambda e, b=b, tt=tt, nn=nn, x=x: e.scalar_tensor_tensor(
                        out=Y[:, tt, nn * 512:nn * 512 + 512], in0=ps[b][:, :], scalar=WC[:, tt, x:x + 1],
                        in1=Y[:, tt, nn * 512:nn * 512 + 512], op0=ALU.mult, op1=ALU.add), t, t_y)
                    ps_free[b] = [a]
            ring_free[idn] = t
        for tt in range(2):
            DVE.op(lambda e, tt=tt: e.tensor_tensor(Y[:, tt, :], Y[:, tt, :], MR[:, 3, :], ALU.mult))
            DVE.op(lambda e, tt=tt: e.tensor_tensor(X[:, tt, :], X[:, tt, :], Y[:, tt, :], ALU.add))
        t = norm_scaled(H2, TMP, DVE.last)
        for tt in range(2):
            t = DVE.op(lambda e, tt=tt: e.tensor_tensor(H2[:, tt, :], H2[:, tt, :], GFI, ALU.mult), dtok("gfi"))
        SP.dma(out[0].rearrange("(t p) d -> p t d", p=128), H2, dsem("out"), t)
        SP.wait(dtok("out"))

        block = ctx.enter_context(nc.Block())
        block.sync(SP.emit)
        block.gpsimd(POOL.emit)
        block.scalar(ACT.emit)
        block.vector(DVE.emit)
        block.tensor(PE.emit)


_INS = ["x", "p", "g_mix_pre", "w_in", "w_sgu_s", "b_sgu_s", "g_sgu_v", "b_sgu_v", "w_sgu_out", "w_dw", "b_dw",
        "g_conv_ln", "b_conv_ln", "w_conv_out", "w_pool", "s_pool", "w_pool_out", "w_out", "g_mix_post",
        "g_ffn_pre", "w_ffn_in", "w_ffn_out", "g_ffn_post", "w_ple", "w_ple_gate", "c_2", "w_ada_2", "b_ada_2",
        "g_mix_2", "w_in_2", "g_dil_out_2", "g_sb_out_2", "w_out_2", "g_ffn_2", "w_group_2", "w_expert_2",
        "w_gate_2", "w_up_2", "w_down_2", "g_final_2"]


def kernel(**inputs):
    import concourse.bacc as _bacc
    from concourse.bass_utils import run_bass_kernel_spmd as _run

    nc = _bacc.Bacc("TRN2", target_bir_lowering=False, num_devices=1)
    arrays, I = {}, {}
    for name in _INS:
        a = np.ascontiguousarray(inputs[name])
        arrays[f"in_{name}"] = a
        I[name] = nc.dram_tensor(f"in_{name}", a.shape, mybir.dt.from_np(a.dtype), kind="ExternalInput").ap()
    cst, at = constants()
    arrays["in_cst"] = cst
    I["cst"] = nc.dram_tensor("in_cst", cst.shape, F32, kind="ExternalInput").ap()
    out = nc.dram_tensor("out_0", (1, T, D), F32, kind="ExternalOutput").ap()
    program(nc, I, out, at)
    r = _run(nc, [arrays], core_ids=[0])
    return r.results[0]["out_0"]
```

```python
from contextlib import ExitStack

import numpy as np

import concourse.bass as bass
from concourse import mybir

F32 = mybir.dt.float32
ALU = mybir.AluOpType
ACTF = mybir.ActivationFunctionType
AX = mybir.AxisListType.X

T = 256
D = 1024
NFF = 22
NE = 32
EPS = 1e-6
WIN = (2, 4, 8, 16)
NSLOT = 5
CAP = 32
BIG = 1e30


def constants():
    p = np.arange(128)
    at, parts, n = {}, [], 0

    def put(name, a):
        nonlocal n
        a = np.asarray(a, np.float32).reshape(128, -1)
        at[name] = (n, a.shape[1])
        parts.append(a)
        n += a.shape[1]

    put("ident", np.eye(128))
    put("ones", np.ones((128, 128)))
    put("mean", np.full((128, 128), 1.0 / D))
    put("upto", p[:, None] >= p[None, :])
    put("before", p[:, None] < p[None, :])
    put("sgum", (p[:, None] // 64) <= (p[None, :] // 64))
    dist = np.concatenate([p[:, None] - p[None, :], p[:, None] + 128 - np.arange(256)[None, :]], 1)
    count = ((dist >= 0) & (dist <= 128)) * 1.0 + ((dist >= 0) & (dist % 4 == 0)) + ((dist >= 0) & (dist % 16 == 0))
    put("dist", np.where(count > 0, dist, 1e30))
    put("count", count)
    sb = np.concatenate([np.where(p[:, None] < p[None, :], 0.0, -BIG), np.zeros((128, 128)),
                         np.where(p[:, None] < p[None, :], 0.0, -BIG)], 1)
    put("sbneg", sb)
    put("invc", np.tile(np.stack([1.0 / np.minimum(np.arange(1, 17), w) for w in WIN]).reshape(1, -1), (128, 1)))
    put("eps", np.full((128, 1), EPS))
    put("one", np.ones((128, 1)))
    put("zero", np.zeros((128, 1)))
    put("iota", np.tile(np.arange(32)[None], (128, 1)))
    return np.concatenate(parts, 1), at


class Tok:

    def __init__(self, sem, val):
        self.sem, self.val = sem, val


class Queue:

    def __init__(self, sem, chained):
        self.sem, self.chained, self.n, self.items, self.last = sem, chained, 0, [], None

    def op(self, fn, *waits):
        waits = [w for w in waits if w is not None]
        if self.chained and self.last:
            waits.append(self.last)
        self.n += 1
        self.last = Tok(self.sem, self.n)
        self.items.append((fn, waits, (self.sem, 1)))
        return self.last

    def quiet(self, fn, *waits):
        self.items.append((fn, [w for w in waits if w is not None], None))

    def dma(self, dst, src, sem, *waits):
        self.items.append((lambda e: e.dma_start(dst, src), [w for w in waits if w is not None], (sem, 16)))

    def wait(self, *waits):
        self.items.append((None, [w for w in waits if w is not None], None))

    def emit(self, eng):
        seen = {}
        for fn, waits, inc in self.items:
            need = {}
            for w in waits:
                need[id(w.sem)] = max(need.get(id(w.sem), (0, None))[0], w.val), w.sem
            for key, (val, sem) in need.items():
                if seen.get(key, 0) < val:
                    eng.wait_ge(sem, val)
                    seen[key] = val
            if fn is None:
                continue
            ins = fn(eng)
            if inc:
                ins.then_inc(*inc)


def program(nc, I, out, const_at):
    with ExitStack() as ctx:
        def sb(name, shape, dt=F32):
            return ctx.enter_context(nc.sbuf_tensor(name, shape, dt))

        def sem(name):
            return ctx.enter_context(nc.semaphore(name))

        PE, ACT, DVE, POOL, SP = (Queue(sem("s_" + n), n in ("act", "dve", "pool"))
                                  for n in ("pe", "act", "dve", "pool", "sp"))
        sems = {}

        def dsem(name):
            if name not in sems:
                sems[name] = [sem("d_" + name), 0]
            sems[name][1] += 16
            return sems[name][0]

        def dtok(name):
            return Tok(*sems[name])

        ps = [ctx.enter_context(nc.psum_tensor(f"ps{i}", [128, 512], F32)) for i in range(8)]
        ps_free = [[] for _ in range(8)]
        ps_next = [0]
        ps_held = set()

        def bank():
            i = ps_next[0]
            while i in ps_held:
                i = (i + 1) % 8
            ps_next[0] = (i + 1) % 8
            return i

        ring = [sb(f"ring{i}", [128, 4096]) for i in range(NSLOT)]
        ring_sem = [sem(f"d_ring{i}") for i in range(NSLOT)]
        ring_n = [0] * NSLOT
        ring_free = [None] * NSLOT
        ring_at = [0]

        def stream(*pieces):
            i = ring_at[0] % NSLOT
            ring_at[0] += 1
            for view, src in pieces:
                SP.dma(view(ring[i]), src, ring_sem[i], ring_free[i])
                ring_n[i] += 16
            return i, Tok(ring_sem[i], ring_n[i])

        def cols(w, a, n):
            return w[:, a:a + n].rearrange("(k p) n -> p k n", p=128)

        def k8(t):
            return t[:, :].rearrange("p (k n) -> p k n", k=8)

        cst_w = const_at["iota"][0] + const_at["iota"][1]
        CST = sb("cst", [128, cst_w])

        def c_(name):
            o, n = const_at[name]
            return CST[:, o:o + n]

        ident, ones, mean = c_("ident"), c_("ones"), c_("mean")
        X = sb("X", [128, 2, D])
        HT = sb("HT", [128, 8, T])
        COL = sb("COL", [128, 328])
        SM = sb("SM", [128, 512])
        sm_at = [0]

        def small(n):
            a = sm_at[0]
            sm_at[0] += n
            assert sm_at[0] <= 512
            return SM[:, a:a + n]

        AR = 24064
        arena = sb("arena", [128, AR])

        def ar(off, n, k=None):
            assert off + n <= AR, (off, n)
            v = arena[:, off:off + n]
            return v if k is None else v.rearrange("p (k n) -> p k n", k=k)

        SP.dma(X[:, :, :], I["x"][0].rearrange("(t p) d -> p t d", p=128), dsem("x"))
        ACT.dma(CST[:, :], I["cst"], dsem("cst"))
        rows = ar(0, 384)
        row_at = {}
        r = 0
        for name, n in (("g_mix_pre", 8), ("b_dw", 8), ("g_conv_ln", 8), ("b_conv_ln", 8), ("s_pool", 8),
                        ("g_ffn_pre", 8), ("c_2", 8), ("g_mix_2", 8), ("g_dil_out_2", 4), ("g_sb_out_2", 4)):
            row_at[name] = r
            ACT.dma(rows[r:r + n, 0:128], I[name][0].rearrange("(a b) -> a b", b=128), dsem("rows"))
            r += n
        NR = r
        wdw = I["w_dw"][0].rearrange("k o (c p) -> (k o c) p", p=128)
        for j in range(2):
            ACT.dma(rows[0:124, 128 + 128 * j:256 + 128 * j], wdw[124 * j:124 * j + 124, :], dsem("rows"))

        def col(name, k):
            a = row_at[name] + k
            return COL[:, a:a + 1]

        def tap(k, c):
            a = NR + k * 8 + c
            return COL[:, a:a + 1]

        bank()
        cst, rws = dtok("cst"), dtok("rows")
        PE.quiet(lambda e: e.transpose(ps[0][:, 0:NR], rows[0:NR, 0:128], ident[0:NR, 0:NR]), cst, rws)
        PE.quiet(lambda e: e.transpose(ps[0][:, NR:NR + 124], rows[0:124, 128:256], ident[0:124, 0:124]))
        t = PE.op(lambda e: e.transpose(ps[0][:, NR + 124:NR + 248], rows[0:124, 256:384], ident[0:124, 0:124]))
        t_col = DVE.op(lambda e: e.tensor_copy(COL[:, 0:NR + 248], ps[0][:, 0:NR + 248]), t)
        ps_free[0] = [t_col]

        def rstd(ss, scale=1.0 / D, *waits):
            t = ACT.op(lambda e: e.activation(ss, ss, ACTF.Sqrt, bias=c_("eps"), scale=scale), cst, *waits)
            return DVE.op(lambda e: e.reciprocal(ss, ss), t)

        def sumsq(srcs, junk, acc, *waits):
            for n, s in enumerate(srcs):
                t = ACT.op(lambda e, s=s, n=n: e.activation(junk, s, ACTF.Square, accum_out=acc[:, n:n + 1]), *waits)
            return t

        def to_T(src, dst, nk, evac, *waits):
            tok = None
            for k0 in range(0, nk, 2):
                b = bank()
                for k in range(k0, k0 + 2):
                    for tt in range(2):
                        o = (k - k0) * 256 + tt * 128
                        f = (lambda e, b=b, o=o, s=src(tt, k): e.transpose(ps[b][:, o:o + 128], s, ident))
                        if k == k0 + 1 and tt == 1:
                            t = PE.op(f, *waits, *ps_free[b])
                        else:
                            PE.quiet(f, *waits, *ps_free[b])
                if evac is None:
                    q = DVE if (k0 // 2) % 2 else ACT
                    v = ps[b][:, :].rearrange("p (k n) -> p k n", k=2)
                    if q is DVE:
                        tok = [DVE.op(lambda e, k0=k0, v=v: e.tensor_copy(dst[:, k0:k0 + 2, :], v), t)]
                    else:
                        tok = [ACT.op(lambda e, k0=k0, v=v: e.activation(dst[:, k0:k0 + 2, :], v, ACTF.Copy), t)]
                    ps_free[b] = tok
                else:
                    done = []
                    for k in range(k0, k0 + 2):
                        s, bi = evac(k)
                        v = ps[b][:, (k - k0) * 256:(k - k0) * 256 + 256]
                        if bi is None:
                            done.append(DVE.op(lambda e, k=k, v=v, s=s: e.tensor_scalar(
                                dst[:, k, :], v, s, None, ALU.mult), t))
                        else:
                            done.append(DVE.op(lambda e, k=k, v=v, s=s, bi=bi: e.tensor_scalar(
                                dst[:, k, :], v, s, bi, ALU.mult, ALU.add), t))
                    ps_free[b] = done
            return [DVE.last, ACT.last]

        def fm(W, nt, xT, nk, b, o, waits, first_free, inc):
            for k in range(nk):
                f = (lambda e, k=k: e.matmul(ps[b][:, o:o + 256], W[:, k, nt * 128:nt * 128 + 128], xT[:, k, :],
                                             start=(k == 0), stop=(k == nk - 1)))
                w = (*waits, *(first_free if k == 0 else ()))
                if inc and k == nk - 1:
                    return PE.op(f, *w)
                PE.quiet(f, *w)

        def fm_slot(W, xT, waits, on_bank, pairs=((0, 1), (2, 3)), nk=8):
            for n, pair in enumerate(pairs):
                b = bank()
                fm(W, pair[0], xT, nk, b, 0, waits, ps_free[b], False)
                t = fm(W, pair[1], xT, nk, b, 256, waits, (), True)
                ps_free[b] = on_bank(n, b, t)
            return t

        def tmaj(xT, W, nk, tt, b, waits, start=True, stop=True, o=0, n=512):
            for k in range(nk):
                f = (lambda e, k=k, x=xT(k)[:, tt * 128:tt * 128 + 128], w=W(k): e.matmul(
                    ps[b][:, o:o + n], x, w, start=(start and k == 0), stop=(stop and k == nk - 1)))
                w = (*waits, *(ps_free[b] if start and k == 0 else ()))
                if k == nk - 1:
                    return PE.op(f, *w)
                PE.quiet(f, *w)

        def post_norm(banks, toks, grow, gtok, tmp):
            ss4, ss = small(4), small(2)
            for j in range(4):
                t = ACT.op(lambda e, j=j: e.activation(tmp[:, 0:512], ps[banks[j]][:, :], ACTF.Square,
                                                       accum_out=ss4[:, j:j + 1]), toks[j], DVE.last)
            v = ss4.rearrange("p (t n) -> p t n", n=2)
            t = DVE.op(lambda e: e.tensor_tensor(ss, v[:, :, 0], v[:, :, 1], ALU.add), t)
            t = rstd(ss, 1.0 / D, t)
            for j in range(4):
                tt, nn = j // 2, j % 2
                a = DVE.op(lambda e, j=j, tt=tt, nn=nn: e.scalar_tensor_tensor(
                    out=tmp[:, 512:1024], in0=ps[banks[j]][:, :], scalar=ss[:, tt:tt + 1],
                    in1=grow[:, nn * 512:nn * 512 + 512], op0=ALU.mult, op1=ALU.mult), gtok)
                ps_free[banks[j]] = [a]
                t = DVE.op(lambda e, tt=tt, nn=nn: e.tensor_tensor(
                    X[:, tt, nn * 512:nn * 512 + 512], X[:, tt, nn * 512:nn * 512 + 512],
                    tmp[:, 512:1024], ALU.add))
            return t

        def norm_scaled(dst, tmp, *waits):
            ss = small(2)
            t = sumsq([X[:, 0, :], X[:, 1, :]], tmp, ss, *waits)
            t = rstd(ss, 1.0 / D, t)
            for tt in range(2):
                t = DVE.op(lambda e, tt=tt: e.tensor_scalar(dst[:, tt, :], X[:, tt, :], ss[:, tt:tt + 1], None,
                                                            ALU.mult), *waits)
            return t

        G = ar(0, 6144, 24)
        CV = ar(6144, 8 * 286, 8)
        CVO = ar(8432, 2048, 8)
        U = ar(10480, 2048, 8)
        V = ar(12528, 2048, 2)
        ZP = ar(14576, 8 * 272, 8)
        ZB = ar(16752, 8 * 272, 8)
        ZC = ar(18928, 8 * 272, 8)
        TMP = ar(21104, 1024)
        TMP2 = ar(22128, 1024)
        XS = V

        t = norm_scaled(XS, TMP, dtok("x"), t_col)
        hts = to_T(lambda tt, k: XS[:, tt, k * 128:k * 128 + 128], HT, 8, lambda k: (col("g_mix_pre", k), None), t)

        mz = POOL.op(lambda e: e.memset(CV[:, :, 0:30], 0.0))
        mz2 = POOL.op(lambda e: e.memset(ZP[:, :, 0:16], 0.0))
        w_in = I["w_in"][0]

        for j in range(4):
            i, tw = stream((lambda r: k8(r)[:, :, 0:256], cols(w_in, 2048 + 256 * j, 256)),
                           (lambda r: k8(r)[:, :, 256:512], cols(w_in, 3072 + 256 * j, 256)))

            def glu(n, b, t, j=j):
                c = 2 * j + n
                h = n * 512
                s = ACT.op(lambda e: e.activation(TMP[:, h:h + 256], ps[b][:, 256:512], ACTF.Sigmoid), t,
                           glu_free[n])
                m = DVE.op(lambda e: e.tensor_tensor(CV[:, c, 30:286], ps[b][:, 0:256], TMP[:, h:h + 256],
                                                     ALU.mult), s, mz)
                glu_free[n] = m
                DVE.op(lambda e: e.tensor_scalar(CVO[:, c, :], CV[:, c, 0:256], tap(0, c), col("b_dw", c),
                                                 ALU.mult, ALU.add))
                for k in range(1, 31):
                    DVE.op(lambda e, k=k: e.scalar_tensor_tensor(
                        out=CVO[:, c, :], in0=CV[:, c, k:k + 256], scalar=tap(k, c), in1=CVO[:, c, :],
                        op0=ALU.mult, op1=ALU.add))
                return [m, s]

            if j == 0:
                glu_free = [None, None]
            ring_free[i] = fm_slot(k8(ring[i]), HT, [tw, *hts], glu, pairs=((0, 2), (1, 3)))
        t_cv = DVE.last

        vt = []
        for nn in range(2):
            i, tw = stream((k8, cols(w_in, 1024 + 512 * nn, 512)))
            for tt in range(2):
                b = bank()
                t = tmaj(lambda k: HT[:, k, :], lambda k, i=i: k8(ring[i])[:, k, :], 8, tt, b, [tw])
                a = ACT.op(lambda e, tt=tt, nn=nn, b=b: e.activation(
                    V[:, tt, nn * 512:nn * 512 + 512], ps[b][:, :], ACTF.Gelu_apprx_tanh), t)
                ps_free[b] = [a]
            ring_free[i] = t
        t_v = ACT.last
        for nn in range(2):
            i, tw = stream((k8, cols(w_in, 512 * nn, 512)))

            def gelu(n, b, t, nn=nn):
                return [ACT.op(lambda e: e.activation(
                    U[:, nn * 4 + 2 * n:nn * 4 + 2 * n + 2, :], ps[b][:, :].rearrange("p (k n) -> p k n", k=2),
                    ACTF.Gelu_apprx_tanh), t)]

            ring_free[i] = fm_slot(k8(ring[i]), HT, [tw], gelu)
        t_u = ACT.last
        GV, BV = ZB[:, :, :].rearrange("p k n -> p (k n)")[:, 0:1024], ZB[:, :, :].rearrange("p k n -> p (k n)")[:, 1024:2048]
        WS = ZC[:, :, :].rearrange("p k n -> p (k n)")[:, 0:1024]
        WST = ZC[:, :, :].rearrange("p k n -> p (k n)")[:, 1024:2048]
        SP.dma(GV, I["g_sgu_v"][0].partition_broadcast(128), dsem("gv"))
        SP.dma(BV, I["b_sgu_v"][0].partition_broadcast(128), dsem("gv"))
        SP.dma(WS.rearrange("p (h j) -> p h j", h=8), I["w_sgu_s"][0].rearrange("h i j -> i h j"), dsem("ws"))
        BSR = sb("bsr", [1, 1024])
        SP.dma(BSR[:, :], I["b_sgu_s"].rearrange("a h i -> a (h i)"), dsem("ws"))
        st, mv = small(24), small(4)
        for tt in range(2):
            for nn in range(2):
                DVE.op(lambda e, tt=tt, nn=nn: e.bn_stats(st[:, (tt * 2 + nn) * 6:(tt * 2 + nn) * 6 + 6],
                                                          V[:, tt, nn * 512:nn * 512 + 512]), t_v)
            t = DVE.op(lambda e, tt=tt: e.bn_aggr(mv[:, 2 * tt:2 * tt + 2], st[:, tt * 12:tt * 12 + 12]))
        for tt in range(2):
            a = ACT.op(lambda e, tt=tt: e.activation(mv[:, 2 * tt + 1:2 * tt + 2], mv[:, 2 * tt + 1:2 * tt + 2],
                                                     ACTF.Sqrt, bias=c_("eps")), t)
        for tt in range(2):
            DVE.op(lambda e, tt=tt: e.reciprocal(mv[:, 2 * tt + 1:2 * tt + 2], mv[:, 2 * tt + 1:2 * tt + 2]), a)
            DVE.op(lambda e, tt=tt: e.tensor_scalar(V[:, tt, :], V[:, tt, :], mv[:, 2 * tt:2 * tt + 1],
                                                    mv[:, 2 * tt + 1:2 * tt + 2], ALU.subtract, ALU.mult))
            DVE.op(lambda e, tt=tt: e.tensor_tensor(V[:, tt, :], V[:, tt, :], GV, ALU.mult), dtok("gv"))
            t_vn = DVE.op(lambda e, tt=tt: e.tensor_tensor(V[:, tt, :], V[:, tt, :], BV, ALU.add))

        gate_toks = []
        for s_ in range(6):
            i, tw = stream((k8, cols(w_in, 5120 + 512 * s_, 512)))

            def sig(n, b, t, s_=s_):
                return [ACT.op(lambda e: e.activation(
                    G[:, s_ * 4 + 2 * n:s_ * 4 + 2 * n + 2, :], ps[b][:, :].rearrange("p (k n) -> p k n", k=2),
                    ACTF.Sigmoid), t, t_col)]

            ring_free[i] = fm_slot(k8(ring[i]), HT, [tw], sig)
        t_g = ACT.last

        for h0 in (0, 4):
            b = bank()
            for h in range(h0, h0 + 4):
                f = (lambda e, h=h, b=b, h0=h0: e.transpose(ps[b][:, (h - h0) * 128:(h - h0) * 128 + 128],
                                                            WS[:, h * 128:h * 128 + 128], ident))
                t = PE.op(f, dtok("ws"), *ps_free[b])
            a = DVE.op(lambda e, b=b, h0=h0: e.tensor_tensor(
                WST[:, h0 * 128:h0 * 128 + 512].rearrange("p (h i) -> p h i", h=4),
                ps[b][:, :].rearrange("p (h i) -> p h i", h=4),
                c_("sgum").unsqueeze(1).broadcast_to((128, 4, 128)), ALU.mult), t)
            ps_free[b] = [a]
        t_ws = a
        for h0 in range(0, 8, 2):
            b = bank()
            for h in (h0, h0 + 1):
                for tt in range(2):
                    o = (h - h0) * 256 + tt * 128
                    PE.quiet(lambda e, b=b, o=o, h=h: e.matmul(ps[b][:, o:o + 128], ones[0:1, :],
                                                               BSR[0:1, h * 128:h * 128 + 128],
                                                               start=True, stop=False), t_ws, t_vn, *ps_free[b])
                    t = PE.op(lambda e, b=b, o=o, h=h, tt=tt: e.matmul(
                        ps[b][:, o:o + 128], V[:, tt, h * 128:h * 128 + 128], WST[:, h * 128:h * 128 + 128],
                        start=False, stop=True))
            a = DVE.op(lambda e, b=b, h0=h0: e.tensor_tensor(
                U[:, h0:h0 + 2, :], U[:, h0:h0 + 2, :], ps[b][:, :].rearrange("p (k n) -> p k n", k=2),
                ALU.mult), t, t_u)
            ps_free[b] = [a]
        t_um = a
        t_mix = t

        def branch(src, w, br, *waits):
            for nn in range(2):
                i, tw = stream((k8, cols(w, 512 * nn, 512)))

                def ev(n, b, t, nn=nn):
                    k = nn * 4 + 2 * n
                    pv = ps[b][:, :].rearrange("p (k n) -> p k n", k=2)
                    if br == 0:
                        return [DVE.op(lambda e: e.tensor_tensor(G[:, k:k + 2, :], G[:, k:k + 2, :], pv, ALU.mult),
                                       t, t_g)]
                    q = G[:, br * 8 + k:br * 8 + k + 2, :]
                    a = DVE.op(lambda e: e.tensor_tensor(q, q, pv, ALU.mult), t, t_g)
                    DVE.op(lambda e: e.tensor_tensor(G[:, k:k + 2, :], G[:, k:k + 2, :], q, ALU.add))
                    return [a]

                ring_free[i] = fm_slot(k8(ring[i]), src, [tw, *waits], ev)

        branch(U, I["w_sgu_out"][0], 0, t_um)

        for nn in range(2):
            i, tw = stream((k8, cols(w_in, 4096 + 512 * nn, 512)))

            def zcp(n, b, t, nn=nn):
                k = nn * 4 + 2 * n
                return [ACT.op(lambda e: e.activation(ZP[:, k:k + 2, 16:272],
                                                      ps[b][:, :].rearrange("p (k n) -> p k n", k=2), ACTF.Copy),
                               t, mz2)]

            ring_free[i] = fm_slot(k8(ring[i]), HT, [tw], zcp)
        t_z = ACT.last
        POOL.op(lambda e: e.tensor_tensor(ZB[:, :, 1:272], ZP[:, :, 1:272], ZP[:, :, 0:271], ALU.add), t_z, t_um,
                t_mix)
        POOL.op(lambda e: e.tensor_tensor(ZC[:, 2:8, 3:272], ZB[:, 2:8, 3:272], ZB[:, 2:8, 1:270], ALU.add))
        POOL.op(lambda e: e.tensor_tensor(ZB[:, 4:8, 7:272], ZC[:, 4:8, 7:272], ZC[:, 4:8, 3:268], ALU.add))
        t_p = POOL.op(lambda e: e.tensor_tensor(ZC[:, 6:8, 15:272], ZB[:, 6:8, 15:272], ZB[:, 6:8, 7:264], ALU.add))
        o = const_at["invc"][0]
        for g, (S_, w) in enumerate(zip((ZB, ZC, ZB, ZC), WIN)):
            k = 2 * g
            inv = CST[:, o + 16 * g:o + 16 * g + 16].unsqueeze(1).broadcast_to((128, 2, 16))
            DVE.op(lambda e, S_=S_, k=k, inv=inv: e.tensor_tensor(S_[:, k:k + 2, 16:32], S_[:, k:k + 2, 16:32], inv,
                                                                  ALU.mult), t_p)
            DVE.op(lambda e, S_=S_, k=k: e.tensor_tensor(ZP[:, k:k + 2, 16:32], S_[:, k:k + 2, 16:32],
                                                         ZP[:, k:k + 2, 16:32], ALU.subtract))
            t_pl = DVE.op(lambda e, S_=S_, k=k, w=w: e.scalar_tensor_tensor(
                out=ZP[:, k:k + 2, 32:272], in0=S_[:, k:k + 2, 32:272], scalar=1.0 / w, in1=ZP[:, k:k + 2, 32:272],
                op0=ALU.mult, op1=ALU.subtract))

        b = bank()
        for c in range(8):
            t = PE.op(lambda e, c=c, b=b: e.matmul(ps[b][:, 0:256], mean, CVO[:, c, :], start=(c == 0),
                                                   stop=(c == 7)), t_cv, *ps_free[b])
        t = DVE.op(lambda e, b=b: e.tensor_tensor(CVO, CVO, ps[b][:, 0:256].unsqueeze(1).broadcast_to((128, 8, 256)),
                                                  ALU.subtract), t)
        ps_free[b] = [t]
        SQ = ZB[:, :, 0:256]
        t = ACT.op(lambda e: e.activation(SQ, CVO, ACTF.Square), t, t_pl)
        b = bank()
        for c in range(8):
            t2 = PE.op(lambda e, c=c, b=b: e.matmul(ps[b][:, 0:256], mean, SQ[:, c, :], start=(c == 0),
                                                    stop=(c == 7)), t, *ps_free[b])
        RS = TMP[:, 0:256]
        t = ACT.op(lambda e, b=b: e.activation(RS, ps[b][:, 0:256], ACTF.Sqrt, bias=c_("eps")), t2, t_cv)
        ps_free[b] = [t]
        t = DVE.op(lambda e: e.reciprocal(RS, RS), t)
        t = DVE.op(lambda e: e.tensor_tensor(CVO, CVO, RS.unsqueeze(1).broadcast_to((128, 8, 256)), ALU.mult))
        for c in range(8):
            t_cs = ACT.op(lambda e, c=c: e.activation(CVO[:, c, :], CVO[:, c, :], ACTF.Silu,
                                                      bias=col("b_conv_ln", c), scale=col("g_conv_ln", c)), t)

        i, tw = stream((lambda r: r[:, 0:2048].rearrange("p (g k n) -> p g k n", g=4, k=2),
                        I["w_pool"][0].rearrange("g (k p) n -> p g k n", p=128)))
        WP = ring[i][:, 0:2048].rearrange("p (g k n) -> p g k n", g=4, k=2)
        PM = ZC[:, :, 0:256]
        for g in range(4):
            b = bank()
            for d in range(2):
                for k in range(2):
                    t = PE.op(lambda e, b=b, d=d, k=k, g=g: e.matmul(
                        ps[b][:, d * 256:d * 256 + 256], WP[:, g, k, d * 128:d * 128 + 128],
                        ZP[:, 2 * g + k, 16:272], start=(k == 0), stop=(k == 1)), tw, t_pl, *ps_free[b])
            for d in range(2):
                a = ACT.op(lambda e, b=b, d=d, g=g: e.activation(PM[:, 2 * g + d, :], ps[b][:, d * 256:d * 256 + 256],
                                                                 ACTF.Copy, scale=col("s_pool", 2 * g + d)), t)
            ps_free[b] = [a]
        ring_free[i] = t
        branch(PM, I["w_pool_out"][0], 2, a)
        branch(CVO, I["w_conv_out"][0], 1, t_cs)
        t_m = DVE.last

        GR = U[:, :, :].rearrange("p k n -> p (k n)")[:, 0:1024]
        SP.dma(GR, I["g_mix_post"][0].partition_broadcast(128), dsem("gmp"), t_um, PE.last)
        banks, toks = [None] * 4, [None] * 4
        for nn in range(2):
            i, tw = stream((k8, cols(I["w_out"][0], 512 * nn, 512)))
            for tt in range(2):
                b = bank()
                toks[tt * 2 + nn] = tmaj(lambda k: G[:, k, :], lambda k, i=i: k8(ring[i])[:, k, :], 8, tt, b,
                                         [tw, t_m])
                banks[tt * 2 + nn] = b
            ring_free[i] = PE.last
        t_x1 = post_norm(banks, toks, GR, dtok("gmp"), TMP)

        XS = V
        t = norm_scaled(XS, TMP, t_x1, PE.last)
        hts = to_T(lambda tt, k: XS[:, tt, k * 128:k * 128 + 128], HT, 8, lambda k: (col("g_ffn_pre", k), None), t)
        FF = ar(0, NFF * 256, NFF)
        ADA = ar(5632, 6144)
        GR2 = ar(14576, 1024)
        SP.dma(GR2, I["g_ffn_post"][0].partition_broadcast(128), dsem("gfp"), PE.last, DVE.last)
        cond = small(8)
        t_c = ACT.op(lambda e: e.activation(cond, COL[:, row_at["c_2"]:row_at["c_2"] + 8], ACTF.Silu))
        t_az = POOL.op(lambda e: e.memset(ADA, 0.0), t_x1, PE.last)
        SP.dma(ADA[0:1, :], I["b_ada_2"], dsem("ada"), t_az)
        w_ff, w_ada = I["w_ffn_in"][0], I["w_ada_2"][0]

        def ada(m):
            i, tw = stream((k8, cols(w_ada, 512 * m, 512)))
            for k in range(8):
                a = DVE.op(lambda e, i=i, k=k, m=m: e.scalar_tensor_tensor(
                    out=ADA[:, 512 * m:512 * m + 512], in0=k8(ring[i])[:, k, :], scalar=cond[:, k:k + 1],
                    in1=ADA[:, 512 * m:512 * m + 512], op0=ALU.mult, op1=ALU.add), tw, t_c, dtok("ada"))
            ring_free[i] = a
            return a

        sil = [None, None]
        t_pe = PE.last
        for j in range(11):
            i, tw = stream((lambda r: k8(r)[:, :, 0:256], cols(w_ff, 256 * j, 256)),
                           (lambda r: k8(r)[:, :, 256:512], cols(w_ff, 2816 + 256 * j, 256)))

            def ffg(n, b, t, j=j):
                h = n * 512
                s = ACT.op(lambda e: e.activation(TMP[:, h:h + 256], ps[b][:, 0:256], ACTF.Silu), t, sil[n], t_x1)
                m = DVE.op(lambda e: e.tensor_tensor(FF[:, 2 * j + n, :], ps[b][:, 256:512], TMP[:, h:h + 256],
                                                     ALU.mult), s, t_pe)
                sil[n] = m
                return [m, s]

            ring_free[i] = fm_slot(k8(ring[i]), HT, [tw, *hts], ffg, pairs=((0, 2), (1, 3)))
            ada(j)
        t_ada = ada(11)
        t_ff = sil[1]
        banks = [bank() for _ in range(4)]
        w_fo = I["w_ffn_out"][0]
        for s_ in range(6):
            n = 4 if s_ < 5 else 2
            i, tw = stream((lambda r, n=n: r[:, 0:1024 * n].rearrange("p (k n) -> p k n", k=n),
                            w_fo[512 * s_:512 * s_ + 128 * n, :].rearrange("(k p) n -> p k n", p=128)))
            W = ring[i][:, :].rearrange("p (k n) -> p k n", k=4)
            for j in range(4):
                tt, nn = j // 2, j % 2
                toks[j] = tmaj(lambda k, s_=s_: FF[:, 4 * s_ + k, :], lambda k, W=W, nn=nn: W[:, k, nn * 512:nn * 512 + 512],
                               n, tt, banks[j], [tw, t_ff], start=(s_ == 0), stop=(s_ == 5))
            ring_free[i] = PE.last
        t_x2 = post_norm(banks, toks, GR2, dtok("gfp"), TMP)

        PT_ = ar(12000, 512, 2)
        PR = ar(12512, 512, 2)
        SP.dma(PR, I["p"][0, 0].rearrange("(t p) d -> p t d", p=128), dsem("p"), t_ff)
        h2 = to_T(lambda tt, k: X[:, tt, k * 128:k * 128 + 128], HT, 8, None, t_x2)
        pts = to_T(lambda tt, k: PR[:, tt, k * 128:k * 128 + 128], PT_, 2, None, dtok("p"))
        i0, tw0 = stream((lambda r: r[:, 0:2048].rearrange("p (k n) -> p k n", k=2),
                          I["w_ple"][0].rearrange("(k p) n -> p k n", p=128)))
        WPL = ring[i0][:, 0:2048].rearrange("p (k n) -> p k n", k=2)
        for nn in range(2):
            i, tw = stream((k8, cols(I["w_ple_gate"][0], 512 * nn, 512)))
            for tt in range(2):
                b = bank()
                t = tmaj(lambda k: HT[:, k, :], lambda k, i=i: k8(ring[i])[:, k, :], 8, tt, b, [tw, *h2])
                b2 = bank()
                t2 = tmaj(lambda k: PT_[:, k, :], lambda k, nn=nn: WPL[:, k, nn * 512:nn * 512 + 512], 2, tt, b2,
                          [tw0, *pts])
                a = ACT.op(lambda e, b=b: e.activation(TMP[:, 0:512], ps[b][:, :], ACTF.Sigmoid), t, DVE.last)
                ps_free[b] = [a]
                a = DVE.op(lambda e, b2=b2: e.tensor_tensor(TMP[:, 512:1024], TMP[:, 0:512], ps[b2][:, :], ALU.mult),
                           a, t2)
                ps_free[b2] = [a]
                t_x3 = DVE.op(lambda e, tt=tt, nn=nn: e.tensor_tensor(
                    X[:, tt, nn * 512:nn * 512 + 512], X[:, tt, nn * 512:nn * 512 + 512], TMP[:, 512:1024], ALU.add))
            ring_free[i] = PE.last
        ring_free[i0] = PE.last

        MC = small(16)
        b = bank()
        for j in range(16):
            t = PE.op(lambda e, j=j, b=b: e.matmul(ps[b][:, j:j + 1], ADA[:, 128 * j:128 * j + 128], ones[:, 0:1],
                                                   start=True, stop=True), t_ada, *ps_free[b])
        t = DVE.op(lambda e, b=b: e.tensor_copy(MC, ps[b][:, 0:16]), t)
        ps_free[b] = [t]
        t_mc = DVE.op(lambda e: e.scalar_tensor_tensor(out=MC[:, 8:16], in0=MC[:, 8:16], scalar=1.0,
                                                       in1=COL[:, row_at["g_mix_2"]:row_at["g_mix_2"] + 8],
                                                       op0=ALU.add, op1=ALU.mult))
        MR = ADA[:, 2048:6144].rearrange("p (k n) -> p k n", k=4)
        for j in range(8):
            b = bank()
            v = ADA[:, 2048 + 512 * j:2560 + 512 * j]
            t = PE.op(lambda e, b=b, v=v: e.matmul(ps[b][:, :], ones, v, start=True, stop=True), *ps_free[b], t_ada)
            a = ACT.op(lambda e, b=b, v=v: e.activation(v, ps[b][:, :], ACTF.Copy), t)
            ps_free[b] = [a]
        t_mr = a

        XS = ar(14576, 2048, 2)
        t = norm_scaled(XS, TMP, t_x3, PE.last)
        hts = to_T(lambda tt, k: XS[:, tt, k * 128:k * 128 + 128], HT, 8,
                   lambda k: (MC[:, 8 + k:9 + k], MC[:, k:k + 1]), t, t_mc)
        w2 = I["w_in_2"][0]
        QK = [ar(1024 * n, 1024, 4) for n in range(4)]
        VV = [ar(4096, 1024, 2), ar(11776, 1024, 2)]
        t_qk = {}
        for n, (kind, a0) in enumerate((("qs", 1536), ("ks", 2048), ("vs", 2560), ("qd", 0), ("kd", 512), ("vd", 1024))):
            i, tw = stream((k8, cols(w2, a0, 512)))
            if kind[0] == "v":
                dst = VV[0] if kind == "vd" else VV[1]
                for tt in range(2):
                    b = bank()
                    t = tmaj(lambda k: HT[:, k, :], lambda k, i=i: k8(ring[i])[:, k, :], 8, tt, b, [tw, *hts])
                    ps_free[b] = [ACT.op(lambda e, tt=tt, b=b, dst=dst: e.activation(dst[:, tt, :], ps[b][:, :],
                                                                                    ACTF.Copy), t, t_x3)]
                ring_free[i] = PE.last
            else:
                dst = QK[("qd", "kd", "qs", "ks").index(kind)]

                def cp(n, b, t, dst=dst):
                    return [ACT.op(lambda e: e.activation(dst[:, 2 * n:2 * n + 2, :],
                                                          ps[b][:, :].rearrange("p (k n) -> p k n", k=2), ACTF.Copy),
                                   t, t_x3)]

                ring_free[i] = fm_slot(k8(ring[i]), HT, [tw, *hts], cp)
            t_qk[kind] = ACT.last

        def head(n, h):
            return QK[n][64 * (h % 2):64 * (h % 2) + 64, h // 2, :]

        OD, OS = ar(14576, 1024, 2), ar(15600, 1024, 2)
        LA = ar(16624, 4 * 384, 4)
        LB = ar(18160, 4 * 384, 4)
        LC = ar(19696, 4 * 384, 4)
        t_hts = PE.last
        before, upto = c_("before"), c_("upto")
        for hg in (0, 4):
            zb = []
            for h in range(hg, hg + 4):
                b = bank()
                zb.append(b)
                PE.quiet(lambda e, b=b, h=h: e.matmul(ps[b][:, 0:256], head(3, h)[:, 0:128], head(2, h),
                                                      start=True, stop=True), t_qk["qs"], t_qk["ks"], *ps_free[b])
                t = PE.op(lambda e, b=b, h=h: e.matmul(ps[b][:, 256:384], head(3, h)[:, 128:256],
                                                       head(2, h)[:, 128:256], start=True, stop=True))
                ACT.op(lambda e, b=b, h=h: e.activation(LA[:, h % 4, :], ps[b][:, 0:384], ACTF.Copy, scale=0.125),
                       t, t_hts, t_x3, DVE.last)
                a = ACT.op(lambda e, b=b, h=h: e.activation(LB[:, h % 4, :], ps[b][:, 0:384], ACTF.Abs, scale=0.125))
                ps_free[b] = [a]
            ACT.op(lambda e: e.activation(LB, LB, ACTF.Exp, scale=-1.0))
            a = ACT.op(lambda e: e.activation(LB, LB, ACTF.Ln, bias=c_("one")))
            DVE.op(lambda e: e.scalar_tensor_tensor(out=LB, in0=LA, scalar=0.0, in1=LB, op0=ALU.max, op1=ALU.add), a)
            for o in (0, 256):
                t = DVE.op(lambda e, o=o: e.tensor_tensor(
                    LB[:, :, o:o + 128], LB[:, :, o:o + 128], before.unsqueeze(1).broadcast_to((128, 4, 128)),
                    ALU.mult))
            for h in range(4):
                b = bank()
                PE.quiet(lambda e, b=b, h=h: e.matmul(ps[b][:, 0:128], upto, LB[:, h, 0:128], start=True, stop=True),
                         t, *ps_free[b])
                PE.quiet(lambda e, b=b, h=h: e.matmul(ps[b][:, 128:256], upto, LB[:, h, 128:256], start=True,
                                                      stop=False))
                PE.quiet(lambda e, b=b, h=h: e.matmul(ps[b][:, 128:256], ones, LB[:, h, 256:384], start=False,
                                                      stop=True))
                t3 = PE.op(lambda e, b=b, h=h: e.matmul(ps[b][:, 256:384], upto, LB[:, h, 256:384], start=True,
                                                        stop=True))
                a = DVE.op(lambda e, b=b, h=h: e.tensor_tensor(LA[:, h, :], LA[:, h, :], ps[b][:, 0:384],
                                                               ALU.subtract), t3)
                ps_free[b] = [a]
            t = DVE.op(lambda e: e.scalar_tensor_tensor(
                out=LA, in0=LA, scalar=0.0, in1=c_("sbneg").unsqueeze(1).broadcast_to((128, 4, 384)),
                op0=ALU.min, op1=ALU.add))
            a = ACT.op(lambda e: e.activation(LA, LA, ACTF.Exp), t)
            b0, b1 = bank(), bank()
            for h in range(4):
                hh = (hg + h) * 64
                o = h * 64
                PE.quiet(lambda e, h=h, o=o, hh=hh, b0=b0: e.matmul(ps[b0][:, o:o + 64], LA[:, h, 0:128],
                                                                    VV[1][:, 0, hh:hh + 64], start=True, stop=True),
                         a, t_qk["vs"], *ps_free[b0])
                PE.quiet(lambda e, h=h, o=o, hh=hh, b1=b1: e.matmul(ps[b1][:, o:o + 64], LA[:, h, 128:256],
                                                                    VV[1][:, 0, hh:hh + 64], start=True, stop=False),
                         *ps_free[b1])
                t = PE.op(lambda e, h=h, o=o, hh=hh, b1=b1: e.matmul(ps[b1][:, o:o + 64], LA[:, h, 256:384],
                                                                     VV[1][:, 1, hh:hh + 64], start=False, stop=True))
            for tt, b in ((0, b0), (1, b1)):
                ps_free[b] = [DVE.op(lambda e, tt=tt, b=b, hg=hg: e.tensor_copy(
                    OS[:, tt, hg * 64:hg * 64 + 256], ps[b][:, 0:256]), t)]

        mx, den = small(16), small(16)
        mx3, den3 = (v.rearrange("p (t h) -> p t h", t=2) for v in (mx, den))
        for hg in (0, 4):
            for h in range(hg, hg + 4):
                b = bank()
                PE.quiet(lambda e, b=b, h=h: e.matmul(ps[b][:, 0:128], head(0, h)[:, 0:128], head(1, h)[:, 0:128],
                                                      start=True, stop=True), t_qk["qd"], t_qk["kd"], *ps_free[b])
                t = PE.op(lambda e, b=b, h=h: e.matmul(ps[b][:, 128:384], head(0, h)[:, 128:256], head(1, h),
                                                       start=True, stop=True))
                slope = 2.0 ** -(h + 1)
                a = DVE.op(lambda e, b=b, h=h, slope=slope: e.scalar_tensor_tensor(
                    out=LC[:, h % 4, :], in0=c_("dist"), scalar=-8.0 * slope, in1=ps[b][:, 0:384],
                    op0=ALU.mult, op1=ALU.add), t, PE.last)
                ps_free[b] = [a]
            DVE.op(lambda e, hg=hg: e.reduce_max(mx3[:, 0, hg:hg + 4], LC[:, :, 0:128], AX))
            DVE.op(lambda e, hg=hg: e.reduce_max(mx3[:, 1, hg:hg + 4], LC[:, :, 128:384], AX))
            t = DVE.op(lambda e, hg=hg: e.tensor_scalar(mx3[:, :, hg:hg + 4], mx3[:, :, hg:hg + 4], -0.125, None,
                                                        ALU.mult))
            for h in range(4):
                for tt, o, n in ((0, 0, 128), (1, 128, 256)):
                    a = ACT.op(lambda e, h=h, tt=tt, o=o, n=n, hg=hg: e.activation(
                        LC[:, h, o:o + n], LC[:, h, o:o + n], ACTF.Exp, bias=mx3[:, tt, hg + h:hg + h + 1],
                        scale=0.125), t)
            DVE.op(lambda e: e.tensor_tensor(LC, LC, c_("count").unsqueeze(1).broadcast_to((128, 4, 384)),
                                             ALU.mult), a)
            t_lc = DVE.last
            DVE.op(lambda e, hg=hg: e.reduce_sum(den3[:, 0, hg:hg + 4], LC[:, :, 0:128], AX))
            DVE.op(lambda e, hg=hg: e.reduce_sum(den3[:, 1, hg:hg + 4], LC[:, :, 128:384], AX))
            DVE.op(lambda e, hg=hg: e.reciprocal(den3[:, :, hg:hg + 4], den3[:, :, hg:hg + 4]))
            for h in range(4):
                b = bank()
                for o in (0, 128, 256):
                    t = PE.op(lambda e, b=b, h=h, o=o: e.transpose(ps[b][:, o:o + 128], LC[:, h, o:o + 128], ident),
                              t_lc, *ps_free[b])
                a = ACT.op(lambda e, b=b, h=h: e.activation(LB[:, h, :], ps[b][:, 0:384], ACTF.Copy), t, DVE.last)
                ps_free[b] = [a]
            b0, b1 = bank(), bank()
            for h in range(4):
                hh = (hg + h) * 64
                o = h * 64
                PE.quiet(lambda e, h=h, o=o, hh=hh, b0=b0: e.matmul(ps[b0][:, o:o + 64], LB[:, h, 0:128],
                                                                    VV[0][:, 0, hh:hh + 64], start=True, stop=True),
                         a, t_qk["vd"], *ps_free[b0])
                PE.quiet(lambda e, h=h, o=o, hh=hh, b1=b1: e.matmul(ps[b1][:, o:o + 64], LB[:, h, 128:256],
                                                                    VV[0][:, 0, hh:hh + 64], start=True, stop=False),
                         *ps_free[b1])
                t = PE.op(lambda e, h=h, o=o, hh=hh, b1=b1: e.matmul(ps[b1][:, o:o + 64], LB[:, h, 256:384],
                                                                     VV[0][:, 1, hh:hh + 64], start=False, stop=True))
            for tt, b in ((0, b0), (1, b1)):
                ps_free[b] = [DVE.op(lambda e, tt=tt, b=b, hg=hg: e.tensor_tensor(
                    OD[:, tt, hg * 64:hg * 64 + 256].rearrange("p (h c) -> p h c", h=4),
                    ps[b][:, 0:256].rearrange("p (h c) -> p h c", h=4),
                    den3[:, tt, hg:hg + 4].unsqueeze(2).broadcast_to((128, 4, 64)), ALU.mult), t)]
        ss = small(4)
        for n, O in enumerate((OD, OS)):
            for tt in range(2):
                t = ACT.op(lambda e, n=n, O=O, tt=tt: e.activation(TMP[:, 0:512], O[:, tt, :], ACTF.Square,
                                                                   accum_out=ss[:, 2 * n + tt:2 * n + tt + 1]),
                           DVE.last)
        t = rstd(ss, 1.0 / 512, t)
        for n, O in enumerate((OD, OS)):
            for tt in range(2):
                t = DVE.op(lambda e, n=n, O=O, tt=tt: e.tensor_scalar(O[:, tt, :], O[:, tt, :],
                                                                      ss[:, 2 * n + tt:2 * n + tt + 1], None, ALU.mult))
        mts = to_T(lambda tt, k: (OD if k < 4 else OS)[:, tt, (k % 4) * 128:(k % 4) * 128 + 128], HT, 8,
                   lambda k: (col("g_dil_out_2", k) if k < 4 else col("g_sb_out_2", k - 4), None), t)
        for nn in range(2):
            i, tw = stream((k8, cols(I["w_out_2"][0], 512 * nn, 512)))
            for tt in range(2):
                b = bank()
                t = tmaj(lambda k: HT[:, k, :], lambda k, i=i: k8(ring[i])[:, k, :], 8, tt, b, [tw, *mts])
                a = DVE.op(lambda e, b=b, nn=nn: e.tensor_tensor(TMP[:, 0:512], ps[b][:, :],
                                                                 MR[:, 0, nn * 512:nn * 512 + 512], ALU.mult),
                           t, t_mr)
                ps_free[b] = [a]
                t_x4 = DVE.op(lambda e, tt=tt, nn=nn: e.tensor_tensor(
                    X[:, tt, nn * 512:nn * 512 + 512], X[:, tt, nn * 512:nn * 512 + 512], TMP[:, 0:512], ALU.add))
            ring_free[i] = PE.last

        GF2 = ar(0, 1024)
        GFI = ar(1024, 1024)
        SP.dma(GF2, I["g_ffn_2"][0].partition_broadcast(128), dsem("gf2"), t_x4)
        SP.dma(GFI, I["g_final_2"].partition_broadcast(128), dsem("gfi"), t_x4)
        WR = ar(2048, 8 * 36, 8)
        SP.dma(WR[:, :, 0:4], I["w_group_2"][0].rearrange("(k p) n -> p k n", p=128), dsem("wr"), t_x4)
        SP.dma(WR[:, :, 4:36], I["w_expert_2"][0].rearrange("(k p) n -> p k n", p=128), dsem("wr"), t_x4)
        H2 = ar(14576, 2048, 2)
        t = norm_scaled(H2, TMP, t_x4, PE.last)
        DVE.op(lambda e: e.scalar_tensor_tensor(out=GF2, in0=MR[:, 2, :], scalar=1.0, in1=GF2, op0=ALU.add,
                                                op1=ALU.mult), dtok("gf2"), t_mr)
        for tt in range(2):
            DVE.op(lambda e, tt=tt: e.tensor_tensor(H2[:, tt, :], H2[:, tt, :], GF2, ALU.mult))
            t = DVE.op(lambda e, tt=tt: e.tensor_tensor(H2[:, tt, :], H2[:, tt, :], MR[:, 1, :], ALU.add))
        hts = to_T(lambda tt, k: H2[:, tt, k * 128:k * 128 + 128], HT, 8, None, t)
        RT = sb("RT", [128, 2, 36])
        for tt in range(2):
            b = bank()
            t = tmaj(lambda k: HT[:, k, :], lambda k: WR[:, k, :], 8, tt, b, [dtok("wr"), *hts], n=36)
            ps_free[b] = [DVE.op(lambda e, tt=tt, b=b: e.tensor_copy(RT[:, tt, :], ps[b][:, 0:36]), t)]
        gm, gs = small(2), small(2)
        GE, G1 = small(8).rearrange("p (t g) -> p t g", t=2), small(8).rearrange("p (t g) -> p t g", t=2)
        iota = c_("iota")
        gl = RT[:, :, 0:4]

        def bc(v, n):
            return v.unsqueeze(2).broadcast_to((128, 2, n))

        def first_max(vals, n, mx_, hot, tmp):
            ix = small(2)
            io = iota[:, 0:n].unsqueeze(1).broadcast_to((128, 2, n))
            DVE.op(lambda e: e.reduce_max(mx_, vals, AX))
            DVE.op(lambda e: e.tensor_tensor(tmp, vals, bc(mx_, n), ALU.is_lt))
            DVE.op(lambda e: e.scalar_tensor_tensor(out=tmp, in0=tmp, scalar=64.0, in1=io, op0=ALU.mult, op1=ALU.add))
            DVE.op(lambda e: e.tensor_reduce(ix, tmp, AX, ALU.min))
            return DVE.op(lambda e: e.tensor_tensor(hot, io, bc(ix, n), ALU.is_equal))

        first_max(gl, 4, gm, G1, GE)
        DVE.op(lambda e: e.tensor_tensor(GE, gl, bc(gm, 4), ALU.subtract))
        t = ACT.op(lambda e: e.activation(GE, GE, ACTF.Exp), DVE.last)
        DVE.op(lambda e: e.reduce_sum(gs, GE, AX), t)
        DVE.op(lambda e: e.reciprocal(gs, gs))
        DVE.op(lambda e: e.tensor_scalar(G1, G1, 1.0, BIG, ALU.subtract, ALU.mult))
        el = RT[:, :, 4:36]
        for g in range(4):
            DVE.op(lambda e, g=g: e.tensor_tensor(el[:, :, 8 * g:8 * g + 8], el[:, :, 8 * g:8 * g + 8],
                                                  bc(G1[:, :, g], 8), ALU.add))
        hot1, hot2, tmp = (small(64).rearrange("p (t g) -> p t g", t=2) for _ in range(3))
        m1, m2, dd = small(2), small(2), small(2)
        first_max(el, 32, m1, hot1, tmp)
        DVE.op(lambda e: e.scalar_tensor_tensor(out=el, in0=hot1, scalar=-3.0 * BIG, in1=el, op0=ALU.mult,
                                                op1=ALU.add))
        first_max(el, 32, m2, hot2, tmp)
        DVE.op(lambda e: e.tensor_tensor(dd, m2, m1, ALU.subtract))
        t = ACT.op(lambda e: e.activation(dd, dd, ACTF.Exp), DVE.last)
        DVE.op(lambda e: e.tensor_scalar(m1, dd, 1.0, None, ALU.add), t)
        DVE.op(lambda e: e.reciprocal(m1, m1))
        DVE.op(lambda e: e.tensor_tensor(m1, m1, gs, ALU.mult))
        DVE.op(lambda e: e.tensor_tensor(m2, m1, dd, ALU.mult))
        WC = sb("WC", [128, 2, 32])
        DVE.op(lambda e: e.tensor_tensor(WC[:, :, :], hot1, bc(m1, 32), ALU.mult))
        DVE.op(lambda e: e.tensor_tensor(tmp, hot2, bc(m2, 32), ALU.mult))
        t_wc = DVE.op(lambda e: e.tensor_tensor(WC[:, :, :], WC[:, :, :], tmp, ALU.add))

        AS, RK, WL = (sb(n, [128, 2, 32]) for n in ("AS", "RK", "WL"))
        t_as = DVE.op(lambda e: e.tensor_tensor(AS[:, :, :], hot1, hot2, ALU.add))
        b = bank()
        before, ones = c_("before"), c_("ones")
        PE.quiet(lambda e, b=b: e.matmul(ps[b][:, 0:32], before, AS[:, 0, :], start=True, stop=True), t_as,
                 *ps_free[b])
        PE.quiet(lambda e, b=b: e.matmul(ps[b][:, 32:64], ones, AS[:, 0, :], start=True, stop=False))
        t = PE.op(lambda e, b=b: e.matmul(ps[b][:, 32:64], before, AS[:, 1, :], start=False, stop=True))
        t = DVE.op(lambda e, b=b: e.scalar_tensor_tensor(
            out=RK[:, :, :], in0=ps[b][:, 0:64].rearrange("p (t n) -> p t n", t=2), scalar=1.0, in1=AS[:, :, :],
            op0=ALU.add, op1=ALU.mult), t)
        ps_free[b] = [t]
        t_rk = DVE.op(lambda e: e.tensor_scalar(RK[:, :, :], RK[:, :, :], 1.0, None, ALU.subtract))
        over, left = small(1), small(1)
        DVE.op(lambda e: e.tensor_scalar(WL[:, :, :], RK[:, :, :], float(CAP), None, ALU.is_ge))
        t = DVE.op(lambda e: e.tensor_reduce(over, WL[:, :, :].rearrange("p t n -> p (t n)"), AX, ALU.max))
        b = bank()
        t = PE.op(lambda e, b=b: e.matmul(ps[b][:, 0:1], ones, over, start=True, stop=True), t, *ps_free[b])
        t = DVE.op(lambda e, b=b: e.tensor_scalar(left, ps[b][:, 0:1], 1.0, None, ALU.min), t)
        ps_free[b] = [t]
        FLAG = sb("FLAG", [128, 1], mybir.dt.int32)
        DVE.op(lambda e: e.tensor_copy(FLAG[:, :], left))
        t_wl = DVE.op(lambda e: e.tensor_tensor(WL[:, :, :], WL[:, :, :], WC[:, :, :], ALU.mult))

        SE = [ar(12800 + 256 * n, 256) for n in range(2)]
        SW = [ar(2400 + 1024 * n, 1024) for n in range(2)]
        XG = [ar(16624 + 1024 * n, 1024, 8) for n in range(2)]
        SWT = [ar(18672 + 256 * n, 256) for n in range(2)]
        YP = [ar(19184 + 1024 * n, 1024) for n in range(2)]
        HS = [ar(21232 + 256 * n, 256) for n in range(2)]
        HE = [ar(21744 + 128 * n, 128) for n in range(2)]
        Y = ar(22016, 2048, 2)
        yb = [bank() for _ in range(4)]
        yfree = [w for b in yb for w in ps_free[b]]
        ps_held.update(yb)
        sw_free = [None, None]
        xg_free = [None, None]
        xg_tok, sw_tok = [None, None], [None, None]
        state = {}

        def gather(g):
            n = g % 2
            io = iota.unsqueeze(1).broadcast_to((128, 4, 32))
            for tt in range(2):
                v = SE[n][:, tt * 128:tt * 128 + 128].rearrange("p (x s) -> p x s", x=4)
                r = RK[:, tt, 4 * g:4 * g + 4].unsqueeze(2).broadcast_to((128, 4, 32))
                t = DVE.op(lambda e, v=v, r=r, io=io: e.tensor_tensor(v, r, io, ALU.is_equal), t_rk, xg_free[n])
            for tt in range(2):
                v = SE[n][:, tt * 128:tt * 128 + 128].rearrange("p (x s) -> p x s", x=4)
                v = v.unsqueeze(2).broadcast_to((128, 4, 4, 32))
                u = SW[n][:, tt * 512:tt * 512 + 512].rearrange("p (x q s) -> p x q s", x=4, q=4)
                r = WC[:, tt, 4 * g:4 * g + 4].unsqueeze(2).unsqueeze(3).broadcast_to((128, 4, 4, 32))
                sw_tok[n] = DVE.op(lambda e, v=v, r=r, u=u: e.tensor_tensor(u, v, r, ALU.mult), sw_free[n])
            done = []
            for k0 in (0, 4):
                b = bank()
                for k in range(k0, k0 + 4):
                    for tt in range(2):
                        p = PE.op(lambda e, b=b, k=k, k0=k0, tt=tt, n=n: e.matmul(
                            ps[b][:, (k - k0) * 128:(k - k0) * 128 + 128], H2[:, tt, k * 128:k * 128 + 128],
                            SE[n][:, tt * 128:tt * 128 + 128], start=(tt == 0), stop=(tt == 1)), t, *ps_free[b])
                v = ps[b][:, :].rearrange("p (k n) -> p k n", k=4)
                d = XG[n][:, k0:k0 + 4, :]
                if k0:
                    c = DVE.op(lambda e, v=v, d=d: e.tensor_copy(d, v), p)
                else:
                    c = ACT.op(lambda e, v=v, d=d: e.activation(d, v, ACTF.Copy), p, xg_free[n])
                ps_free[b] = [c]
                done.append(c)
            xg_tok[n] = done

        def gate_up(x):
            n = (x // 4) % 2
            ig, tg = stream((k8, cols(I["w_gate_2"][0, x], 0, 512)))
            iu, tu = stream((k8, cols(I["w_up_2"][0, x], 0, 512)))
            b = bank()
            for k in range(8):
                for q in range(4):
                    w = k8(ring[ig if q < 2 else iu])[:, k, (q % 2) * 256:(q % 2) * 256 + 256]
                    xs = XG[n][:, k, (x % 4) * 32:(x % 4) * 32 + 32]
                    f = (lambda e, b=b, q=q, w=w, xs=xs, k=k: e.matmul(ps[b][32 * q:32 * q + 32, 0:256], xs, w,
                                                                       start=(k == 0), stop=(k == 7)))
                    if k == 7 and q == 3:
                        t = PE.op(f)
                    else:
                        PE.quiet(f, tg, tu, *xg_tok[n], *ps_free[b])
            ring_free[ig] = ring_free[iu] = t
            if x % 4 == 3:
                xg_free[n] = t
            h = HS[x % 2]
            a = ACT.op(lambda e, b=b, h=h: e.activation(h[0:64, :], ps[b][0:64, 0:256], ACTF.Silu), t,
                       state.get(("T", x - 2)))
            a = DVE.op(lambda e, b=b, h=h: e.tensor_tensor(h[0:64, :], h[0:64, :], ps[b][64:128, 0:256], ALU.mult), a)
            ps_free[b] = [a]
            state["H", x] = a

        def turn(x):
            n = (x // 4) % 2
            h = HS[x % 2]
            b = bank()
            for j in range(2):
                t = PE.op(lambda e, b=b, j=j, h=h: e.transpose(ps[b][:, 64 * j:64 * j + 64],
                                                               h[0:64, 128 * j:128 * j + 128], ident[0:64, 0:64]),
                          state["H", x], *ps_free[b])
            state["T", x] = t
            for tt in range(2):
                v = SW[n][:, tt * 512 + (x % 4) * 128:tt * 512 + (x % 4) * 128 + 128]
                t2 = PE.op(lambda e, b=b, v=v, tt=tt: e.transpose(ps[b][:, 128 + 128 * tt:256 + 128 * tt], v, ident),
                           sw_tok[n])
            if x % 4 == 3:
                sw_free[n] = t2
            d = HE[x % 2]
            state["HE", x] = DVE.op(lambda e, b=b, d=d: e.tensor_copy(d, ps[b][:, 0:128]), t, t2,
                                    state.get(("DN", x - 2)))
            d = SWT[x % 2]
            state["SWT", x] = DVE.op(lambda e, b=b, d=d: e.tensor_copy(d, ps[b][:, 128:384]), t2,
                                     state.get(("SC", x - 2)))
            ps_free[b] = [DVE.last]

        def down(x):
            i, td = stream((lambda r: r[:, :].rearrange("p (k n) -> p k n", k=4),
                            I["w_down_2"][0, x].rearrange("(k p) n -> p k n", p=128)))
            W = ring[i][:, :].rearrange("p (k n) -> p k n", k=4)
            bb = [bank(), bank()]
            for nn in range(2):
                for j in range(4):
                    f = (lambda e, nn=nn, j=j, W=W, x=x, b=bb[nn]: e.matmul(
                        ps[b][32 * j:32 * j + 32, :], HE[x % 2][:, 32 * j:32 * j + 32],
                        W[:, 2 * (j % 2) + j // 2, nn * 512:nn * 512 + 512], start=True, stop=True))
                    t = PE.op(f, td, state["HE", x], *ps_free[bb[nn]])
                d = YP[x % 2][:, nn * 512:nn * 512 + 512]
                if nn:
                    c = DVE.op(lambda e, d=d, b=bb[nn]: e.tensor_copy(d, ps[b][:, :]), t, state.get(("SC", x - 2)))
                else:
                    c = ACT.op(lambda e, d=d, b=bb[nn]: e.activation(d, ps[b][:, :], ACTF.Copy), t,
                               state.get(("SC", x - 2)))
                ps_free[bb[nn]] = [c]
                state["YP", x, nn] = c
            ring_free[i] = state["DN", x] = t

        def scatter(x):
            for tt in range(2):
                for nn in range(2):
                    t = PE.op(lambda e, tt=tt, nn=nn, x=x: e.matmul(
                        ps[yb[tt * 2 + nn]][:, :], SWT[x % 2][:, tt * 128:tt * 128 + 128],
                        YP[x % 2][:, nn * 512:nn * 512 + 512], start=(x == 0), stop=(x == NE - 1)),
                        state["SWT", x], state["YP", x, 0], state["YP", x, 1], *yfree)
            state["SC", x] = t

        gather(0)
        for x in range(NE + 2):
            if x < NE:
                gate_up(x)
            if 1 <= x <= NE:
                turn(x - 1)
            if x >= 2:
                scatter(x - 2)
            if 1 <= x <= NE:
                down(x - 1)
            if x % 4 == 1 and x + 3 < NE:
                gather(x // 4 + 1)
        for j in range(4):
            DVE.op(lambda e, j=j: e.tensor_copy(Y[:, j // 2, (j % 2) * 512:(j % 2) * 512 + 512], ps[yb[j]][:, :]),
                   state["SC", NE - 1])

        def emit_all():
            with nc.Block() as block:
                block.sync(SP.emit)
                block.gpsimd(POOL.emit)
                block.scalar(ACT.emit)
                block.vector(DVE.emit)
                block.tensor(PE.emit)
            for q in (SP, POOL, ACT, DVE, PE):
                q.items = []

        emit_all()
        general(nc, ctx, I, nc.values_load(FLAG[0:1, 0:1], min_val=0, max_val=1), HT, Y, WL, ring, ps,
                (YP[1], ar(18672, 1024, 4)))
        for tt in range(2):
            DVE.op(lambda e, tt=tt: e.tensor_tensor(Y[:, tt, :], Y[:, tt, :], MR[:, 3, :], ALU.mult))
            DVE.op(lambda e, tt=tt: e.tensor_tensor(X[:, tt, :], X[:, tt, :], Y[:, tt, :], ALU.add))
        t = norm_scaled(H2, YP[0], DVE.last)
        for tt in range(2):
            t = DVE.op(lambda e, tt=tt: e.tensor_tensor(H2[:, tt, :], H2[:, tt, :], GFI, ALU.mult), dtok("gfi"))
        SP.dma(out[0].rearrange("(t p) d -> p t d", p=128), H2, dsem("out"), t)
        SP.wait(dtok("out"))
        emit_all()


def general(nc, ctx, I, flag, HT, Y, WL, ring, ps, room):
    TMP, HH = room
    names = ("gpe", "gact", "gdve", "dg", "du", "dd")
    s_pe, s_act, s_dve, s_g, s_u, s_d = sems = [ctx.enter_context(nc.semaphore(n)) for n in names]
    G, U = (ring[n][:, :].rearrange("p (k n) -> p k n", k=8) for n in (0, 1))
    W = ring[2][:, :].rearrange("p (k n) -> p k n", k=4)
    with nc.If(flag > 0):
        with nc.Fori(0, NE) as x:
            with nc.Block() as block:
                @block.sync
                def _(eng):
                    for dst, name, s in ((G, "w_gate_2", s_g), (U, "w_up_2", s_u), (W, "w_down_2", s_d)):
                        eng.dma_start(dst, I[name][0, bass.ds(x, 1)].rearrange("a (k p) n -> p (a k) n", p=128))\
                           .then_inc(s, 16)

                @block.tensor
                def _(eng):
                    eng.wait_ge(s_g, 16)
                    eng.wait_ge(s_u, 16)
                    for f in range(4):
                        for n, S in enumerate((G, U)):
                            for k in range(8):
                                mm = eng.matmul(ps[f][:, n * 256:n * 256 + 256], S[:, k, f * 128:f * 128 + 128],
                                                HT[:, k, :], start=(k == 0), stop=(k == 7))
                        mm.then_inc(s_pe, 1)
                    eng.wait_ge(s_d, 16)
                    eng.wait_ge(s_dve, 4)
                    for j in range(4):
                        for k in range(4):
                            mm = eng.matmul(ps[4 + j][:, :], HH[:, k, (j // 2) * 128:(j // 2) * 128 + 128],
                                            W[:, k, (j % 2) * 512:(j % 2) * 512 + 512], start=(k == 0), stop=(k == 3))
                        mm.then_inc(s_pe, 1)

                @block.scalar
                def _(eng):
                    for f in range(4):
                        eng.wait_ge(s_pe, f + 1)
                        eng.activation(TMP[:, f * 256:f * 256 + 256], ps[f][:, 0:256], ACTF.Silu).then_inc(s_act, 1)

                @block.vector
                def _(eng):
                    for f in range(4):
                        eng.wait_ge(s_act, f + 1)
                        eng.tensor_tensor(HH[:, f, :], ps[f][:, 256:512], TMP[:, f * 256:f * 256 + 256], ALU.mult)\
                           .then_inc(s_dve, 1)
                    for j in range(4):
                        y = Y[:, j // 2, (j % 2) * 512:(j % 2) * 512 + 512]
                        eng.wait_ge(s_pe, 5 + j)
                        eng.scalar_tensor_tensor(out=y, in0=ps[4 + j][:, :], scalar=WL[:, j // 2, bass.ds(x, 1)],
                                                 in1=y, op0=ALU.mult, op1=ALU.add).then_inc(s_dve, 1)
            for s in sems:
                nc.sync.sem_clear(s)
            nc.all_engine_barrier()


_INS = ["x", "p", "g_mix_pre", "w_in", "w_sgu_s", "b_sgu_s", "g_sgu_v", "b_sgu_v", "w_sgu_out", "w_dw", "b_dw",
        "g_conv_ln", "b_conv_ln", "w_conv_out", "w_pool", "s_pool", "w_pool_out", "w_out", "g_mix_post",
        "g_ffn_pre", "w_ffn_in", "w_ffn_out", "g_ffn_post", "w_ple", "w_ple_gate", "c_2", "w_ada_2", "b_ada_2",
        "g_mix_2", "w_in_2", "g_dil_out_2", "g_sb_out_2", "w_out_2", "g_ffn_2", "w_group_2", "w_expert_2",
        "w_gate_2", "w_up_2", "w_down_2", "g_final_2"]


def kernel(**inputs):
    import concourse.bacc as _bacc
    from concourse.bass_utils import run_bass_kernel_spmd as _run

    nc = _bacc.Bacc("TRN2", target_bir_lowering=False, num_devices=1)
    arrays, I = {}, {}
    for name in _INS:
        a = np.ascontiguousarray(inputs[name])
        arrays[f"in_{name}"] = a
        I[name] = nc.dram_tensor(f"in_{name}", a.shape, mybir.dt.from_np(a.dtype), kind="ExternalInput").ap()
    cst, at = constants()
    arrays["in_cst"] = cst
    I["cst"] = nc.dram_tensor("in_cst", cst.shape, F32, kind="ExternalInput").ap()
    out = nc.dram_tensor("out_0", (1, T, D), F32, kind="ExternalOutput").ap()
    program(nc, I, out, at)
    r = _run(nc, [arrays], core_ids=[0])
    return r.results[0]["out_0"]
```

```python
from contextlib import ExitStack

import numpy as np

import concourse.bass as bass
from concourse import mybir

F32 = mybir.dt.float32
F32R = mybir.dt.float32r
ALU = mybir.AluOpType
ACTF = mybir.ActivationFunctionType
AX = mybir.AxisListType.X

T = 256
D = 1024
NFF = 22
NE = 32
EPS = 1e-6
WIN = (2, 4, 8, 16)
NRAW = 5
CAP = 32
BIG = 1e30


def constants():
    p = np.arange(128)
    at, parts, n = {}, [], 0

    def put(name, a):
        nonlocal n
        a = np.asarray(a, np.float32).reshape(128, -1)
        at[name] = (n, a.shape[1])
        parts.append(a)
        n += a.shape[1]

    put("ident", np.eye(128))
    put("eps", np.full((128, 1), EPS))
    put("one", np.ones((128, 1)))
    put("zero", np.zeros((128, 1)))
    put("iota", np.tile(np.arange(32)[None], (128, 1)))
    put("ones", np.ones((128, 128)))
    put("upto", p[:, None] >= p[None, :])
    put("before", p[:, None] < p[None, :])
    put("mean", np.full((128, 128), 1.0 / D))
    put("sgum", (p[:, None] // 64) <= (p[None, :] // 64))
    put("invc", np.tile(np.stack([1.0 / np.minimum(np.arange(1, 17), w) for w in WIN]).reshape(1, -1), (128, 1)))
    dist = np.concatenate([p[:, None] - p[None, :], p[:, None] + 128 - np.arange(256)[None, :]], 1)
    count = ((dist >= 0) & (dist <= 128)) * 1.0 + ((dist >= 0) & (dist % 4 == 0)) + ((dist >= 0) & (dist % 16 == 0))
    put("dist", np.where(count > 0, dist, 1e30))
    put("count", count)
    sb = np.concatenate([np.where(p[:, None] < p[None, :], 0.0, -BIG), np.zeros((128, 128)),
                         np.where(p[:, None] < p[None, :], 0.0, -BIG)], 1)
    put("sbneg", sb)
    return np.concatenate(parts, 1), at


class Tok:

    def __init__(self, sem, val):
        self.sem, self.val = sem, val


def flat(waits):
    for w in waits:
        if isinstance(w, list):
            yield from flat(w)
        else:
            yield w


class Queue:

    def __init__(self, sem, chained):
        self.sem, self.chained, self.n, self.items, self.last = sem, chained, 0, [], None

    def op(self, fn, *waits):
        if self.chained and self.last:
            waits = (*waits, self.last)
        self.n += 1
        self.last = Tok(self.sem, self.n)
        self.items.append((fn, waits, (self.sem, 1)))
        return self.last

    def quiet(self, fn, *waits):
        self.items.append((fn, waits, None))

    def dma(self, dst, src, sem, *waits):
        self.items.append((lambda e: e.dma_start(dst, src), waits, (sem, 16)))

    def wait(self, *waits):
        self.items.append((None, waits, None))

    def emit(self, eng):
        seen = {}
        for fn, waits, inc in self.items:
            need = {}
            for w in flat(waits):
                if w is not None:
                    need[id(w.sem)] = max(need.get(id(w.sem), (0, None))[0], w.val), w.sem
            for key, (val, sem) in need.items():
                if seen.get(key, 0) < val:
                    eng.wait_ge(sem, val)
                    seen[key] = val
            if fn is None:
                continue
            ins = fn(eng)
            if inc:
                ins.then_inc(*inc)


def program(nc, I, out, const_at):
    with ExitStack() as ctx:
        def sb(name, shape, dt=F32):
            return ctx.enter_context(nc.sbuf_tensor(name, shape, dt))

        def sem(name):
            return ctx.enter_context(nc.semaphore(name))

        PE, ACT, DVE, POOL, SP = (Queue(sem("s_" + n), n in ("act", "dve", "pool"))
                                  for n in ("pe", "act", "dve", "pool", "sp"))
        sems = {}

        def dsem(name):
            if name not in sems:
                sems[name] = [sem("d_" + name), 0]
            sems[name][1] += 16
            return sems[name][0]

        def dtok(name):
            return Tok(*sems[name])

        ps = [ctx.enter_context(nc.psum_tensor(f"ps{i}", [128, 512], F32)) for i in range(8)]
        ps_free = [[] for _ in range(8)]
        ps_next = [0]
        ps_held = set()

        def bank():
            i = ps_next[0]
            while i in ps_held:
                i = (i + 1) % 8
            ps_next[0] = (i + 1) % 8
            return i

        base = (nc.sbuf_base + 31) // 32 * 32

        def at(name, off, n, dt=F32, parts=128):
            assert base + 4 * (off + n) <= nc.sbuf_usable_end, (name, off, n)
            return nc.alloc_sbuf_tensor_at(name, [parts, n], dt, offset=base + 4 * off)[:, :]

        def cols(w, a, n):
            return w[:, a:a + n].rearrange("(k p) n -> p k n", p=128)

        def k8(t):
            return t.rearrange("p (k n) -> p k n", k=8)

        O_X, O_RAW, O_SPL, O_XA, O_XB, O_AR = 3456, 5504, 15744, 23936, 28032, 32128
        TOP = 53208
        cst_w = max(o + n for o, n in const_at.values())
        CST = at("cst", 0, 2056)

        def c_(name):
            o, n = const_at[name]
            return CST[:, o:o + n]

        ident, ones, mean = c_("ident"), c_("ones"), c_("mean")
        X = at("X", O_X, 2048).rearrange("p (t n) -> p t n", t=2)
        COL = at("COL", 2056, 320)
        SM = at("SM", 2376, 640)
        RAW = [at(f"raw{i}", O_RAW + 2048 * i, 2048) for i in range(NRAW)]
        SPH = [at(f"sph{i}", O_SPL + 4096 * i, 2048, F32R) for i in range(2)]
        SPLO = [at(f"spl{i}", O_SPL + 4096 * i + 2048, 2048, F32R) for i in range(2)]
        XAH, XAL = (k8(at(n, O_XA + 2048 * i, 2048, F32R)) for i, n in enumerate(("xah", "xal")))
        XBH, XBL = (k8(at(n, O_XB + 2048 * i, 2048, F32R)) for i, n in enumerate(("xbh", "xbl")))
        XA, XB = (XAH, XAL), (XBH, XBL)
        sm_at = [0]

        def small(n):
            a = sm_at[0]
            sm_at[0] += n
            assert sm_at[0] <= 640
            return SM[:, a:a + n]

        names = [0]

        def ar(off, n, k=None):
            names[0] += 1
            v = at(f"ar{names[0]}", O_AR + off, n)
            return v if k is None else v.rearrange("p (k n) -> p k n", k=k)

        raw_sem = [sem(f"d_raw{i}") for i in range(NRAW)]
        raw_n = [0] * NRAW
        units, took, n_split = [], [0], [0]
        spl_free, spl_half = [[[], []], [[], []]], [None, None]

        class Unit:
            def __init__(self, pieces, half, lo):
                self.pieces, self.half, self.lo, self.freed = pieces, half, lo, []

        def by_columns(r, h):
            return k8(r)[:, :, 128 * h:128 * h + 128]

        def by_rows(r, h):
            return r[:, 1024 * h:1024 * h + 1024]

        def plan(pieces, half=by_columns, lo="pool"):
            units.append(Unit(pieces, half, lo))

        def load_all(a, b):
            for v in range(a, b):
                u = units[v]
                i = v % NRAW
                for view, src in u.pieces:
                    SP.dma(view(RAW[i]), src, raw_sem[i], units[v - NRAW].freed if v >= NRAW else None)
                    raw_n[i] += 16
                u.raw, u.tok = RAW[i], Tok(raw_sem[i], raw_n[i])

        def do_split(u):
            if not u.half or hasattr(u, "hi"):
                return
            i = n_split[0] % 2
            n_split[0] += 1
            u.i, u.hi, u.lo_, u.ready = i, SPH[i], SPLO[i], []
            q = POOL if u.lo == "pool" else DVE
            for h in range(2):
                H, L, R = u.half(u.hi, h), u.half(u.lo_, h), u.half(u.raw, h)
                free = spl_free[i][h] if spl_half[i] is u.half else [*spl_free[i]]
                a = ACT.op(lambda e, H=H, R=R: e.activation(H, R, ACTF.Copy), u.tok, free)
                u.ready.append(q.op(lambda e, H=H, R=R, L=L: e.tensor_tensor(L, R, H, ALU.subtract), a))
            spl_half[i] = u.half
            u.freed.append(u.ready[1])

        def take():
            v = took[0]
            took[0] += 1
            do_split(units[v])
            for n in range(v + 1, min(v + 4, len(units))):
                if units[n].half:
                    do_split(units[n])
                    break
            return units[v]

        def done(u, h, tok):
            spl_free[u.i][h] = [tok]

        def whole(w, a, half=by_columns):
            plan([(k8, cols(w, a, 256))], half)

        def halves(w, a, b):
            plan([(lambda r: k8(r)[:, :, 0:128], cols(w, a, 128)), (lambda r: k8(r)[:, :, 128:256], cols(w, b, 128))])

        w_in, w_ff, w_ada, w2 = I["w_in"][0], I["w_ffn_in"][0], I["w_ada_2"][0], I["w_in_2"][0]
        for n in range(4):
            whole(w_in, 1024 + 256 * n, by_rows)
        for c in range(8):
            halves(w_in, 2048 + 128 * c, 3072 + 128 * c)
        for a in [256 * n for n in range(4)] + [4096 + 256 * n for n in range(4)]:
            whole(w_in, a)
        for n in range(12):
            whole(w_in, 5120 + 256 * n)
        for n in range(4):
            whole(I["w_sgu_out"][0], 256 * n)
        plan([(lambda r: r.rearrange("p (g k n) -> p g k n", g=4, k=2),
               I["w_pool"][0].rearrange("g (k p) n -> p g k n", p=128))], None)
        for name, half in (("w_pool_out", by_columns), ("w_conv_out", by_columns), ("w_out", by_rows)):
            for n in range(4):
                whole(I[name][0], 256 * n, half)
        n_ada = 0
        for c in range(NFF):
            halves(w_ff, 128 * c, 2816 + 128 * c)
            if c % 3:
                plan([(k8, cols(w_ada, 256 * n_ada, 256))], None)
                n_ada += 1
        for c in range(11):
            if c:
                plan([(k8, cols(w_ada, 256 * n_ada, 256))], None)
                n_ada += 1
            plan([(lambda r: r.rearrange("p (k n) -> p k n", k=2),
                   I["w_ffn_out"][0][256 * c:256 * c + 256, :].rearrange("(k p) n -> p k n", p=128))], by_rows)
        plan([(lambda r: r.rearrange("p (k n) -> p k n", k=2), I["w_ple"][0].rearrange("(k p) n -> p k n", p=128))],
             by_rows)
        for n in range(4):
            whole(I["w_ple_gate"][0], 256 * n, by_rows)
        for a, half in ((1536, by_columns), (1792, by_columns), (2048, by_columns), (2304, by_columns),
                        (2560, by_rows), (2816, by_rows), (0, by_columns), (512, by_columns), (256, by_columns),
                        (768, by_columns), (1024, by_rows), (1280, by_rows)):
            whole(w2, a, half)
        for n in range(4):
            whole(I["w_out_2"][0], 256 * n, by_rows)

        e0 = const_at["iota"][0] + const_at["iota"][1]
        SP.dma(X[:, 0, :], I["x"][0, 0:128, :], dsem("x0"))
        SP.dma(CST[:, 0:e0], I["cst"][:, 0:e0], dsem("idn"))
        SP.dma(X[:, 1, :], I["x"][0, 128:256, :], dsem("x1"))
        rows = ar(10472, 384)
        row_at = {}
        r = 0
        for name, n in (("g_mix_pre", 8), ("b_dw", 8), ("g_conv_ln", 8), ("b_conv_ln", 8), ("s_pool", 8),
                        ("g_ffn_pre", 8), ("c_2", 8), ("g_mix_2", 8), ("g_dil_out_2", 4), ("g_sb_out_2", 4)):
            row_at[name] = r
            (POOL if r else ACT).dma(rows[r:r + n, 0:128], I[name][0].rearrange("(a b) -> a b", b=128), dsem("vecs" if r else "rows"))
            r += n
        NR = r
        wdw = I["w_dw"][0].rearrange("k o (c p) -> (k o c) p", p=128)
        for j in range(2):
            ACT.dma(rows[0:124, 128 + 128 * j:256 + 128 * j], wdw[124 * j:124 * j + 124, :], dsem("rows"))

        def col(name, k):
            a = row_at[name] + k
            return COL[:, a:a + 1]

        def tap(k, c):
            a = NR + k * 8 + c
            return COL[:, a:a + 1]

        idn, rws = dtok("idn"), [dtok("rows"), dtok("vecs")]
        load_all(0, 2)
        SP.wait(rws)
        load_all(2, 5)
        SP.dma(CST[:, e0:cst_w], I["cst"][:, e0:cst_w], dsem("cst"))
        cst = dtok("cst")
        load_all(5, len(units))

        blank = small(1)
        t_blank = DVE.op(lambda e: e.memset(blank, 1.0))

        def warm(func):
            ACT.op(lambda e, f=func, d=small(1): e.activation(d, blank, f), t_blank)

        warm(ACTF.Sqrt)
        def rstd(ss, scale, *waits):
            t = ACT.op(lambda e: e.activation(ss, ss, ACTF.Sqrt, bias=c_("eps"), scale=scale), idn, *waits)
            return DVE.op(lambda e: e.reciprocal(ss, ss), t)

        def scale_of(ss, scale, dg, *waits):
            t = rstd(ss, scale, *waits)
            return DVE.op(lambda e: e.tensor_scalar(dg, ident, ss, None, ALU.mult), t)

        def norm_T(dg, tmp, dst, evac, xw, free, put=None, mid=None):
            ss = small(2)
            banks = [bank() for _ in range(4)]
            for tt in range(2):
                t = ACT.op(lambda e, tt=tt: e.activation(tmp[:, 0:1024], X[:, tt, :], ACTF.Square,
                                                         accum_out=ss[:, tt:tt + 1]), xw[tt], free)
                t = scale_of(ss[:, tt:tt + 1], 1.0 / D, dg[:, 128 * tt:128 * tt + 128], t)
                for k in range(8):
                    o = (k % 2) * 256 + tt * 128
                    p = PE.op(lambda e, b=banks[k // 2], o=o, k=k, tt=tt: e.matmul(
                        ps[b][:, o:o + 128], X[:, tt, k * 128:k * 128 + 128], dg[:, 128 * tt:128 * tt + 128],
                        start=True, stop=True), t, *ps_free[banks[k // 2]])
            if mid:
                mid()
            return [put(banks[n], 2 * n, p) if put else out_T(banks[n], dst, 2 * n, evac, p) for n in range(4)]

        def out_T(b, dst, k0, evac, t):
            hi, lo = dst
            vs = [(k, ps[b][:, (k - k0) * 256:(k - k0) * 256 + 256], evac(k) if evac else None)
                  for k in range(k0, k0 + 2)]
            for k, v, s in vs:
                if s is None:
                    a = ACT.op(lambda e, h=hi[:, k, :], v=v: e.activation(h, v, ACTF.Copy), t)
                else:
                    a = ACT.op(lambda e, h=hi[:, k, :], v=v, s=s: e.activation(h, v, ACTF.Copy, scale=s), t, t_col)
            for k, v, s in vs:
                h, l = hi[:, k, :], lo[:, k, :]
                if s is None:
                    d = DVE.op(lambda e, h=h, l=l, v=v: e.tensor_tensor(l, v, h, ALU.subtract), a)
                else:
                    d = DVE.op(lambda e, h=h, l=l, v=v, s=s: e.scalar_tensor_tensor(
                        out=l, in0=v, scalar=s, in1=h, op0=ALU.mult, op1=ALU.subtract), a)
            ps_free[b] = [d]
            return d

        def to_T(src, dst, nk, evac, *waits, each=(None, None)):
            banks = [bank() for _ in range(0, nk, 2)]
            for tt in range(2):
                for k in range(nk):
                    b, o = banks[k // 2], (k % 2) * 256 + tt * 128
                    t = PE.op(lambda e, b=b, o=o, s=src(tt, k): e.transpose(ps[b][:, o:o + 128], s, ident),
                              *waits, each[tt], *ps_free[b])
            toks = []
            for k0 in range(0, nk, 2):
                b = banks[k0 // 2]
                if isinstance(dst, tuple):
                    toks.append(out_T(b, dst, k0, evac, t))
                    continue
                v = ps[b][:, :].rearrange("p (k n) -> p k n", k=2)
                if (k0 // 2) % 2:
                    c = DVE.op(lambda e, k0=k0, v=v: e.tensor_copy(dst[:, k0:k0 + 2, :], v), t)
                else:
                    c = ACT.op(lambda e, k0=k0, v=v: e.activation(dst[:, k0:k0 + 2, :], v, ACTF.Copy), t)
                ps_free[b] = [c]
                toks.append(c)
            return toks

        def split_operand(src, dst, k0, n, wait, *free):
            hi, lo = dst
            a = ACT.op(lambda e: e.activation(hi[:, k0:k0 + n, :], src, ACTF.Copy), wait, *free)
            return DVE.op(lambda e: e.tensor_tensor(lo[:, k0:k0 + n, :], src, hi[:, k0:k0 + n, :], ALU.subtract), a)

        def products(out_ap, pairs, waits, start=True, stop=True, each=None):
            n = len(pairs)
            for i, ((sh, sl), (mh, ml)) in enumerate(pairs):
                first, last = start and i == 0, stop and i == n - 1
                PE.quiet(lambda e, a=sh, b=mh, f=first: e.matmul(out_ap, a, b, start=f, stop=False), *waits,
                         each[i] if each else None)
                PE.quiet(lambda e, a=sh, b=ml: e.matmul(out_ap, a, b, start=False, stop=False))
                t = PE.op(lambda e, a=sl, b=mh, l=last: e.matmul(out_ap, a, b, start=False, stop=l))
            return t

        def fm_unit(xT, xw, on_bank):
            u = take()
            H, L = k8(u.hi), k8(u.lo_)
            b = bank()
            for h in range(2):
                t = products(ps[b][:, h * 256:h * 256 + 256],
                             [((H[:, k, h * 128:h * 128 + 128], L[:, k, h * 128:h * 128 + 128]),
                               (xT[0][:, k, :], xT[1][:, k, :])) for k in range(8)],
                             [u.ready[h], *ps_free[b]], each=[xw[k // 2] for k in range(8)] if xw else None)
                done(u, h, t)
            ps_free[b] = on_bank(b, t)
            return t

        def tm_unit(xT, xw, outs, waits):
            u = take()
            H, L = k8(u.hi), k8(u.lo_)
            ts = []
            for h in range(2):
                ks = range(4 * h, 4 * h + 4)
                for tt in range(2):
                    c = slice(tt * 128, tt * 128 + 128)
                    t = products(outs[tt], [((xT[0][:, k, c], xT[1][:, k, c]), (H[:, k, :], L[:, k, :]))
                                            for k in ks], [u.ready[h], *waits], h == 0, h == 1,
                                 [xw[k // 2] for k in ks] if xw else None)
                    ts.append(t)
                done(u, h, t)
            return ts[2:]

        def tm_pair(xT, xw):
            bb = [bank(), bank()]
            return bb, tm_unit(xT, xw, [ps[b][:, 0:256] for b in bb], [*ps_free[bb[0]], *ps_free[bb[1]]])

        def wide(xT, outs, waits, first, last):
            u = take()
            H, L = (v.rearrange("p (k n) -> p k n", k=2) for v in (u.hi, u.lo_))
            ts = [None] * 4
            for k in range(2):
                for j in range(4):
                    cc, cn = slice((j // 2) * 128, (j // 2) * 128 + 128), slice((j % 2) * 512, (j % 2) * 512 + 512)
                    ts[j] = products(ps[outs[j]][:, :], [((xT[0][:, k, cc], xT[1][:, k, cc]), (H[:, k, cn], L[:, k, cn]))],
                                     [u.ready[k], waits, *ps_free[outs[j]]], first and k == 0, last and k == 1)
                done(u, k, ts[3])
            return ts

        def plain(xT, W, nk, tt, b, n, *waits):
            for k in range(nk):
                t = PE.op(lambda e, x=xT[:, k, tt * 128:tt * 128 + 128], w=W[:, k, :], k=k: e.matmul(
                    ps[b][:, 0:n], x, w, start=(k == 0), stop=(k == nk - 1)), *waits, *ps_free[b])
            return t

        def pair(b):
            return ps[b][:, :].rearrange("p (k n) -> p k n", k=2)

        def token_major(xT, xw):
            banks, toks = [bank() for _ in range(4)], [None] * 4
            for n in range(4):
                nn, h = n // 2, n % 2
                outs = [ps[banks[tt * 2 + nn]][:, h * 256:h * 256 + 256] for tt in range(2)]
                toks[nn], toks[2 + nn] = tm_unit(xT, xw, outs, [*ps_free[banks[nn]], *ps_free[banks[2 + nn]]])
            return banks, toks

        def post_norm(banks, toks, grow, gtok, tmp):
            ss4, ss = small(4), small(2)
            out_, free = [], DVE.last
            warm(ACTF.Sqrt)
            for tt in range(2):
                for j in (2 * tt, 2 * tt + 1):
                    t = ACT.op(lambda e, j=j: e.activation(tmp[:, 0:512], ps[banks[j]][:, :], ACTF.Square,
                                                           accum_out=ss4[:, j:j + 1]), toks[j], free)
                s1 = ss[:, tt:tt + 1]
                t = DVE.op(lambda e, tt=tt, s1=s1: e.tensor_tensor(s1, ss4[:, 2 * tt:2 * tt + 1],
                                                                   ss4[:, 2 * tt + 1:2 * tt + 2], ALU.add), t)
                t = rstd(s1, 1.0 / D, t)
                for nn in range(2):
                    j, c = 2 * tt + nn, slice(nn * 512, nn * 512 + 512)
                    a = DVE.op(lambda e, j=j, s1=s1, c=c: e.scalar_tensor_tensor(
                        out=tmp[:, 512:1024], in0=ps[banks[j]][:, :], scalar=s1, in1=grow[:, c],
                        op0=ALU.mult, op1=ALU.mult), gtok, t)
                    ps_free[banks[j]] = [a]
                    t = DVE.op(lambda e, tt=tt, c=c: e.tensor_tensor(X[:, tt, c], X[:, tt, c], tmp[:, 512:1024],
                                                                     ALU.add))
                out_.append(t)
            return out_

        G = ar(0, 6144, 24)
        CV = ar(6144, 8 * 286, 8)
        CVO = ar(8432, 2048, 8)
        U = ar(10480, 2048, 8)
        V = ar(12528, 2048, 2)
        ZP = ar(14576, 8 * 272, 8)
        ZC = ar(16752, 8 * 272, 8)
        TMP = ar(18928, 1024)
        TMP2 = ar(19952, 1024)
        ZB = ar(6144, 8 * 272, 8)
        GV, BV = ar(16752, 1024), ar(17776, 1024)
        WS, WST = ar(0, 1024), ar(1024, 1024)
        BSR = ar(2048, 1024)

        t_col = []

        def columns():
            b = bank()
            PE.quiet(lambda e: e.transpose(ps[b][:, 0:NR], rows[0:NR, 0:128], ident[0:NR, 0:NR]), idn, rws)
            PE.quiet(lambda e: e.transpose(ps[b][:, NR:NR + 124], rows[0:124, 128:256], ident[0:124, 0:124]))
            t = PE.op(lambda e: e.transpose(ps[b][:, NR + 124:NR + 248], rows[0:124, 256:384], ident[0:124, 0:124]))
            t_col.append(DVE.op(lambda e: e.tensor_copy(COL[:, 0:NR + 248], ps[b][:, 0:NR + 248]), t))
            ps_free[b] = [t_col[0]]
            do_split(units[0])

        hts = norm_T(V[:, 0, :], TMP, XA, lambda k: col("g_mix_pre", k), [dtok("x0"), dtok("x1")], None, mid=columns)
        ACT.dma(WS.rearrange("p (h j) -> p h j", h=8), I["w_sgu_s"][0].rearrange("h i j -> i h j"), dsem("ws"))
        ACT.dma(BSR, I["b_sgu_s"].rearrange("a h i -> a (h i)")[0].partition_broadcast(128), dsem("ws"))
        ACT.dma(GV, I["g_sgu_v"][0].partition_broadcast(128), dsem("gv"))
        ACT.dma(BV, I["b_sgu_v"][0].partition_broadcast(128), dsem("gv"))

        mz = POOL.op(lambda e: e.memset(CV[:, :, 0:30], 0.0))
        mz2 = POOL.op(lambda e: e.memset(ZP[:, :, 0:16], 0.0))

        taps = []

        def conv(n):
            for _ in range(min(n, len(taps))):
                taps.pop(0)()

        def glu_unit(c):
            def glu(b, t):
                h = (c % 2) * 256
                s = ACT.op(lambda e: e.activation(TMP[:, h:h + 256], ps[b][:, 256:512], ACTF.Sigmoid), t,
                           glu_free[c % 2])
                m = DVE.op(lambda e: e.tensor_tensor(CV[:, c, 30:286], ps[b][:, 0:256], TMP[:, h:h + 256],
                                                     ALU.mult), s, mz)
                glu_free[c % 2] = m
                taps.append(lambda: DVE.op(lambda e: e.tensor_scalar(
                    CVO[:, c, :], CV[:, c, 0:256], tap(0, c), col("b_dw", c), ALU.mult, ALU.add)))
                for k in range(1, 31):
                    taps.append(lambda k=k: DVE.op(lambda e: e.scalar_tensor_tensor(
                        out=CVO[:, c, :], in0=CV[:, c, k:k + 256], scalar=tap(k, c), in1=CVO[:, c, :],
                        op0=ALU.mult, op1=ALU.add)))
                return [m, s]
            return glu

        for n in range(4):
            bb, ts = tm_pair(XA, hts)
            for tt in range(2):
                ps_free[bb[tt]] = [ACT.op(lambda e, n=n, b=bb[tt], tt=tt: e.activation(
                    V[:, tt, n * 256:n * 256 + 256], ps[b][:, 0:256], ACTF.Gelu_apprx_tanh), ts[tt])]
        t_v = ACT.last
        st, mv = small(24), small(4)
        rs = mv.rearrange("p (t n) -> p t n", t=2)[:, :, 1]

        def v_stats():
            for tt in range(2):
                for nn in range(2):
                    DVE.op(lambda e, tt=tt, nn=nn: e.bn_stats(st[:, (tt * 2 + nn) * 6:(tt * 2 + nn) * 6 + 6],
                                                              V[:, tt, nn * 512:nn * 512 + 512]), t_v)
                DVE.op(lambda e, tt=tt: e.bn_aggr(mv[:, 2 * tt:2 * tt + 2], st[:, tt * 12:tt * 12 + 12]))

        def v_norm():
            DVE.op(lambda e: e.reciprocal(rs, rs), t_vs)
            for tt in range(2):
                DVE.op(lambda e, tt=tt: e.tensor_scalar(V[:, tt, :], V[:, tt, :], mv[:, 2 * tt:2 * tt + 1],
                                                        mv[:, 2 * tt + 1:2 * tt + 2], ALU.subtract, ALU.mult))
                DVE.op(lambda e, tt=tt: e.tensor_tensor(V[:, tt, :], V[:, tt, :], GV, ALU.mult), dtok("gv"))
                DVE.op(lambda e, tt=tt: e.tensor_tensor(V[:, tt, :], V[:, tt, :], BV, ALU.add))
            return DVE.last

        glu_free = [None, None]
        for c in range(8):
            fm_unit(XA, hts, glu_unit(c))
            if c == 0:
                v_stats()
                t_vs = DVE.last
            elif c == 1:
                t_vs = ACT.op(lambda e: e.activation(rs, rs, ACTF.Sqrt, bias=c_("eps")), t_vs)
            elif c == 2:
                t_vn = v_norm()
            conv(11 if c > 2 else 6 if c < 2 else 0)

        for q in (PE, DVE, ACT, POOL):
            q.wait(cst)
        for h0 in (0, 4):
            b = bank()
            for h in range(h0, h0 + 4):
                t = PE.op(lambda e, h=h, b=b, h0=h0: e.transpose(ps[b][:, (h - h0) * 128:(h - h0) * 128 + 128],
                                                                 WS[:, h * 128:h * 128 + 128], ident),
                          dtok("ws"), *ps_free[b])
            a = DVE.op(lambda e, b=b, h0=h0: e.tensor_tensor(
                WST[:, h0 * 128:h0 * 128 + 512].rearrange("p (h i) -> p h i", h=4),
                ps[b][:, :].rearrange("p (h i) -> p h i", h=4),
                c_("sgum").unsqueeze(1).broadcast_to((128, 4, 128)), ALU.mult), t)
            ps_free[b] = [a]
        t_ws = a


        t_um = []

        def mix(h0):
            b = bank()
            for h in (h0, h0 + 1):
                for tt in range(2):
                    o = (h - h0) * 256 + tt * 128
                    t = PE.op(lambda e, b=b, o=o, h=h, tt=tt: e.matmul(
                        ps[b][:, o:o + 128], V[:, tt, h * 128:h * 128 + 128], WST[:, h * 128:h * 128 + 128],
                        start=True, stop=True), t_ws, t_vn, *ps_free[b])
            v = TMP2[:, (h0 % 4) * 256:(h0 % 4) * 256 + 512]
            a = DVE.op(lambda e, b=b, h0=h0, v=v: e.tensor_tensor(
                v.rearrange("p (h t i) -> p h t i", h=2, t=2), ps[b][:, :].rearrange("p (h t i) -> p h t i", h=2, t=2),
                BSR[:, h0 * 128:h0 * 128 + 256].rearrange("p (h i) -> p h i", h=2).unsqueeze(2)
                .broadcast_to((128, 2, 2, 128)), ALU.add), t, dtok("ws"))
            ps_free[b] = [a]
            a = DVE.op(lambda e, h0=h0, v=v: e.tensor_tensor(U[:, h0:h0 + 2, :], U[:, h0:h0 + 2, :],
                                                             v.rearrange("p (k n) -> p k n", k=2), ALU.mult), ACT.last)
            t_um.append(split_operand(U[:, h0:h0 + 2, :], XB, h0, 2, a))
            return t

        for n in range(4):
            fm_unit(XA, [], lambda b, t, n=n: [ACT.op(lambda e: e.activation(
                U[:, 2 * n:2 * n + 2, :], pair(b), ACTF.Gelu_apprx_tanh), t)])
            if n:
                mix(2 * n - 2)
            conv(9)
        for n in range(4):
            fm_unit(XA, [], lambda b, t, n=n: [ACT.op(lambda e: e.activation(
                ZP[:, 2 * n:2 * n + 2, 16:272], pair(b), ACTF.Copy), t, mz2)])
            if n == 0:
                t_mix = mix(6)
            conv(11)
        t_z = ACT.last

        def pool_sums():
            DVE.op(lambda e: e.tensor_tensor(ZB[:, :, 1:272], ZP[:, :, 1:272], ZP[:, :, 0:271], ALU.add), t_z, t_vn)
            DVE.op(lambda e: e.tensor_tensor(ZC[:, 2:8, 3:272], ZB[:, 2:8, 3:272], ZB[:, 2:8, 1:270], ALU.add))
            DVE.op(lambda e: e.tensor_tensor(ZB[:, 4:8, 7:272], ZC[:, 4:8, 7:272], ZC[:, 4:8, 3:268], ALU.add))
            DVE.op(lambda e: e.tensor_tensor(ZC[:, 6:8, 15:272], ZB[:, 6:8, 15:272], ZB[:, 6:8, 7:264], ALU.add))

        def pool_means():
            o = const_at["invc"][0]
            for g, (S_, w) in enumerate(zip((ZB, ZC, ZB, ZC), WIN)):
                k = 2 * g
                inv = CST[:, o + 16 * g:o + 16 * g + 16].unsqueeze(1).broadcast_to((128, 2, 16))
                DVE.op(lambda e, S_=S_, k=k, inv=inv: e.tensor_tensor(S_[:, k:k + 2, 16:32], S_[:, k:k + 2, 16:32],
                                                                      inv, ALU.mult))
                DVE.op(lambda e, S_=S_, k=k: e.tensor_tensor(ZP[:, k:k + 2, 16:32], S_[:, k:k + 2, 16:32],
                                                             ZP[:, k:k + 2, 16:32], ALU.subtract))
                DVE.op(lambda e, S_=S_, k=k, w=w: e.scalar_tensor_tensor(
                    out=ZP[:, k:k + 2, 32:272], in0=S_[:, k:k + 2, 32:272], scalar=1.0 / w,
                    in1=ZP[:, k:k + 2, 32:272], op0=ALU.mult, op1=ALU.subtract))
            return DVE.last

        def channel_mean(src, wait):
            b = bank()
            for c in range(8):
                t = PE.op(lambda e, c=c, b=b: e.matmul(ps[b][:, 0:256], mean, src[:, c, :], start=(c == 0),
                                                       stop=(c == 7)), wait, *ps_free[b])
            return b, t

        SQ = ar(12528, 2048, 8)
        RS = TMP2[:, 0:256]
        t_cs = []

        def silu(c0):
            for c in (c0, c0 + 1):
                a = ACT.op(lambda e, c=c: e.activation(CVO[:, c, :], CVO[:, c, :], ACTF.Silu,
                                                       bias=col("b_conv_ln", c), scale=col("g_conv_ln", c)), var["n"])
            t_cs.append(a)

        for n in range(12):
            fm_unit(XA, [], lambda b, t, n=n: [ACT.op(lambda e: e.activation(
                G[:, 2 * n:2 * n + 2, :], pair(b), ACTF.Sigmoid), t, t_mix)])
            conv(12)
            if n == 9:
                conv(400)
                t_cv = DVE.last
                pool_sums()
            elif n == 10:
                bm, t = channel_mean(CVO, t_cv)
                t_cc = DVE.op(lambda e, b=bm: e.tensor_tensor(
                    CVO, CVO, ps[b][:, 0:256].unsqueeze(1).broadcast_to((128, 8, 256)), ALU.subtract), t)
                ps_free[bm] = [t_cc]
            elif n == 11:
                t_sq = ACT.op(lambda e: e.activation(SQ, CVO, ACTF.Square), t_cc, t_mix)
                t_pl = pool_means()
        t_g = ACT.last
        t_xa = PE.last

        def branch(src, br, waits, between=None):
            for n in range(4):
                def ev(b, t, n=n):
                    k = 2 * n
                    if br == 0:
                        return [DVE.op(lambda e: e.tensor_tensor(G[:, k:k + 2, :], G[:, k:k + 2, :], pair(b),
                                                                 ALU.mult), t, t_g)]
                    q = G[:, br * 8 + k:br * 8 + k + 2, :]
                    a = DVE.op(lambda e: e.tensor_tensor(q, q, pair(b), ALU.mult), t, t_g)
                    m = DVE.op(lambda e: e.tensor_tensor(G[:, k:k + 2, :], G[:, k:k + 2, :], q, ALU.add))
                    if br == 1:
                        merged.append(split_operand(G[:, k:k + 2, :], XA, k, 2, m, t_brc))
                    return [a]

                t = fm_unit(src, waits, ev)
                if between:
                    between(2 * n)
            return t

        merged = []
        var = {}

        def conv_norm(k):
            if k == 0:
                var["b"], var["t"] = channel_mean(SQ, t_sq)
            elif k == 2:
                t = ACT.op(lambda e: e.activation(RS, ps[var["b"]][:, 0:256], ACTF.Sqrt, bias=c_("eps")), var["t"])
                ps_free[var["b"]] = [t]
                DVE.op(lambda e: e.reciprocal(RS, RS), t)
                var["n"] = DVE.op(lambda e: e.tensor_tensor(CVO, CVO, RS.unsqueeze(1).broadcast_to((128, 8, 256)),
                                                            ALU.mult))
            else:
                silu(2 * k - 8), silu(2 * k - 6)

        t_bra = branch(XB, 0, t_um, conv_norm)

        u = take()
        WP = u.raw.rearrange("p (g k n) -> p g k n", g=4, k=2)
        PM = ZC[:, :, 0:256]
        t_pm = []
        for g in range(4):
            b = bank()
            for d in range(2):
                for k in range(2):
                    t = PE.op(lambda e, b=b, d=d, k=k, g=g: e.matmul(
                        ps[b][:, d * 256:d * 256 + 256], WP[:, g, k, d * 128:d * 128 + 128],
                        ZP[:, 2 * g + k, 16:272], start=(k == 0), stop=(k == 1)), u.tok, t_pl, *ps_free[b])
            for d in range(2):
                a = ACT.op(lambda e, b=b, d=d, g=g: e.activation(PM[:, 2 * g + d, :], ps[b][:, d * 256:d * 256 + 256],
                                                                 ACTF.Copy, scale=col("s_pool", 2 * g + d)), t)
            ps_free[b] = [a]
            t_pm.append(split_operand(PM[:, 2 * g:2 * g + 2, :], XA, 2 * g, 2, a, t_xa))
        u.freed.append(t)
        t_brc = branch(XA, 2, t_pm)
        for n in range(4):
            t_cs[n] = split_operand(CVO[:, 2 * n:2 * n + 2, :], XB, 2 * n, 2, t_cs[n], t_bra)
        branch(XB, 1, t_cs)
        ADA = ar(0, 6144)
        t_az = DVE.op(lambda e: e.memset(ADA, 0.0), ACT.last)

        GR = ar(10480, 1024)
        ACT.dma(GR, I["g_mix_post"][0].partition_broadcast(128), dsem("gmp"), t_bra)
        banks, toks = token_major(XA, merged)
        ACT.dma(ADA[0:1, :], I["b_ada_2"], dsem("ada"), t_az)
        t_x1 = post_norm(banks, toks, GR, dtok("gmp"), TMP)

        hts = norm_T(V[:, 0, :], TMP2, XB, lambda k: col("g_ffn_pre", k), t_x1, t_pm[3])
        t_end1 = [PE.last, DVE.last, ACT.last]
        GR2 = ar(17408, 1024)
        FF = [at(f"ff{p}", O_AR + 6144 + 5632 * p, NFF * 256, F32R).rearrange("p (k n) -> p k n", k=NFF)
              for p in range(2)]
        TMPF = ar(18432, 1024)
        PR = ar(19456, 512, 2)
        cond = small(8)
        t_c = ACT.op(lambda e: e.activation(cond, COL[:, row_at["c_2"]:row_at["c_2"] + 8], ACTF.Silu))

        def ada(m):
            u = take()
            for k in range(8):
                a = DVE.op(lambda e, u=u, k=k, m=m: e.scalar_tensor_tensor(
                    out=ADA[:, 256 * m:256 * m + 256], in0=k8(u.raw)[:, k, :], scalar=cond[:, k:k + 1],
                    in1=ADA[:, 256 * m:256 * m + 256], op0=ALU.mult, op1=ALU.add), u.tok, t_c, dtok("ada"))
            u.freed.append(a)
            return a

        sil, t_ff = [None, None], []
        n_ada = 0
        for c in range(NFF):
            def ffg(b, t, c=c):
                h = (c % 2) * 512
                s = ACT.op(lambda e: e.activation(TMPF[:, h:h + 256], ps[b][:, 0:256], ACTF.Silu), t, sil[c % 2],
                           t_end1)
                m = DVE.op(lambda e: e.tensor_tensor(TMPF[:, h + 256:h + 512], ps[b][:, 256:512],
                                                     TMPF[:, h:h + 256], ALU.mult), s)
                a = ACT.op(lambda e: e.activation(FF[0][:, c, :], TMPF[:, h + 256:h + 512], ACTF.Copy), m)
                sil[c % 2] = DVE.op(lambda e: e.tensor_tensor(FF[1][:, c, :], TMPF[:, h + 256:h + 512],
                                                              FF[0][:, c, :], ALU.subtract), a)
                t_ff.append(sil[c % 2])
                return [m, s]

            fm_unit(XB, hts, ffg)
            if c == 1:
                ACT.dma(GR2, I["g_ffn_post"][0].partition_broadcast(128), dsem("gfp"), t_end1)
                ACT.dma(PR, I["p"][0, 0].rearrange("(t p) d -> p t d", p=128), dsem("p"), t_end1)
            if c % 3:
                ada(n_ada)
                n_ada += 1
        PT = tuple(at(f"pt{p}", O_AR + 19968 + 512 * p, 512, F32R).rearrange("p (k n) -> p k n", k=2)
                   for p in range(2))
        banks = [bank() for _ in range(4)]
        ps_held.update(banks)
        pts = to_T(lambda tt, k: PR[:, tt, k * 128:k * 128 + 128], PT, 2, None, dtok("p"), t_end1)
        for c in range(11):
            if c:
                t_ada = ada(n_ada)
                n_ada += 1
            toks = wide([f[:, 2 * c:2 * c + 2, :] for f in FF], banks, t_ff[2 * c + 1], c == 0, c == 10)
        b2 = [bank() for _ in range(4)]
        t2 = wide(PT, b2, pts, True, True)[3]
        ps_held.clear()
        ps_held.update(b2)
        t_x2 = post_norm(banks, toks, GR2, dtok("gfp"), TMPF)

        h2 = to_T(lambda tt, k: X[:, tt, k * 128:k * 128 + 128], XA, 8, None, each=t_x2)
        t_x3 = []
        for n in range(4):
            bb, ts = tm_pair(XA, h2)
            h = (n % 2) * 512
            for tt in range(2):
                v, b, w = TMPF[:, h + tt * 256:h + tt * 256 + 256], bb[tt], b2[tt * 2 + n // 2]
                a = ACT.op(lambda e, b=b, v=v: e.activation(v, ps[b][:, 0:256], ACTF.Sigmoid), ts[tt],
                           t_x3[n - 2] if n > 1 else t_x2[1])
                ps_free[b] = [a]
                a = DVE.op(lambda e, v=v, w=w, n=n: e.tensor_tensor(
                    v, v, ps[w][:, (n % 2) * 256:(n % 2) * 256 + 256], ALU.mult), a, t2)
                ps_free[w] = [a]
                t = DVE.op(lambda e, v=v, tt=tt, n=n: e.tensor_tensor(
                    X[:, tt, n * 256:n * 256 + 256], X[:, tt, n * 256:n * 256 + 256], v, ALU.add))
            t_x3.append(t)
        t_x3 = t_x3[3]
        ps_held.clear()

        MC = small(16)
        o_wr = const_at["mean"][0]
        WR = CST[:, o_wr:o_wr + 288].rearrange("p (k n) -> p k n", k=8)
        ACT.dma(WR[:, :, 0:4], I["w_group_2"][0].rearrange("(k p) n -> p k n", p=128), dsem("wr"), t_end1)
        ACT.dma(WR[:, :, 4:36], I["w_expert_2"][0].rearrange("(k p) n -> p k n", p=128), dsem("wr"), t_end1)
        b = bank()
        for j in range(16):
            t = PE.op(lambda e, j=j, b=b: e.matmul(ps[b][:, j:j + 1], ADA[:, 128 * j:128 * j + 128], ones[:, 0:1],
                                                   start=True, stop=True), t_ada, *ps_free[b])
        t_mcp = t
        t = DVE.op(lambda e, b=b: e.tensor_copy(MC, ps[b][:, 0:16]), t)
        ps_free[b] = [t]
        t_mc = DVE.op(lambda e: e.scalar_tensor_tensor(out=MC[:, 8:16], in0=MC[:, 8:16], scalar=1.0,
                                                       in1=COL[:, row_at["g_mix_2"]:row_at["g_mix_2"] + 8],
                                                       op0=ALU.add, op1=ALU.mult))
        MR = ADA[:, 2048:6144].rearrange("p (k n) -> p k n", k=4)

        QK = [ar(6144 + 1024 * n, 1024, 4) for n in range(4)]
        VV = [ar(10240 + 1024 * n, 1024, 2) for n in range(2)]
        TMPA = ar(12288, 1024)
        L4 = [ar(13312 + 1536 * n, 1536, 4) for n in range(4)]
        DG = ar(13312, 256)
        HF = ar(15360, 2048, 8)
        OD, OS = ar(0, 1024, 2), ar(1024, 1024, 2)

        def modulated(b, k0, p):
            for k in range(k0, k0 + 2):
                a = DVE.op(lambda e, k=k, v=ps[b][:, (k - k0) * 256:(k - k0) * 256 + 256]: e.tensor_scalar(
                    HF[:, k, :], v, MC[:, 8 + k:9 + k], MC[:, k:k + 1], ALU.mult, ALU.add), p)
            ps_free[b] = [a]
            return split_operand(HF[:, k0:k0 + 2, :], XB, k0, 2, a)

        warm(ACTF.Sqrt)
        hts = norm_T(DG, TMPA, None, None, [t_x3] * 2, [PE.last, DVE.last], modulated)
        t_mr = [None] * 4

        def spread(n):
            for j in (2 * n, 2 * n + 1):
                b = bank()
                v = ADA[:, 2048 + 512 * j:2560 + 512 * j]
                t = PE.op(lambda e, b=b, v=v: e.matmul(ps[b][:, :], ones, v, start=True, stop=True), *ps_free[b],
                          t_ada)
                ps_free[b] = [ACT.op(lambda e, b=b, v=v: e.activation(v, ps[b][:, :], ACTF.Copy), t)]
            t_mr[n] = ACT.last

        t_in = [DVE.last, ACT.last, PE.last]

        t_qk = {}

        def qk(kind, n):
            dst = QK[("qd", "kd", "qs", "ks").index(kind)]
            fm_unit(XB, hts, lambda b, t: [ACT.op(lambda e: e.activation(
                dst[:, 2 * n:2 * n + 2, :], pair(b), ACTF.Copy), t, t_in)])
            t_qk[kind, n] = ACT.last

        def vv(kind, n):
            dst = VV[("vd", "vs").index(kind)]
            bb, ts = tm_pair(XB, hts)
            for tt in range(2):
                ps_free[bb[tt]] = [ACT.op(lambda e, b=bb[tt], tt=tt: e.activation(
                    dst[:, tt, 256 * n:256 * n + 256], ps[b][:, 0:256], ACTF.Copy), ts[tt], t_in)]
            t_qk[kind, n] = ACT.last

        def head(n, h):
            return QK[n][64 * (h % 2):64 * (h % 2) + 64, h // 2, :]

        before, upto = c_("before"), c_("upto")
        S = {}

        def sb_scores(g):
            LA, LB = L4[2 * g], L4[2 * g + 1]
            for h in range(4 * g, 4 * g + 4):
                b = bank()
                PE.quiet(lambda e, b=b, h=h: e.matmul(ps[b][:, 0:256], head(3, h)[:, 0:128], head(2, h),
                                                      start=True, stop=True), t_qk["qs", g], t_qk["ks", g],
                         *ps_free[b])
                t = PE.op(lambda e, b=b, h=h: e.matmul(ps[b][:, 256:384], head(3, h)[:, 128:256],
                                                       head(2, h)[:, 128:256], start=True, stop=True))
                a = ACT.op(lambda e, b=b, h=h: e.activation(LB[:, h % 4, :], ps[b][:, 0:384], ACTF.Abs, scale=0.125),
                           t, t_in)
                d = DVE.op(lambda e, b=b, h=h: e.tensor_scalar(LA[:, h % 4, :], ps[b][:, 0:384], 0.125, None,
                                                               ALU.mult), a, t_in)
                ps_free[b] = [d]
            ACT.op(lambda e: e.activation(LB, LB, ACTF.Exp, scale=-1.0))
            a = ACT.op(lambda e: e.activation(LB, LB, ACTF.Ln, bias=c_("one")))
            DVE.op(lambda e: e.scalar_tensor_tensor(out=LB, in0=LA, scalar=0.0, in1=LB, op0=ALU.max, op1=ALU.add), a)
            for o in (0, 256):
                t = DVE.op(lambda e, o=o: e.tensor_tensor(
                    LB[:, :, o:o + 128], LB[:, :, o:o + 128], before.unsqueeze(1).broadcast_to((128, 4, 128)),
                    ALU.mult))
            S["sb", g] = t

        def sb_sums(g):
            LA, LB = L4[2 * g], L4[2 * g + 1]
            for h in range(4):
                b = bank()
                PE.quiet(lambda e, b=b, h=h: e.matmul(ps[b][:, 0:128], upto, LB[:, h, 0:128], start=True, stop=True),
                         S["sb", g], *ps_free[b])
                PE.quiet(lambda e, b=b, h=h: e.matmul(ps[b][:, 128:256], upto, LB[:, h, 128:256], start=True,
                                                      stop=False))
                PE.quiet(lambda e, b=b, h=h: e.matmul(ps[b][:, 128:256], ones, LB[:, h, 256:384], start=False,
                                                      stop=True))
                t3 = PE.op(lambda e, b=b, h=h: e.matmul(ps[b][:, 256:384], upto, LB[:, h, 256:384], start=True,
                                                        stop=True))
                a = DVE.op(lambda e, b=b, h=h: e.tensor_tensor(LA[:, h, :], LA[:, h, :], ps[b][:, 0:384],
                                                               ALU.subtract), t3)
                ps_free[b] = [a]
            t = DVE.op(lambda e: e.scalar_tensor_tensor(
                out=LA, in0=LA, scalar=0.0, in1=c_("sbneg").unsqueeze(1).broadcast_to((128, 4, 384)),
                op0=ALU.min, op1=ALU.add))
            S["sw", g] = ACT.op(lambda e: e.activation(LA, LA, ACTF.Exp), t)

        def values(P, V_, g, waits):
            b0, b1 = bank(), bank()
            for h in range(4):
                hh, o = (4 * g + h) * 64, h * 64
                PE.quiet(lambda e, h=h, o=o, hh=hh: e.matmul(ps[b0][:, o:o + 64], P[:, h, 0:128],
                                                             V_[:, 0, hh:hh + 64], start=True, stop=True),
                         *waits, *ps_free[b0])
                PE.quiet(lambda e, h=h, o=o, hh=hh: e.matmul(ps[b1][:, o:o + 64], P[:, h, 128:256],
                                                             V_[:, 0, hh:hh + 64], start=True, stop=False),
                         *ps_free[b1])
                t = PE.op(lambda e, h=h, o=o, hh=hh: e.matmul(ps[b1][:, o:o + 64], P[:, h, 256:384],
                                                              V_[:, 1, hh:hh + 64], start=False, stop=True))
            return b0, b1, t

        def sb_values(g):
            b0, b1, t = values(L4[2 * g], VV[1], g, [S["sw", g], t_qk["vs", g]])
            for tt, b in ((0, b0), (1, b1)):
                ps_free[b] = [DVE.op(lambda e, tt=tt, b=b: e.tensor_copy(
                    OS[:, tt, g * 256:g * 256 + 256], ps[b][:, 0:256]), t, t_mcp)]
            S["sv", g] = t

        mx, den = small(16), small(16)
        mx3, den3 = (v.rearrange("p (t h) -> p t h", t=2) for v in (mx, den))

        def di_scores(g):
            LC = L4[2 * g]
            for h in range(4 * g, 4 * g + 4):
                b = bank()
                PE.quiet(lambda e, b=b, h=h: e.matmul(ps[b][:, 0:128], head(0, h)[:, 0:128], head(1, h)[:, 0:128],
                                                      start=True, stop=True), t_qk["qd", g], t_qk["kd", g],
                         *ps_free[b])
                t = PE.op(lambda e, b=b, h=h: e.matmul(ps[b][:, 128:384], head(0, h)[:, 128:256], head(1, h),
                                                       start=True, stop=True))
                slope = 2.0 ** -(h + 1)
                a = DVE.op(lambda e, b=b, h=h, slope=slope: e.scalar_tensor_tensor(
                    out=LC[:, h % 4, :], in0=c_("dist"), scalar=-8.0 * slope, in1=ps[b][:, 0:384],
                    op0=ALU.mult, op1=ALU.add), t, S["sv", g])
                ps_free[b] = [a]

        def di_soft(g):
            LC, hg = L4[2 * g], 4 * g
            DVE.op(lambda e: e.reduce_max(mx3[:, 0, hg:hg + 4], LC[:, :, 0:128], AX))
            DVE.op(lambda e: e.reduce_max(mx3[:, 1, hg:hg + 4], LC[:, :, 128:384], AX))
            t = DVE.op(lambda e: e.tensor_scalar(mx3[:, :, hg:hg + 4], mx3[:, :, hg:hg + 4], -0.125, None, ALU.mult))
            for h in range(4):
                for tt, o, n in ((0, 0, 128), (1, 128, 256)):
                    a = ACT.op(lambda e, h=h, tt=tt, o=o, n=n: e.activation(
                        LC[:, h, o:o + n], LC[:, h, o:o + n], ACTF.Exp, bias=mx3[:, tt, hg + h:hg + h + 1],
                        scale=0.125), t)
            S["lc", g] = DVE.op(lambda e: e.tensor_tensor(
                LC, LC, c_("count").unsqueeze(1).broadcast_to((128, 4, 384)), ALU.mult), a)
            DVE.op(lambda e: e.reduce_sum(den3[:, 0, hg:hg + 4], LC[:, :, 0:128], AX))
            DVE.op(lambda e: e.reduce_sum(den3[:, 1, hg:hg + 4], LC[:, :, 128:384], AX))
            DVE.op(lambda e: e.reciprocal(den3[:, :, hg:hg + 4], den3[:, :, hg:hg + 4]))

        def di_turn(g):
            LC, LP = L4[2 * g], L4[2 * g + 1]
            for h in range(4):
                b = bank()
                for o in (0, 128, 256):
                    t = PE.op(lambda e, b=b, h=h, o=o: e.transpose(ps[b][:, o:o + 128], LC[:, h, o:o + 128], ident),
                              S["lc", g], *ps_free[b])
                a = ACT.op(lambda e, b=b, h=h: e.activation(LP[:, h, :], ps[b][:, 0:384], ACTF.Copy), t)
                ps_free[b] = [a]
            S["lp", g] = a

        def di_values(g):
            b0, b1, t = values(L4[2 * g + 1], VV[0], g, [S["lp", g], t_qk["vd", g]])
            for tt, b in ((0, b0), (1, b1)):
                ps_free[b] = [DVE.op(lambda e, tt=tt, b=b: e.tensor_tensor(
                    OD[:, tt, g * 256:g * 256 + 256].rearrange("p (h c) -> p h c", h=4),
                    ps[b][:, 0:256].rearrange("p (h c) -> p h c", h=4),
                    den3[:, tt, 4 * g:4 * g + 4].unsqueeze(2).broadcast_to((128, 4, 64)), ALU.mult), t, t_mcp)]

        qk("qs", 0), qk("qs", 1), qk("ks", 0), qk("ks", 1)
        sb_scores(0)
        vv("vs", 0)
        sb_scores(1)
        vv("vs", 1)
        sb_sums(0)
        qk("qd", 0)
        sb_sums(1)
        qk("kd", 0)
        sb_values(0)
        qk("qd", 1)
        sb_values(1)
        di_scores(0)
        qk("kd", 1)
        di_soft(0)
        di_scores(1)
        vv("vd", 0)
        di_soft(1)
        di_turn(0)
        vv("vd", 1)
        di_values(0)
        spread(0)
        di_turn(1)
        di_values(1)
        warm(ACTF.Sqrt)
        ss = small(4)
        for n, O in enumerate((OD, OS)):
            for tt in range(2):
                t = ACT.op(lambda e, n=n, O=O, tt=tt: e.activation(TMPA[:, 0:512], O[:, tt, :], ACTF.Square,
                                                                   accum_out=ss[:, 2 * n + tt:2 * n + tt + 1]),
                           DVE.last)
        t = rstd(ss, 1.0 / 512, t)
        DGA = ar(8192, 512, 4)
        t = DVE.op(lambda e: e.tensor_tensor(DGA, ident.unsqueeze(1).broadcast_to((128, 4, 128)),
                                             ss.unsqueeze(2).broadcast_to((128, 4, 128)), ALU.mult), t)
        t_at, t_atd = PE.last, t
        spread(1)
        spread(2)
        GF2 = ar(7168, 1024)
        ACT.dma(GF2, I["g_ffn_2"][0].partition_broadcast(128), dsem("gf2"), t_at, t_atd)
        mts = []
        for k0 in range(0, 8, 2):
            b = bank()
            for k in range(k0, k0 + 2):
                for tt in range(2):
                    o = (k - k0) * 256 + tt * 128
                    p = PE.op(lambda e, b=b, o=o, s=(OD if k < 4 else OS)[:, tt, (k % 4) * 128:(k % 4) * 128 + 128],
                              d=DGA[:, 2 * (k // 4) + tt, :]: e.matmul(ps[b][:, o:o + 128], s, d, start=True,
                                                                       stop=True), t, *ps_free[b])
            mts.append(out_T(b, XA, k0, lambda k: col("g_dil_out_2", k) if k < 4 else col("g_sb_out_2", k - 4), p))
        t_ot = PE.last
        banks, toks = token_major(XA, mts)
        DVE.op(lambda e: e.scalar_tensor_tensor(out=GF2, in0=MR[:, 2, :], scalar=1.0, in1=GF2, op0=ALU.add,
                                                op1=ALU.mult), dtok("gf2"), t_mr[2])
        t_w2o = PE.last
        TMPX = at("tmp4", O_XB, 1024)
        TMPY = at("tmp5", O_XB + 1024, 512)
        spread(3)
        t_x4 = []
        for j in range(4):
            tt, nn = j // 2, j % 2
            a = DVE.op(lambda e, b=banks[j], nn=nn: e.tensor_tensor(TMPY, ps[b][:, :],
                                                                   MR[:, 0, nn * 512:nn * 512 + 512], ALU.mult),
                       toks[j], t_mr[0])
            ps_free[banks[j]] = [a]
            t = DVE.op(lambda e, tt=tt, nn=nn: e.tensor_tensor(
                X[:, tt, nn * 512:nn * 512 + 512], X[:, tt, nn * 512:nn * 512 + 512], TMPY, ALU.add))
            if nn:
                t_x4.append(t)

        H2 = at("h2", O_SPL + 6144, 2048).rearrange("p (t n) -> p t n", t=2)
        HT = k8(at("ht", O_XA, 2048))
        SLOT = ([at(f"slot{n}", TOP - 12288 + 4096 * n, 4096) for n in range(3)] +
                [at(f"slot{n + 3}", O_RAW + 4096 * n, 4096) for n in range(4)] + [at("slot7", O_XB, 4096)])
        NS, t_xb = len(SLOT), []

        def read(*raws):
            return [u.freed for u in units[-NRAW:] if any(u.raw is RAW[i] for i in raws)]

        before_slot = [[t_at, t_atd]] * 3 + [read(0, 1), read(2, 3), [read(4), t_w2o], [t_w2o], t_xb]
        slot_sem, slot_n = [sem(f"d_slot{n}") for n in range(NS)], [0] * NS
        slot_free = list(before_slot)
        n_slots = [0]

        def stream(*pieces):
            i = n_slots[0] % NS
            n_slots[0] += 1
            for view, src in pieces:
                SP.dma(view(SLOT[i]), src, slot_sem[i], slot_free[i])
                slot_n[i] += 16
            return i, Tok(slot_sem[i], slot_n[i])

        sh = small(2)
        GFI = ar(4096, 1024)
        th = []
        for tt in range(2):
            s1 = sh[:, tt:tt + 1]
            t = ACT.op(lambda e, tt=tt, s1=s1: e.activation(TMPX, X[:, tt, :], ACTF.Square, accum_out=s1), t_x4[tt])
            t = rstd(s1, 1.0 / D, t)
            DVE.op(lambda e, tt=tt, s1=s1: e.scalar_tensor_tensor(
                out=H2[:, tt, :], in0=X[:, tt, :], scalar=s1, in1=GF2, op0=ALU.mult, op1=ALU.mult), t_w2o)
            th.append(DVE.op(lambda e, tt=tt: e.tensor_tensor(H2[:, tt, :], H2[:, tt, :], MR[:, 1, :], ALU.add),
                             t_mr[1]))
        t_xb.extend([t, t_w2o, DVE.last])
        hts = to_T(lambda tt, k: H2[:, tt, k * 128:k * 128 + 128], HT, 8, None, each=th)
        warm(ACTF.Exp)
        ACT.dma(GFI, I["g_final_2"].partition_broadcast(128), dsem("gfi"), DVE.last)
        RT = at("RT", 3016, 72).rearrange("p (t n) -> p t n", t=2)
        for tt in range(2):
            b = bank()
            t = plain(HT, WR, 8, tt, b, 36, dtok("wr"), *hts)
            ps_free[b] = [DVE.op(lambda e, tt=tt, b=b: e.tensor_copy(RT[:, tt, :], ps[b][:, 0:36]), t)]
        gm, gs = small(2), small(2)
        GE, G1 = small(8).rearrange("p (t g) -> p t g", t=2), small(8).rearrange("p (t g) -> p t g", t=2)
        iota = c_("iota")
        gl = RT[:, :, 0:4]

        def bc(v, n):
            return v.unsqueeze(2).broadcast_to((128, 2, n))

        def first_max(vals, n, mx_, hot, tmp):
            ix = small(2)
            io = iota[:, 0:n].unsqueeze(1).broadcast_to((128, 2, n))
            DVE.op(lambda e: e.reduce_max(mx_, vals, AX))
            DVE.op(lambda e: e.tensor_tensor(tmp, vals, bc(mx_, n), ALU.is_lt))
            DVE.op(lambda e: e.scalar_tensor_tensor(out=tmp, in0=tmp, scalar=64.0, in1=io, op0=ALU.mult, op1=ALU.add))
            DVE.op(lambda e: e.tensor_reduce(ix, tmp, AX, ALU.min))
            return DVE.op(lambda e: e.tensor_tensor(hot, io, bc(ix, n), ALU.is_equal))

        first_max(gl, 4, gm, G1, GE)
        DVE.op(lambda e: e.tensor_tensor(GE, gl, bc(gm, 4), ALU.subtract))
        t = ACT.op(lambda e: e.activation(GE, GE, ACTF.Exp), DVE.last)
        DVE.op(lambda e: e.reduce_sum(gs, GE, AX), t)
        DVE.op(lambda e: e.reciprocal(gs, gs))
        DVE.op(lambda e: e.tensor_scalar(G1, G1, 1.0, BIG, ALU.subtract, ALU.mult))
        el = RT[:, :, 4:36]
        for g in range(4):
            DVE.op(lambda e, g=g: e.tensor_tensor(el[:, :, 8 * g:8 * g + 8], el[:, :, 8 * g:8 * g + 8],
                                                  bc(G1[:, :, g], 8), ALU.add))
        hot1, hot2, tmp = (small(64).rearrange("p (t g) -> p t g", t=2) for _ in range(3))
        m1, m2, dd = small(2), small(2), small(2)
        first_max(el, 32, m1, hot1, tmp)
        DVE.op(lambda e: e.scalar_tensor_tensor(out=el, in0=hot1, scalar=-3.0 * BIG, in1=el, op0=ALU.mult,
                                                op1=ALU.add))
        first_max(el, 32, m2, hot2, tmp)
        DVE.op(lambda e: e.tensor_tensor(dd, m2, m1, ALU.subtract))
        t = ACT.op(lambda e: e.activation(dd, dd, ACTF.Exp), DVE.last)
        warm(ACTF.Silu)
        DVE.op(lambda e: e.tensor_scalar(m1, dd, 1.0, None, ALU.add), t)
        DVE.op(lambda e: e.reciprocal(m1, m1))
        DVE.op(lambda e: e.tensor_tensor(m1, m1, gs, ALU.mult))
        DVE.op(lambda e: e.tensor_tensor(m2, m1, dd, ALU.mult))
        WC = at("WC", 3088, 64).rearrange("p (t n) -> p t n", t=2)
        DVE.op(lambda e: e.tensor_tensor(WC[:, :, :], hot1, bc(m1, 32), ALU.mult))
        DVE.op(lambda e: e.tensor_tensor(tmp, hot2, bc(m2, 32), ALU.mult))
        t_wc = DVE.op(lambda e: e.tensor_tensor(WC[:, :, :], WC[:, :, :], tmp, ALU.add))

        AS, RK, WL = (at(n, 3152 + 64 * i, 64).rearrange("p (t n) -> p t n", t=2)
                      for i, n in enumerate(("AS", "RK", "WL")))
        t_as = DVE.op(lambda e: e.tensor_tensor(AS[:, :, :], hot1, hot2, ALU.add))
        b = bank()
        before, ones = c_("before"), c_("ones")
        PE.quiet(lambda e, b=b: e.matmul(ps[b][:, 0:32], before, AS[:, 0, :], start=True, stop=True), t_as,
                 *ps_free[b])
        PE.quiet(lambda e, b=b: e.matmul(ps[b][:, 32:64], ones, AS[:, 0, :], start=True, stop=False))
        t = PE.op(lambda e, b=b: e.matmul(ps[b][:, 32:64], before, AS[:, 1, :], start=False, stop=True))
        t = DVE.op(lambda e, b=b: e.scalar_tensor_tensor(
            out=RK[:, :, :], in0=ps[b][:, 0:64].rearrange("p (t n) -> p t n", t=2), scalar=1.0, in1=AS[:, :, :],
            op0=ALU.add, op1=ALU.mult), t)
        ps_free[b] = [t]
        t_rk = DVE.op(lambda e: e.tensor_scalar(RK[:, :, :], RK[:, :, :], 1.0, None, ALU.subtract))

        SE = [ar(256 * n, 256) for n in range(2)]
        SW = [ar(512 + 1024 * n, 1024) for n in range(2)]
        SWT = [ar(2560 + 256 * n, 256) for n in range(2)]
        HS = [ar(3072 + 256 * n, 256) for n in range(2)]
        HE = [ar(3584 + 128 * n, 128) for n in range(2)]
        YP = [ar(6144 + 1024 * n, 1024) for n in range(2)]
        XG = [k8(at(f"xg{n}", O_XA + 2048 + 1024 * n, 1024)) for n in range(2)]
        yb = [bank() for _ in range(4)]
        yfree = [w for b in yb for w in ps_free[b]]
        ps_held.update(yb)
        sw_free = [None, None]
        xg_free = [None, None]
        xg_tok, sw_tok = [None, None], [None, None]
        state = {}

        def gather(g):
            n = g % 2
            io = iota.unsqueeze(1).broadcast_to((128, 4, 32))
            for tt in range(2):
                v = SE[n][:, tt * 128:tt * 128 + 128].rearrange("p (x s) -> p x s", x=4)
                r = RK[:, tt, 4 * g:4 * g + 4].unsqueeze(2).broadcast_to((128, 4, 32))
                t = DVE.op(lambda e, v=v, r=r, io=io: e.tensor_tensor(v, r, io, ALU.is_equal), t_rk, xg_free[n])
            for tt in range(2):
                v = SE[n][:, tt * 128:tt * 128 + 128].rearrange("p (x s) -> p x s", x=4)
                v = v.unsqueeze(2).broadcast_to((128, 4, 4, 32))
                u = SW[n][:, tt * 512:tt * 512 + 512].rearrange("p (x q s) -> p x q s", x=4, q=4)
                r = WC[:, tt, 4 * g:4 * g + 4].unsqueeze(2).unsqueeze(3).broadcast_to((128, 4, 4, 32))
                sw_tok[n] = DVE.op(lambda e, v=v, r=r, u=u: e.tensor_tensor(u, v, r, ALU.mult), sw_free[n])
            done = []
            for k0 in (0, 4):
                b = bank()
                for k in range(k0, k0 + 4):
                    for tt in range(2):
                        p = PE.op(lambda e, b=b, k=k, k0=k0, tt=tt, n=n: e.matmul(
                            ps[b][:, (k - k0) * 128:(k - k0) * 128 + 128], H2[:, tt, k * 128:k * 128 + 128],
                            SE[n][:, tt * 128:tt * 128 + 128], start=(tt == 0), stop=(tt == 1)), t, *ps_free[b])
                v = ps[b][:, :].rearrange("p (k n) -> p k n", k=4)
                d = XG[n][:, k0:k0 + 4, :]
                if k0:
                    c = DVE.op(lambda e, v=v, d=d: e.tensor_copy(d, v), p)
                else:
                    c = ACT.op(lambda e, v=v, d=d: e.activation(d, v, ACTF.Copy), p, xg_free[n])
                ps_free[b] = [c]
                done.append(c)
            xg_tok[n] = done

        def gate_up(x):
            n = (x // 4) % 2
            half = [stream(*((lambda r, w=w: r.rearrange("p (w k n) -> p w k n", w=2, k=4)[:, w],
                              I[name][0, x, 512 * j:512 * j + 512, :].rearrange("(k p) n -> p k n", p=128))
                             for w, name in enumerate(("w_gate_2", "w_up_2")))) for j in range(2)]
            b = bank()
            for k in range(8):
                i, tw = half[k // 4]
                v = SLOT[i].rearrange("p (w k n) -> p w k n", w=2, k=4)
                for q in range(4):
                    w = v[:, q // 2, k % 4, (q % 2) * 256:(q % 2) * 256 + 256]
                    xs = XG[n][:, k, (x % 4) * 32:(x % 4) * 32 + 32]
                    f = (lambda e, b=b, q=q, w=w, xs=xs, k=k: e.matmul(ps[b][32 * q:32 * q + 32, 0:256], xs, w,
                                                                       start=(k == 0), stop=(k == 7)))
                    if k % 4 == 3 and q == 3:
                        slot_free[i] = t = PE.op(f)
                    else:
                        PE.quiet(f, tw, *xg_tok[n], *ps_free[b])
            if x % 4 == 3:
                xg_free[n] = t
            h = HS[x % 2]
            a = ACT.op(lambda e, b=b, h=h: e.activation(h[0:64, :], ps[b][0:64, 0:256], ACTF.Silu), t,
                       state.get(("T", x - 2)))
            a = DVE.op(lambda e, b=b, h=h: e.tensor_tensor(h[0:64, :], h[0:64, :], ps[b][64:128, 0:256], ALU.mult), a)
            ps_free[b] = [a]
            state["H", x] = a

        def turn(x):
            n = (x // 4) % 2
            h = HS[x % 2]
            b = bank()
            for j in range(2):
                t = PE.op(lambda e, b=b, j=j, h=h: e.transpose(ps[b][:, 64 * j:64 * j + 64],
                                                               h[0:64, 128 * j:128 * j + 128], ident[0:64, 0:64]),
                          state["H", x], *ps_free[b])
            state["T", x] = t
            for tt in range(2):
                v = SW[n][:, tt * 512 + (x % 4) * 128:tt * 512 + (x % 4) * 128 + 128]
                t2 = PE.op(lambda e, b=b, v=v, tt=tt: e.transpose(ps[b][:, 128 + 128 * tt:256 + 128 * tt], v, ident),
                           sw_tok[n])
            if x % 4 == 3:
                sw_free[n] = t2
            d = HE[x % 2]
            state["HE", x] = DVE.op(lambda e, b=b, d=d: e.tensor_copy(d, ps[b][:, 0:128]), t, t2,
                                    state.get(("DN", x - 2)))
            d = SWT[x % 2]
            state["SWT", x] = DVE.op(lambda e, b=b, d=d: e.tensor_copy(d, ps[b][:, 128:384]), t2,
                                     state.get(("SC", x - 2)))
            ps_free[b] = [DVE.last]

        def down(x):
            i, td = stream((lambda r: r.rearrange("p (k n) -> p k n", k=4),
                            I["w_down_2"][0, x].rearrange("(k p) n -> p k n", p=128)))
            W = SLOT[i].rearrange("p (k n) -> p k n", k=4)
            bb = [bank(), bank()]
            for nn in range(2):
                for j in range(4):
                    f = (lambda e, nn=nn, j=j, W=W, x=x, b=bb[nn]: e.matmul(
                        ps[b][32 * j:32 * j + 32, :], HE[x % 2][:, 32 * j:32 * j + 32],
                        W[:, 2 * (j % 2) + j // 2, nn * 512:nn * 512 + 512], start=True, stop=True))
                    t = PE.op(f, td, state["HE", x], *ps_free[bb[nn]])
                d = YP[x % 2][:, nn * 512:nn * 512 + 512]
                if nn:
                    c = DVE.op(lambda e, d=d, b=bb[nn]: e.tensor_copy(d, ps[b][:, :]), t, state.get(("SC", x - 2)))
                else:
                    c = ACT.op(lambda e, d=d, b=bb[nn]: e.activation(d, ps[b][:, :], ACTF.Copy), t,
                               state.get(("SC", x - 2)))
                ps_free[bb[nn]] = [c]
                state["YP", x, nn] = c
            slot_free[i] = state["DN", x] = t

        def scatter(x):
            for tt in range(2):
                for nn in range(2):
                    t = PE.op(lambda e, tt=tt, nn=nn, x=x: e.matmul(
                        ps[yb[tt * 2 + nn]][:, :], SWT[x % 2][:, tt * 128:tt * 128 + 128],
                        YP[x % 2][:, nn * 512:nn * 512 + 512], start=(x == 0), stop=(x == NE - 1)),
                        state["SWT", x], state["YP", x, 0], state["YP", x, 1], *yfree)
            state["SC", x] = t

        FLAG = at("FLAG", 3344, 1, mybir.dt.int32)

        def leftover():
            over, left = small(1), small(1)
            DVE.op(lambda e: e.tensor_scalar(WL[:, :, :], RK[:, :, :], float(CAP), None, ALU.is_ge))
            t = DVE.op(lambda e: e.tensor_reduce(over, WL[:, :, :].rearrange("p t n -> p (t n)"), AX, ALU.max))
            b = bank()
            t = PE.op(lambda e, b=b: e.matmul(ps[b][:, 0:1], ones, over, start=True, stop=True), t, *ps_free[b])
            t = DVE.op(lambda e, b=b: e.tensor_scalar(left, ps[b][:, 0:1], 1.0, None, ALU.min), t)
            ps_free[b] = [t]
            DVE.op(lambda e: e.tensor_copy(FLAG[:, :], left))
            t_wl = DVE.op(lambda e: e.tensor_tensor(WL[:, :, :], WL[:, :, :], WC[:, :, :], ALU.mult))

        gather(0)
        for x in range(NE + 2):
            if x == 3:
                leftover()
            if x < NE:
                gate_up(x)
            if 1 <= x <= NE:
                turn(x - 1)
            if x >= 2:
                scatter(x - 2)
            if 1 <= x <= NE:
                down(x - 1)
            if x % 4 == 1 and x + 3 < NE:
                gather(x // 4 + 1)
        for tt in range(2):
            for nn in range(2):
                c = slice(nn * 512, nn * 512 + 512)
                DVE.op(lambda e, b=yb[2 * tt + nn], tt=tt, c=c: e.tensor_tensor(H2[:, tt, c], ps[b][:, :],
                                                                               MR[:, 3, c], ALU.mult),
                       state["SC", NE - 1], t_mr[3])
            DVE.op(lambda e, tt=tt: e.tensor_tensor(X[:, tt, :], X[:, tt, :], H2[:, tt, :], ALU.add))

        def emit_all():
            with nc.Block() as block:
                block.sync(SP.emit)
                block.gpsimd(POOL.emit)
                block.scalar(ACT.emit)
                block.vector(DVE.emit)
                block.tensor(PE.emit)
            for q in (SP, POOL, ACT, DVE, PE):
                q.items = []

        warm(ACTF.Sqrt)
        emit_all()
        Y = SLOT[6][:, 0:2048].rearrange("p (t n) -> p t n", t=2)
        general(nc, ctx, I, nc.values_load(FLAG[0:1, 0:1], min_val=0, max_val=1), HT, (X, MR[:, 3, :], Y), WL, SLOT,
                ps, (YP[1], YP[0].rearrange("p (k n) -> p k n", k=4)))
        so = small(2)
        for tt in range(2):
            s1 = so[:, tt:tt + 1]
            t = ACT.op(lambda e, tt=tt, s1=s1: e.activation(YP[tt], X[:, tt, :], ACTF.Square, accum_out=s1), DVE.last)
            t = rstd(s1, 1.0 / D, t)
            t = DVE.op(lambda e, tt=tt, s1=s1: e.scalar_tensor_tensor(
                out=H2[:, tt, :], in0=X[:, tt, :], scalar=s1, in1=GFI, op0=ALU.mult, op1=ALU.mult), dtok("gfi"))
            SP.dma(out[0, 128 * tt:128 * tt + 128, :], H2[:, tt, :], dsem("out"), t)
        SP.wait(dtok("out"))
        emit_all()


def general(nc, ctx, I, flag, HT, sums, WL, ring, ps, room):
    X, gate, Y = sums
    TMP, HH = room
    s_y = ctx.enter_context(nc.semaphore("gy"))
    names = ("gpe", "gact", "gdve", "dg", "du", "dd")
    s_pe, s_act, s_dve, s_g, s_u, s_d = sems = [ctx.enter_context(nc.semaphore(n)) for n in names]
    G, U = (ring[n].rearrange("p (k n) -> p k n", k=8) for n in (0, 1))
    W = ring[2].rearrange("p (k n) -> p k n", k=4)
    with nc.If(flag > 0):
        nc.vector.memset(Y, 0.0)
        nc.all_engine_barrier()
        with nc.Fori(0, NE) as x:
            with nc.Block() as block:
                @block.sync
                def _(eng):
                    for dst, name, s in ((G, "w_gate_2", s_g), (U, "w_up_2", s_u), (W, "w_down_2", s_d)):
                        eng.dma_start(dst, I[name][0, bass.ds(x, 1)].rearrange("a (k p) n -> p (a k) n", p=128))\
                           .then_inc(s, 16)

                @block.tensor
                def _(eng):
                    eng.wait_ge(s_g, 16)
                    eng.wait_ge(s_u, 16)
                    for f in range(4):
                        for n, S in enumerate((G, U)):
                            for k in range(8):
                                mm = eng.matmul(ps[f][:, n * 256:n * 256 + 256], S[:, k, f * 128:f * 128 + 128],
                                                HT[:, k, :], start=(k == 0), stop=(k == 7))
                        mm.then_inc(s_pe, 1)
                    eng.wait_ge(s_d, 16)
                    eng.wait_ge(s_dve, 4)
                    for j in range(4):
                        for k in range(4):
                            mm = eng.matmul(ps[4 + j][:, :], HH[:, k, (j // 2) * 128:(j // 2) * 128 + 128],
                                            W[:, k, (j % 2) * 512:(j % 2) * 512 + 512], start=(k == 0), stop=(k == 3))
                        mm.then_inc(s_pe, 1)

                @block.scalar
                def _(eng):
                    for f in range(4):
                        eng.wait_ge(s_pe, f + 1)
                        eng.activation(TMP[:, f * 256:f * 256 + 256], ps[f][:, 0:256], ACTF.Silu).then_inc(s_act, 1)

                @block.vector
                def _(eng):
                    for f in range(4):
                        eng.wait_ge(s_act, f + 1)
                        eng.tensor_tensor(HH[:, f, :], ps[f][:, 256:512], TMP[:, f * 256:f * 256 + 256], ALU.mult)\
                           .then_inc(s_dve, 1)
                    for j in range(4):
                        y = Y[:, j // 2, (j % 2) * 512:(j % 2) * 512 + 512]
                        eng.wait_ge(s_pe, 5 + j)
                        eng.scalar_tensor_tensor(out=y, in0=ps[4 + j][:, :], scalar=WL[:, j // 2, bass.ds(x, 1)],
                                                 in1=y, op0=ALU.mult, op1=ALU.add).then_inc(s_dve, 1)
            for s in sems:
                nc.sync.sem_clear(s)
            nc.all_engine_barrier()
        for tt in range(2):
            nc.vector.tensor_tensor(Y[:, tt, :], Y[:, tt, :], gate, ALU.mult).then_inc(s_y, 1)
        for tt in range(2):
            nc.vector.wait_ge(s_y, tt + 1)
            nc.vector.tensor_tensor(X[:, tt, :], X[:, tt, :], Y[:, tt, :], ALU.add)
        nc.all_engine_barrier()


_INS = ["x", "p", "g_mix_pre", "w_in", "w_sgu_s", "b_sgu_s", "g_sgu_v", "b_sgu_v", "w_sgu_out", "w_dw", "b_dw",
        "g_conv_ln", "b_conv_ln", "w_conv_out", "w_pool", "s_pool", "w_pool_out", "w_out", "g_mix_post",
        "g_ffn_pre", "w_ffn_in", "w_ffn_out", "g_ffn_post", "w_ple", "w_ple_gate", "c_2", "w_ada_2", "b_ada_2",
        "g_mix_2", "w_in_2", "g_dil_out_2", "g_sb_out_2", "w_out_2", "g_ffn_2", "w_group_2", "w_expert_2",
        "w_gate_2", "w_up_2", "w_down_2", "g_final_2"]


def kernel(**inputs):
    import concourse.bacc as _bacc
    from concourse.bass_utils import run_bass_kernel_spmd as _run

    nc = _bacc.Bacc("TRN2", target_bir_lowering=False, num_devices=1)
    arrays, I = {}, {}
    for name in _INS:
        a = np.ascontiguousarray(inputs[name])
        arrays[f"in_{name}"] = a
        I[name] = nc.dram_tensor(f"in_{name}", a.shape, mybir.dt.from_np(a.dtype), kind="ExternalInput").ap()
    cst, at = constants()
    arrays["in_cst"] = cst
    I["cst"] = nc.dram_tensor("in_cst", cst.shape, F32, kind="ExternalInput").ap()
    out = nc.dram_tensor("out_0", (1, T, D), F32, kind="ExternalOutput").ap()
    program(nc, I, out, at)
    r = _run(nc, [arrays], core_ids=[0])
    return r.results[0]["out_0"]
```
